# Optimizing a Trainium2 kernel written in Bass

```python
import math
import jax
import jax.numpy as jnp
from jax import lax
import numpy as np
import jax, jax.numpy as jnp

D_MODEL = 1024
BATCH = 1
SEQ = 512
DEPTH = 2

N_A_LAYERS = DEPTH // 2
N_B_LAYERS = DEPTH - N_A_LAYERS
EPS = 1e-6

GDN_HEADS = 6
GDN_DK = 128
GDN_DV = 128
GDN_QK_W = GDN_HEADS * GDN_DK
GDN_V_W = GDN_HEADS * GDN_DV
CONV_K = 4
CHUNK = 64

SWA_HEADS = 12
SWA_KV_HEADS = 2
SWA_DH = 64
SWA_GROUP = SWA_HEADS // SWA_KV_HEADS
SWA_Q_W = SWA_HEADS * SWA_DH
KV_W = SWA_KV_HEADS * SWA_DH
WINDOW = 128
SWA_BLOCK = 128
ROPE_THETA = 500000.0
ROT_DIM = SWA_DH // 4

MEM_LEN = 256
MEM_HEADS = 4
MEM_DH = 64
MEM_W = MEM_HEADS * MEM_DH

D_MIX = GDN_V_W + MEM_W
GDN_IN = 2 * GDN_QK_W + 2 * GDN_V_W + 2 * GDN_HEADS + MEM_W
SWA_IN = SWA_Q_W + MEM_W
D_FF = -(-8 * D_MODEL // (3 * 256)) * 256


def rms_norm(x, g):
    xf = x.astype(jnp.float32)
    y = xf * lax.rsqrt(jnp.mean(xf * xf, axis=-1, keepdims=True) + EPS)
    return (y * g.astype(jnp.float32)).astype(x.dtype)

def l2_normalize(x):
    xf = x.astype(jnp.float32)
    return xf * lax.rsqrt(jnp.sum(xf * xf, axis=-1, keepdims=True) + EPS)

def rope_tables(positions):
    inv = ROPE_THETA ** (-jnp.arange(0, ROT_DIM, 2, dtype=jnp.float32) / ROT_DIM)
    ang = positions.astype(jnp.float32)[..., None] * inv
    return jnp.cos(ang), jnp.sin(ang)

def apply_partial_rope(x, cos, sin):
    half = ROT_DIM // 2
    xf = x.astype(jnp.float32)
    x1, x2 = xf[..., :half], xf[..., half:ROT_DIM]
    c, s = cos[:, :, None, :], sin[:, :, None, :]
    out = jnp.concatenate([x1 * c - x2 * s, x2 * c + x1 * s, xf[..., ROT_DIM:]], axis=-1)
    return out.astype(x.dtype)

def causal_depthwise_conv(x, w):
    c = x.shape[-1]
    return lax.conv_general_dilated(
        x, w[:, None, :].astype(x.dtype), window_strides=(1,), padding=[(CONV_K - 1, 0)],
        dimension_numbers=("NWC", "WIO", "NWC"), feature_group_count=c)

def swiglu(h, w_gate_up, w_down):
    gu = h @ w_gate_up
    return (jax.nn.silu(gu[..., :D_FF]) * gu[..., D_FF:]) @ w_down

def gated_delta_rule_chunked(q, k, v, g, beta):
    b_sz, s_len, n_h, dk = q.shape
    dv = v.shape[-1]
    n_ch = s_len // CHUNK

    def chunks(t):
        t = t.reshape((b_sz, n_ch, CHUNK, n_h) + t.shape[3:])
        return jnp.moveaxis(t, 3, 1)

    q = chunks(q) * (dk ** -0.5)
    k = chunks(k)
    v = chunks(v)
    beta = chunks(beta)
    gc = jnp.cumsum(chunks(g), axis=-1)
    tril = jnp.tril(jnp.ones((CHUNK, CHUNK), dtype=bool))
    strict = jnp.tril(jnp.ones((CHUNK, CHUNK), dtype=bool), -1)
    decay = jnp.exp(jnp.where(tril, gc[..., :, None] - gc[..., None, :], -jnp.inf))
    kb = k * beta[..., None]
    lower = jnp.where(strict, jnp.einsum("bhncd,bhnkd->bhnck", kb, k) * decay, 0.0)
    rhs = jnp.concatenate([v * beta[..., None], kb * jnp.exp(gc)[..., None]], axis=-1)
    sol = lax.linalg.triangular_solve(lower, rhs, left_side=True, lower=True, unit_diagonal=True)
    u, w = sol[..., :dv], sol[..., dv:]
    intra = jnp.einsum("bhncd,bhnkd->bhnck", q, k) * decay
    q_g = q * jnp.exp(gc)[..., None]
    k_g = k * jnp.exp(gc[..., -1:] - gc)[..., None]
    g_last = jnp.exp(gc[..., -1])
    xs = tuple(jnp.moveaxis(t, 2, 0) for t in (u, w, intra, q_g, k_g, g_last))

    def step(state, inp):
        u_n, w_n, a_n, qg_n, kg_n, gl_n = inp
        v_new = u_n - jnp.einsum("bhck,bhkv->bhcv", w_n, state)
        o_n = jnp.einsum("bhck,bhkv->bhcv", qg_n, state) + jnp.einsum("bhcs,bhsv->bhcv", a_n, v_new)
        state = state * gl_n[..., None, None] + jnp.einsum("bhck,bhcv->bhkv", kg_n, v_new)
        return state, o_n

    s0 = jnp.zeros((b_sz, n_h, dk, dv), jnp.float32)
    _, o = lax.scan(step, s0, xs)
    return jnp.transpose(o, (1, 0, 3, 2, 4)).reshape(b_sz, s_len, n_h, dv)

def gated_deltanet_mixer(h, w_in, conv_w, a_log, dt_bias, norm_g):
    b_sz, s_len, _ = h.shape
    proj = h @ w_in
    o1 = 2 * GDN_QK_W + GDN_V_W
    qkv = jax.nn.silu(causal_depthwise_conv(proj[..., :o1], conv_w))
    z = proj[..., o1:o1 + GDN_V_W]
    o2 = o1 + GDN_V_W
    b_logit = proj[..., o2:o2 + GDN_HEADS].astype(jnp.float32)
    a_logit = proj[..., o2 + GDN_HEADS:o2 + 2 * GDN_HEADS].astype(jnp.float32)
    mem_q = proj[..., o2 + 2 * GDN_HEADS:]
    q = l2_normalize(qkv[..., :GDN_QK_W].reshape(b_sz, s_len, GDN_HEADS, GDN_DK))
    k = l2_normalize(qkv[..., GDN_QK_W:2 * GDN_QK_W].reshape(b_sz, s_len, GDN_HEADS, GDN_DK))
    v = qkv[..., 2 * GDN_QK_W:].reshape(b_sz, s_len, GDN_HEADS, GDN_DV).astype(jnp.float32)
    beta = jax.nn.sigmoid(b_logit)
    g = -jnp.exp(a_log.astype(jnp.float32)) * jax.nn.softplus(a_logit + dt_bias.astype(jnp.float32))
    o = gated_delta_rule_chunked(q, k, v, g, beta)
    o = rms_norm(o, norm_g) * jax.nn.silu(z.reshape(b_sz, s_len, GDN_HEADS, GDN_DV).astype(jnp.float32))
    return o.reshape(b_sz, s_len, GDN_V_W).astype(h.dtype), mem_q

def sliding_window_attention(q, k, v, sinks):
    b_sz, s_len = q.shape[:2]
    nb = s_len // SWA_BLOCK
    qb = q.reshape(b_sz, nb, SWA_BLOCK, SWA_KV_HEADS, SWA_GROUP, SWA_DH)
    kb = k.reshape(b_sz, nb, SWA_BLOCK, SWA_KV_HEADS, SWA_DH)
    vb = v.reshape(b_sz, nb, SWA_BLOCK, SWA_KV_HEADS, SWA_DH)
    pad = jnp.zeros_like(kb[:, :1])
    kw = jnp.concatenate([jnp.concatenate([pad, kb[:, :-1]], axis=1), kb], axis=2)
    vw = jnp.concatenate([jnp.concatenate([pad, vb[:, :-1]], axis=1), vb], axis=2)
    s = jnp.einsum("bnqhgd,bnkhd->bnhgqk", qb, kw).astype(jnp.float32) * (SWA_DH ** -0.5)
    qi = jnp.arange(SWA_BLOCK)[:, None] + SWA_BLOCK
    ki = jnp.arange(2 * SWA_BLOCK)[None, :]
    diff = qi - ki
    band = (diff >= 0) & (diff < WINDOW)
    has_prev = jnp.arange(nb) > 0
    mask = band[None] & (has_prev[:, None, None] | (ki >= SWA_BLOCK)[None])
    s = jnp.where(mask[None, :, None, None], s, -jnp.inf)
    sink = sinks.astype(jnp.float32).reshape(SWA_KV_HEADS, SWA_GROUP)[None, None, :, :, None, None]
    m = jnp.maximum(jnp.max(s, axis=-1, keepdims=True), sink)
    p = jnp.exp(s - m)
    p = (p / (jnp.sum(p, axis=-1, keepdims=True) + jnp.exp(sink - m))).astype(v.dtype)
    o = jnp.einsum("bnhgqk,bnkhd->bnqhgd", p, vw)
    return o.reshape(b_sz, s_len, SWA_Q_W)

def memory_attention(q, mem_k, mem_v):
    s = jnp.einsum("bshd,bmhd->bhsm", q, mem_k).astype(jnp.float32) * (MEM_DH ** -0.5)
    p = jax.nn.softmax(s, axis=-1).astype(q.dtype)
    o = jnp.einsum("bhsm,bmhd->bshd", p, mem_v)
    return o.reshape(q.shape[0], q.shape[1], MEM_W)

def first_inputs(seed: int = 0) -> dict:
    key = jax.random.key(seed)
    ks = jax.random.split(key, 24)
    f32 = jnp.float32

    def dense(k, shape, fan_in):
        return jax.random.normal(k, shape, f32) * (fan_in ** -0.5)

    def gain(k, shape):
        return 1.0 + 0.02 * jax.random.normal(k, shape, f32)

    x = jax.random.normal(ks[0], (BATCH, SEQ, D_MODEL), f32)
    mem = jax.random.normal(ks[1], (BATCH, MEM_LEN, D_MODEL), f32)
    positions = (jnp.arange(SEQ, dtype=jnp.int32)[None, :]
                 + jax.random.randint(ks[2], (BATCH, 1), 0, 4096, dtype=jnp.int32))
    dt0 = jnp.exp(jax.random.uniform(ks[15], (N_A_LAYERS, GDN_HEADS), f32,
                                     math.log(1e-3), math.log(1e-1)))
    return {
        "x": x,
        "mem": mem,
        "positions": positions,
        "ln_mix": gain(ks[3], (DEPTH, D_MODEL)),
        "ln_ffn": gain(ks[4], (DEPTH, D_MODEL)),
        "ln_mem": gain(ks[5], (D_MODEL,)),
        "w_mem_kv": dense(ks[6], (DEPTH, D_MODEL, 2 * MEM_W), D_MODEL),
        "w_out": dense(ks[7], (DEPTH, D_MIX, D_MODEL), D_MIX),
        "w_gate_up": dense(ks[8], (DEPTH, D_MODEL, 2 * D_FF), D_MODEL),
        "w_down": dense(ks[9], (DEPTH, D_FF, D_MODEL), D_FF),
        "gdn_w_in": dense(ks[10], (N_A_LAYERS, D_MODEL, GDN_IN), D_MODEL),
        "gdn_conv": dense(ks[11], (N_A_LAYERS, CONV_K, 2 * GDN_QK_W + GDN_V_W), CONV_K),
        "gdn_A_log": jnp.log(jax.random.uniform(ks[12], (N_A_LAYERS, GDN_HEADS), f32, 1.0, 16.0)),
        "gdn_dt_bias": dt0 + jnp.log(-jnp.expm1(-dt0)),
        "gdn_norm": gain(ks[13], (N_A_LAYERS, GDN_DV)),
        "swa_w_q": dense(ks[14], (N_B_LAYERS, D_MODEL, SWA_IN), D_MODEL),
        "swa_sinks": 0.5 * jax.random.normal(ks[16], (N_B_LAYERS, SWA_HEADS), f32),
        "ln_kv": gain(ks[17], (D_MODEL,)),
        "w_kv": dense(ks[18], (D_MODEL, 2 * KV_W), D_MODEL),
        "ln_final": gain(ks[19], (D_MODEL,)),
    }

def first_block(x, mem, positions, ln_mix, ln_ffn, ln_mem, w_mem_kv, w_out, w_gate_up, w_down,
              gdn_w_in, gdn_conv, gdn_A_log, gdn_dt_bias, gdn_norm,
              swa_w_q, swa_sinks, ln_kv, w_kv, ln_final):
    b_sz, s_len, _ = x.shape
    cos, sin = rope_tables(positions)
    mem_n = rms_norm(mem, ln_mem)
    shared_k = None
    shared_v = None
    for layer in range(DEPTH):
        h = rms_norm(x, ln_mix[layer])
        mkv = mem_n @ w_mem_kv[layer]
        mem_k = mkv[..., :MEM_W].reshape(b_sz, MEM_LEN, MEM_HEADS, MEM_DH)
        mem_v = mkv[..., MEM_W:].reshape(b_sz, MEM_LEN, MEM_HEADS, MEM_DH)
        if layer < N_A_LAYERS:
            a = layer
            mix_out, mem_q = gated_deltanet_mixer(h, gdn_w_in[a], gdn_conv[a], gdn_A_log[a],
                                                  gdn_dt_bias[a], gdn_norm[a])
        else:
            bl = layer - N_A_LAYERS
            proj = h @ swa_w_q[bl]
            q = apply_partial_rope(proj[..., :SWA_Q_W].reshape(b_sz, s_len, SWA_HEADS, SWA_DH), cos, sin)
            mix_out = sliding_window_attention(q, shared_k, shared_v, swa_sinks[bl])
            mem_q = proj[..., SWA_Q_W:]
        mem_o = memory_attention(mem_q.reshape(b_sz, s_len, MEM_HEADS, MEM_DH), mem_k, mem_v)
        x = x + jnp.concatenate([mix_out.astype(x.dtype), mem_o.astype(x.dtype)], axis=-1) @ w_out[layer]
        x = x + swiglu(rms_norm(x, ln_ffn[layer]), w_gate_up[layer], w_down[layer])
        if layer == N_A_LAYERS - 1:
            kv = rms_norm(x, ln_kv) @ w_kv
            shared_k = apply_partial_rope(kv[..., :KV_W].reshape(b_sz, s_len, SWA_KV_HEADS, SWA_DH), cos, sin)
            shared_v = kv[..., KV_W:].reshape(b_sz, s_len, SWA_KV_HEADS, SWA_DH)
    return rms_norm(x, ln_final)


DEPTH_2 = 1

Q_BLOCK = 128
ATTN_HEADS = 16
HEAD_DIM = 64
Q_RANK = 256
KV_RANK = 128
IDX_HEADS = 16
IDX_DIM = 64
TOPK_MAX = 256
NUM_BUCKETS = 32
MAX_DISTANCE = 128
D_INNER = 2 * D_MODEL
SSD_HEADDIM = 64
SSD_HEADS = D_INNER // SSD_HEADDIM
SSD_GROUPS = 8
D_STATE = 128
CONV_W = 4
CONV_DIM = D_INNER + 2 * SSD_GROUPS * D_STATE
D_FF_2 = -(-8 * D_MODEL // (3 * 256)) * 256
IN_SIZES = [Q_RANK, KV_RANK, IDX_DIM, IDX_HEADS, D_INNER, CONV_DIM, SSD_HEADS, D_MODEL, D_MODEL]
IN_COLS = int(sum(IN_SIZES))
IN_SPLITS = [int(v) for v in np.cumsum(IN_SIZES)[:-1]]


def rmsnorm(x, w):
    x32 = x.astype(jnp.float32)
    y = x32 * lax.rsqrt(jnp.mean(x32 * x32, axis=-1, keepdims=True) + EPS)
    return (y * w.astype(jnp.float32)).astype(x.dtype)

def t5_bucket(rel):
    half = NUM_BUCKETS // 2
    max_exact = half // 2
    side = jnp.where(rel > 0, half, 0)
    n = jnp.abs(rel)
    large = max_exact + (jnp.log(jnp.maximum(n, max_exact).astype(jnp.float32) / max_exact)
                         / math.log(MAX_DISTANCE / max_exact) * (half - max_exact)).astype(jnp.int32)
    large = jnp.minimum(large, half - 1)
    return side + jnp.where(n < max_exact, n, large)

def sparse_mla_attention(q_lat, kv_lat, k_idx_raw, w_idx_raw, positions,
                         q_norm, kv_norm, w_uq, w_uv, w_qidx, kidx_norm, rel_bias):
    Bsz, L, _ = q_lat.shape
    nb = L // Q_BLOCK
    k_sel_n = min(TOPK_MAX, L // 4)
    qn = rmsnorm(q_lat, q_norm)
    q = (qn @ w_uq).reshape(Bsz, L, ATTN_HEADS, KV_RANK)
    q_idx = (qn @ w_qidx).reshape(Bsz, L, IDX_HEADS, IDX_DIM)
    kv = rmsnorm(kv_lat, kv_norm)
    k_idx = rmsnorm(k_idx_raw, kidx_norm)
    w_idx = w_idx_raw * (IDX_HEADS ** -0.5 * IDX_DIM ** -0.5)
    key_chunk = positions // CHUNK
    scale = KV_RANK ** -0.5

    def to_blocks(a):
        return jnp.moveaxis(a.reshape((Bsz, nb, Q_BLOCK) + a.shape[2:]), 1, 0)

    def block_fn(args):
        q_b, qi_b, w_b, pos_b = args
        q_chunk = pos_b // CHUNK
        rel = jax.nn.relu(jnp.einsum('bqhd,bsd->bqhs', qi_b, k_idx).astype(jnp.float32))
        iscore = jnp.einsum('bqh,bqhs->bqs', w_b.astype(jnp.float32), rel)
        admissible = key_chunk[:, None, :] <= q_chunk[:, :, None]
        iscore = jnp.where(admissible, iscore, -jnp.inf)
        _, idx = lax.top_k(iscore, k_sel_n)
        kv_sel = jax.vmap(lambda kv_b, i_b: kv_b[i_b])(kv, idx)
        pos_sel = jax.vmap(lambda p_b, i_b: p_b[i_b])(positions, idx)
        valid = (pos_sel // CHUNK) <= q_chunk[..., None]
        bias = rel_bias[t5_bucket(pos_sel - pos_b[..., None])]
        logits = jnp.einsum('bqhc,bqkc->bhqk', q_b, kv_sel).astype(jnp.float32) * scale
        logits = logits + jnp.transpose(bias, (0, 3, 1, 2)).astype(jnp.float32)
        logits = jnp.where(valid[:, None], logits, -jnp.inf)
        probs = jax.nn.softmax(logits, axis=-1).astype(kv_sel.dtype)
        return jnp.einsum('bhqk,bqkc->bqhc', probs, kv_sel)

    o = lax.map(block_fn, (to_blocks(q), to_blocks(q_idx), to_blocks(w_idx), to_blocks(positions)))
    o = jnp.moveaxis(o, 0, 1).reshape(Bsz, L, ATTN_HEADS, KV_RANK)
    o = jnp.einsum('blhc,hcd->blhd', o, w_uv)
    return o.reshape(Bsz, L, ATTN_HEADS * HEAD_DIM)

def ssd_mixer(z, xbc, dt_raw, conv_w, conv_b, dt_bias, a_log, d_skip, ssd_norm):
    Bsz, L, _ = xbc.shape
    nc = L // CHUNK
    R = SSD_HEADS // SSD_GROUPS
    xbc = lax.conv_general_dilated(xbc, conv_w[:, None, :], window_strides=(1,),
                                   padding=[(CONV_W - 1, 0)],
                                   dimension_numbers=('NWC', 'WIO', 'NWC'),
                                   feature_group_count=CONV_DIM) + conv_b
    xbc = jax.nn.silu(xbc)
    xs, Bm, Cm = jnp.split(xbc, [D_INNER, D_INNER + SSD_GROUPS * D_STATE], axis=-1)
    dt = jax.nn.softplus((dt_raw + dt_bias).astype(jnp.float32))
    A = -jnp.exp(a_log.astype(jnp.float32))
    xh = xs.reshape(Bsz, L, SSD_HEADS, SSD_HEADDIM)
    X = (xh * dt[..., None]).reshape(Bsz, nc, CHUNK, SSD_GROUPS, R, SSD_HEADDIM)
    Bc = Bm.reshape(Bsz, nc, CHUNK, SSD_GROUPS, D_STATE)
    Cc = Cm.reshape(Bsz, nc, CHUNK, SSD_GROUPS, D_STATE)
    dA = (dt * A).reshape(Bsz, nc, CHUNK, SSD_GROUPS, R).transpose(0, 1, 3, 4, 2)
    a_cum = jnp.cumsum(dA, axis=-1)
    causal = jnp.tril(jnp.ones((CHUNK, CHUNK), dtype=bool))
    seg = jnp.where(causal, a_cum[..., :, None] - a_cum[..., None, :], -jnp.inf)
    Lmat = jnp.exp(seg)
    CB = jnp.einsum('bclgn,bcsgn->bcgls', Cc, Bc)
    y_diag = jnp.einsum('bcgls,bcgrls,bcsgrp->bclgrp', CB, Lmat, X)
    decay = jnp.exp(a_cum[..., -1:] - a_cum)
    states = jnp.einsum('bclgn,bcgrl,bclgrp->bcgrpn', Bc, decay, X)
    chunk_decay = jnp.exp(a_cum[..., -1])

    def step(h, inp):
        s_c, d_c = inp
        return h * d_c[..., None, None] + s_c, h

    h0 = jnp.zeros_like(states[:, 0])
    _, prev = lax.scan(step, h0, (jnp.moveaxis(states, 1, 0), jnp.moveaxis(chunk_decay, 1, 0)))
    prev = jnp.moveaxis(prev, 0, 1)
    y_off = jnp.einsum('bclgn,bcgrpn,bcgrl->bclgrp', Cc, prev, jnp.exp(a_cum))
    y = (y_diag + y_off).reshape(Bsz, L, SSD_HEADS, SSD_HEADDIM) + d_skip[:, None] * xh
    y = y.reshape(Bsz, L, D_INNER)
    return rmsnorm(y * jax.nn.silu(z), ssd_norm)

def second_inputs(seed: int = 0) -> dict:
    key = jax.random.key(seed)
    ks = jax.random.split(key, 32)
    nrm = lambda k, shape, s: jax.random.normal(k, shape, jnp.float32) * s
    gain = lambda k, n: 1.0 + 0.05 * jax.random.normal(k, (n,), jnp.float32)
    offset = jax.random.randint(ks[2], (BATCH, 1), 0, 16) * CHUNK
    positions = (offset + jnp.arange(SEQ, dtype=jnp.int32)[None, :]).astype(jnp.int32)
    dt0 = jnp.exp(jax.random.uniform(ks[20], (SSD_HEADS,), jnp.float32, math.log(1e-3), math.log(1e-1)))
    return {
        "x": nrm(ks[0], (BATCH, SEQ, D_MODEL), 1.0),
        "c": nrm(ks[1], (BATCH, D_MODEL), 1.0),
        "positions": positions,
        "ada_w": nrm(ks[3], (D_MODEL, 6 * D_MODEL), 0.5 * D_MODEL ** -0.5),
        "ada_b": nrm(ks[4], (6 * D_MODEL,), 0.02),
        "pre_norm_mix": gain(ks[5], D_MODEL),
        "post_norm_mix": gain(ks[6], D_MODEL),
        "pre_norm_ffn": gain(ks[7], D_MODEL),
        "post_norm_ffn": gain(ks[8], D_MODEL),
        "w_in": nrm(ks[9], (D_MODEL, IN_COLS), D_MODEL ** -0.5),
        "q_norm": gain(ks[10], Q_RANK),
        "kv_norm": gain(ks[11], KV_RANK),
        "w_uq": nrm(ks[12], (Q_RANK, ATTN_HEADS * KV_RANK), Q_RANK ** -0.5),
        "w_uv": nrm(ks[13], (ATTN_HEADS, KV_RANK, HEAD_DIM), KV_RANK ** -0.5),
        "rel_bias": nrm(ks[14], (NUM_BUCKETS, ATTN_HEADS), 0.3),
        "w_qidx": nrm(ks[15], (Q_RANK, IDX_HEADS * IDX_DIM), Q_RANK ** -0.5),
        "kidx_norm": gain(ks[16], IDX_DIM),
        "conv_w": nrm(ks[17], (CONV_W, CONV_DIM), CONV_W ** -0.5),
        "conv_b": nrm(ks[18], (CONV_DIM,), 0.02),
        "dt_bias": dt0 + jnp.log(-jnp.expm1(-dt0)),
        "a_log": jnp.log(jax.random.uniform(ks[21], (SSD_HEADS,), jnp.float32, 1.0, 16.0)),
        "d_skip": 1.0 + 0.1 * jax.random.normal(ks[22], (SSD_HEADS,), jnp.float32),
        "ssd_norm": gain(ks[23], D_INNER),
        "w_o_attn": nrm(ks[24], (ATTN_HEADS * HEAD_DIM, D_MODEL), (ATTN_HEADS * HEAD_DIM) ** -0.5),
        "w_o_ssd": nrm(ks[25], (D_INNER, D_MODEL), D_INNER ** -0.5),
        "w_out": nrm(ks[26], (D_MODEL, D_MODEL), D_MODEL ** -0.5),
        "w_ffn_in": nrm(ks[27], (D_MODEL, 2 * D_FF_2), D_MODEL ** -0.5),
        "w_ffn_out": nrm(ks[28], (D_FF_2, D_MODEL), D_FF_2 ** -0.5),
    }

def second_block(x, c, positions, ada_w, ada_b, pre_norm_mix, post_norm_mix, pre_norm_ffn,
              post_norm_ffn, w_in, q_norm, kv_norm, w_uq, w_uv, rel_bias, w_qidx, kidx_norm,
              conv_w, conv_b, dt_bias, a_log, d_skip, ssd_norm, w_o_attn, w_o_ssd, w_out,
              w_ffn_in, w_ffn_out):
    mod = (jax.nn.silu(c) @ ada_w + ada_b)[:, None, :]
    shift_m, scale_m, gate_m, shift_f, scale_f, gate_f = jnp.split(mod, 6, axis=-1)
    for _ in range(DEPTH_2):
        h = rmsnorm(x, pre_norm_mix) * (1.0 + scale_m) + shift_m
        proj = h @ w_in
        q_lat, kv_lat, k_idx, w_idx, z, xbc, dt_raw, g_a, g_b = jnp.split(proj, IN_SPLITS, axis=-1)
        y_a = sparse_mla_attention(q_lat, kv_lat, k_idx, w_idx, positions, q_norm, kv_norm,
                                   w_uq, w_uv, w_qidx, kidx_norm, rel_bias) @ w_o_attn
        y_b = ssd_mixer(z, xbc, dt_raw, conv_w, conv_b, dt_bias, a_log, d_skip, ssd_norm) @ w_o_ssd
        mix = (jax.nn.sigmoid(g_a) * y_a + jax.nn.sigmoid(g_b) * y_b) @ w_out
        x = x + gate_m * rmsnorm(mix, post_norm_mix)
        h2 = rmsnorm(x, pre_norm_ffn) * (1.0 + scale_f) + shift_f
        u_gate, u_up = jnp.split(h2 @ w_ffn_in, 2, axis=-1)
        f = (jax.nn.silu(u_gate) * u_up) @ w_ffn_out
        x = x + gate_f * rmsnorm(f, post_norm_ffn)
    return x


def setup_inputs(seed=0):
    out = dict(first_inputs(seed))
    for name, value in second_inputs(seed + 1).items():
        if name != "x":
            out[name + "_2"] = value
    return out


def reference(
    x, mem, positions, ln_mix, ln_ffn, ln_mem, w_mem_kv, w_out, w_gate_up, w_down, gdn_w_in,
    gdn_conv, gdn_A_log, gdn_dt_bias, gdn_norm, swa_w_q, swa_sinks, ln_kv, w_kv, ln_final, c_2,
    positions_2, ada_w_2, ada_b_2, pre_norm_mix_2, post_norm_mix_2, pre_norm_ffn_2,
    post_norm_ffn_2, w_in_2, q_norm_2, kv_norm_2, w_uq_2, w_uv_2, rel_bias_2, w_qidx_2,
    kidx_norm_2, conv_w_2, conv_b_2, dt_bias_2, a_log_2, d_skip_2, ssd_norm_2, w_o_attn_2,
    w_o_ssd_2, w_out_2, w_ffn_in_2, w_ffn_out_2,
):
    x = first_block(
        x, mem, positions, ln_mix, ln_ffn, ln_mem, w_mem_kv, w_out, w_gate_up, w_down, gdn_w_in,
        gdn_conv, gdn_A_log, gdn_dt_bias, gdn_norm, swa_w_q, swa_sinks, ln_kv, w_kv, ln_final,
    )
    return second_block(
        x, c_2, positions_2, ada_w_2, ada_b_2, pre_norm_mix_2, post_norm_mix_2, pre_norm_ffn_2,
        post_norm_ffn_2, w_in_2, q_norm_2, kv_norm_2, w_uq_2, w_uv_2, rel_bias_2, w_qidx_2,
        kidx_norm_2, conv_w_2, conv_b_2, dt_bias_2, a_log_2, d_skip_2, ssd_norm_2, w_o_attn_2,
        w_o_ssd_2, w_out_2, w_ffn_in_2, w_ffn_out_2,
    )


_drawn_inputs = setup_inputs


def setup_inputs(seed=0):
    import zlib

    import numpy as np

    out = dict(_drawn_inputs(seed))
    spreads = {}
    factors = {'ln_mix': 2.789,
     'ln_mem': 8.0,
     'gdn_norm': 4.174,
     'swa_sinks': 8.0,
     'ln_kv': 8.0,
     'post_norm_mix_2': 3.794,
     'pre_norm_ffn_2': 2.822,
     'post_norm_ffn_2': 4.09,
     'q_norm_2': 7.847,
     'kv_norm_2': 8.0,
     'rel_bias_2': 5.514,
     'kidx_norm_2': 8.0,
     'conv_b_2': 7.989,
     'd_skip_2': 3.503,
     'ssd_norm_2': 10.905}
    for name, (base, spread) in spreads.items():
        noise = np.random.default_rng([zlib.crc32(name.encode()), seed]).standard_normal(out[name].shape)
        drawn = base * np.exp(spread * noise) if base else spread * noise
        out[name] = jnp.asarray(drawn.astype(out[name].dtype))
    for name, factor in factors.items():
        out[name] = (out[name] * factor).astype(out[name].dtype)
    return out
```

```python
import math
from contextlib import ExitStack

import numpy as np

import concourse.bass as bass
from concourse import mybir

F32 = mybir.dt.float32
F32R = mybir.dt.float32r
BF16 = mybir.dt.bfloat16
I32 = mybir.dt.int32
ALU = mybir.AluOpType
ACT = mybir.ActivationFunctionType
AX = mybir.AxisListType.X

P = 128
T = 512
D = 1024
KT = D // P
MEM = 256
HG = 6
NC = T // P
FF = 2816
FT = FF // P
CHUNKS = [8, 8, 6]
EPS = 1e-6
NEG = -1e30
ROUND = 12582912.0
PI2 = (6.28125, 0.0019340515136718750, 1.2556659146e-06)
PI_IN = 3.14159250
ROPE_LOADS = 4
ROPE_AFTER = [(), (6, 0, 1), (2, 3), (4, 5)]
NG = 64
RD = 16
FILL, MARK = -3.0e38, -3.4e38
BUCKET_STEPS = (12, 16, 23, 32, 46, 64, 91)
UW = 2048


def unit_list():
    units = []

    def add(name, n):
        units.extend((name, i) for i in range(n))

    def ffn(f):
        for name, c in (("gu", 0), ("gu", 1), ("dn", 0), ("gu", 2), ("dn", 1), ("dn", 2)):
            add(f"{name}{f}{c}", CHUNKS[c] if name == "gu" else 4)

    add("mem", 4)
    add("ba", 1)
    add("qkv", 9)
    add("z", 3)
    add("memq", 1)
    add("wout0", 4)
    ffn(0)
    add("kv", 1)
    add("swaq", 4)
    add("ada", 24)
    add("wout1", 4)
    ffn(1)
    add("qlat", 1)
    add("misc", 1)
    add("zed", 8)
    add("qidx", 1)
    add("xbc", 16)
    add("gab", 8)
    add("uq", 2)
    add("oattn", 4)
    add("ossd0", 4)
    add("ossd1", 4)
    add("wout2", 4)
    ffn(2)
    return units


UNITS = unit_list()
NU = len(UNITS)
U = {}
for _u, (_name, _i) in enumerate(UNITS):
    U[_name, _i] = _u


def attention_items(layer):
    items = []
    if layer == 1:
        items += [("swa", t, b) for t in range(6) for b in range(NC)]
    items += [("mem", t, b) for t in range(2) for b in range(NC)]
    return items


class Banks:

    def __init__(self):
        self.uses = [0] * 8
        self.at = {}

    def add(self, key, bank):
        assert key not in self.at, key
        self.at[key] = (bank, self.uses[bank])
        self.uses[bank] += 1

    def rotate(self, keys, banks):
        for i, key in enumerate(keys):
            self.add(key, banks[i % len(banks)])


def bank_plan():
    k = Banks()

    def units(name, tiles=2):
        i = 0
        while (name, i) in U:
            u = U[name, i]
            for t in range(tiles):
                k.add(("unit", u, t), 2 * (u % 2) + t % 2 if tiles < 8 else t % 4)
            i += 1

    def ffn(f):
        for name in ("gu", 0), ("gu", 1), ("dn", 0), ("gu", 2), ("dn", 1), ("dn", 2):
            units(f"{name[0]}{f}{name[1]}")

    def attention(layer):
        items = attention_items(layer)
        for n in range(len(items) + 2):
            if n < len(items):
                for s in range(2):
                    k.add(("score", layer, n, s), (4, 2)[n % 2] + s)
            if 1 <= n <= len(items):
                k.add(("turn", layer, n - 1), 6 + (n - 1) % 2)
            if n >= 2 and items[n - 2][2] == 0:
                k.add(("value", layer, (n - 2) // NC), 0)
            if layer == 1:
                if 1 <= n <= 24:
                    k.add(("ada_turn", n - 1), 1)
                if n < 24:
                    k.add(("unit", U["ada", n], 0), 1)

    k.add(("norm", 0), 4)
    units("mem")
    k.add(("norm", 1), 4)
    units("ba", 1)
    k.add(("cols",), 6)
    k.add(("l2",), 4)
    units("qkv")
    units("z")
    units("memq")
    k.rotate([("l2b", j) for j in range(2 * HG)], [5, 6, 7])
    k.rotate([(x, h) for h in range(HG) for x in ("gm", "gp", "bb", "kk", "qk")], range(8))
    k.rotate([(x, lv, h) for lv in range(7) for x in ("iz", "iw") for h in range(HG)
              for x in ([x] if x == "iz" else ["iw", "iv"]) if not (x == "iw" and lv == 6)], range(8))
    k.rotate([(x, h) for h in range(HG) for x in ("vt", "kt")], range(8))
    for c in range(NC):
        k.rotate([(x, c, h) for x in ("ks", "vn") for h in range(HG) if c or x == "vn"], range(8))
        k.rotate([(x, c, h) for h in range(HG) for x in ("oo", "su") if c < NC - 1 or x == "oo"], range(8))
    k.add(("onorm",), 0)
    k.rotate([("ob", h) for h in range(HG)], [1, 2, 3])
    attention(0)
    units("wout0")
    k.add(("norm", 2), 4)
    ffn(0)
    k.add(("norm", 3), 4)
    units("kv")
    units("swaq")
    k.rotate([("rope", j) for j in (6, 0, 1, 2, 3, 4, 5)], [4, 5, 6, 7])
    attention(1)
    units("wout1")
    k.add(("norm", 5), 4)
    ffn(1)
    k.add(("norm", 6), 4)
    k.add(("norm", 7), 4)
    units("qlat")
    units("misc")
    units("zed")
    for i, name in enumerate(("qn", "kvn", "kin", "kid", "kvt", "c1", "c2", "cl")):
        k.add((name,), 4 + i % 4)
    units("qidx", 8)
    for i in range(24):
        name, j = ("xbc", i) if i < 16 else ("gab", i - 16)
        for t in range(2):
            k.add(("unit", U[name, j], t), 2 * (U[name, j] % 2) + t)
        for n in (2 * i, 2 * i + 1):
            if n < 32:
                for s in range(2):
                    k.add(("index", n, s), 4 + 2 * (n % 2) + s)
    units("uq", 8)
    for n in range(NG + 5):
        if n < NG:
            for e in range(2):
                k.add(("ohb", n, e), e)
        if 1 <= n <= NG:
            k.add(("logit", n - 1), 2 + (n - 1) % 2)
        if 3 <= n < NG + 3:
            k.add(("ptp", n - 3), 4 + (n - 3) % 2)
        if n >= 4 and (n - 4) % 4 == 3:
            k.add(("latent", (n - 4) // 4), 6 + (n - 4) // 4 % 2)
    k.rotate([("uv", t) for t in range(8)], [0, 1, 2, 3])
    units("oattn")
    for part in range(2):
        for g in range(4 * part, 4 * part + 4):
            k.add(("bt", g), 0)
            k.rotate([("xt", g, t) for t in range(2)], [1, 2])
            k.add(("cb", g), 3)
            for c in range(NC - 1):
                k.add(("st", g, c), 1)
            for t in range(2):
                for s in range(2):
                    k.add(("lm", g, t, s), 4 + s)
                k.add(("ea", g, t), 6)
                k.add(("yd", g, t), 0)
                k.add(("yo", g, t), 2)
        units(f"ossd{part}")
    k.add(("ssn",), 7)
    units("wout2")
    k.add(("post", 0), 4)
    k.add(("norm", 8), 4)
    ffn(2)
    k.add(("post", 1), 4)
    return k.at


BANK = bank_plan()
COUNT = {name: sum(n == name for n, _ in UNITS) for name, _ in UNITS}
LAST_TILE = [{"ba": 0, "ada": 0, "qidx": 7, "uq": 7}.get(name, 1) for name, _ in UNITS]


def build(nc, I, O):
    ctx = ExitStack()
    with ctx:
        names = {}

        def S(name):
            if name not in names:
                names[name] = ctx.enter_context(nc.semaphore(name))
            return names[name]

        def sb(name, shape, dt, scope=ctx):
            return scope.enter_context(nc.sbuf_tensor(name, shape, dt))

        banks = ctx.enter_context(nc.psum_tensor("banks", [P, 8, T], F32))
        psum = [banks[:, b, :] for b in range(8)]
        bank_full = [S(f"bank_full{b}") for b in range(8)]
        bank_read = [S(f"bank_read{b}") for b in range(8)]

        def bank(key):
            return psum[BANK[key][0]]

        def open_bank(pe, key):
            b, n = BANK[key]
            if n:
                pe.wait_ge(bank_read[b], n)

        def fills(key):
            return bank_full[BANK[key][0]]

        def full(eng, key):
            b, n = BANK[key]
            eng.wait_ge(bank_full[b], n + 1)

        def reads(key):
            return bank_read[BANK[key][0]]

        def taken(eng, key):
            b, n = BANK[key]
            eng.wait_ge(bank_read[b], n + 1)

        x = sb("x", [P, KT, T], F32)
        raw = sb("raw", [P, 2, UW], F32)
        w_hi = sb("w_hi", [P, 2, UW], F32R)
        w_lo = sb("w_lo", [P, 2, UW], F32R)
        rs = sb("rs", [P, T], F32)
        ident = sb("ident", [P, P], F32)
        identb = sb("identb", [P, P], BF16)
        ones = sb("ones", [P, P], F32)
        eps = sb("eps", [P, 1], F32)
        gains = sb("gains", [P, 7, KT], F32)
        mem_k = sb("mem_k", [P, 2, 2, MEM], F32)
        mem_v = sb("mem_v", [P, 2, 2, MEM], F32)
        mem_q = sb("mem_q", [P, 2, T], F32)
        stat = sb("stat", [P, 2, 5, 2], F32)
        sinks = sb("sinks", [P, 8, 2], F32)
        nsinks = sb("nsinks", [P, 8, 2], F32)
        mod = sb("mod", [P, 48], F32)
        gain2 = sb("gain2", [P, 4, KT], F32)
        c_col = sb("c_col", [P, KT], F32)
        c_pair = sb("c_pair", [P, KT, 2], F32R)
        arow = sb("arow", [2, 2, 256], F32)

        with ExitStack() as core:
            lt = sb("lt", [P, HG, T], F32, core)
            at = sb("at", [P, HG, T], F32, core)
            xi = sb("xi", [P, HG, T], F32, core)
            xt = sb("xt", [P, HG, T], F32, core)
        with ExitStack() as lat:
            qsel4 = sb("qsel4", [P, 32 * P], BF16, lat)
            qsel8 = sb("qsel8", [P, 16 * P], BF16, lat)
            oh = sb("oh", [P, 2, 2, T], F32R, lat)
            pr2 = sb("pr2", [P, 3, T], F32, lat)
            ptt = sb("ptt", [P, 2, NC, T], F32, lat)
            tbl = sb("tbl", [P, 2 * P], F32, lat)
            tbl_hi = sb("tbl_hi", [P, 2 * P], F32R, lat)
            tbl_lo = sb("tbl_lo", [P, 2 * P], F32R, lat)
        hn_hi = sb("hn_hi", [P, KT, T], F32R)
        hn_lo = sb("hn_lo", [P, KT, T], F32R)
        tmp = sb("tmp", [P, KT, T], F32)
        with ExitStack() as s1:
            qkv = sb("qkv", [P, 3 * HG, T], F32, s1)
            zs = sb("zs", [P, HG, T], F32, s1)
            bg = sb("bg", [64, T], F32, s1)
            rows = sb("rows", [64, T], F32, s1)
            cols = sb("cols", [P, NC, 64], F32, s1)
            nbe = sb("nbe", [P, NC, HG], F32, s1)
            elast = sb("elast", [P, HG, NC], F32, s1)
            glast = sb("glast", [P, HG, NC], F32, s1)
            cw = sb("cw", [P, 3 * HG, 4], F32, s1)
            gcst = sb("gcst", [64, 2], F32, s1)
            gng = sb("gng", [P, 1], F32, s1)
            col1 = sb("col1", [P, 127], F32, s1)
            sel = sb("sel", [64, 2 * HG, P], F32, s1)
            mask4 = sb("mask4", [P, T], BF16, s1)
            strict = sb("strict", [P, P], F32, s1)
            levels = sb("levels", [P, 7, P], F32, s1)
            with ExitStack() as z1:
                bt = sb("bt", [64, 3, T], F32, z1)
                reset = sb("reset", [64, T], F32, z1)
                sq = sb("sq", [P, 2, T], F32, z1)
            with ExitStack() as z2:
                kb = sb("kb", [P, 2, T], F32, z2)
                dec = sb("dec", [P, 2, T], F32, z2)
                eg = sb("eg", [P, 2, T], F32, z2)
            with ExitStack() as z3:
                zm = sb("zm", [P, HG, T], F32, z3)
            with ExitStack() as z4:
                state = sb("state", [P, HG, P], F32, z4)
                vn = sb("vn", [P, HG, P], F32, z4)
                rr = sb("rr", [P, HG, P], F32, z4)
                osq = sb("osq", [P, T], F32, z4)
        with ExitStack() as s2:
            pr = sb("pr", [P, 2, 2, 256], F32, s2)
            pt = sb("pt", [P, 2, T], F32, s2)
            qr = sb("qr", [P, 6, T], F32, s2)
            kr = sb("kr", [P, T], F32, s2)
            qraw = sb("qraw", [P, 7, T], F32, s2)
            vs = sb("vs", [P, NC, P], F32, s2)
            cosv = sb("cosv", [P, T], F32, s2)
            sinv = sb("sinv", [P, T], F32, s2)
            ang = sb("ang", [P, 4, T], F32, s2)
            posi = sb("posi", [P, T], I32, s2)
            rcol = sb("rcol", [P, 2], F32, s2)
            perm = sb("perm", [P, P], F32, s2)
            band = sb("band", [P, 256], BF16, s2)
        with ExitStack() as s3:
            hid_hi = sb("hid_hi", [P, 2, 8, T], F32R, s3)
            hid_lo = sb("hid_lo", [P, 2, 8, T], F32R, s3)
            sg = sb("sg", [P, 2, T], F32, s3)
            prod = sb("prod", [P, 2, T], F32, s3)
        with ExitStack() as s4:
            c1 = sb("c1", [P, NC, P], F32, s4)
            c2 = sb("c2", [P, NC, 32], F32, s4)
            r2 = sb("r2", [P, T], F32, s4)
            small2 = sb("small2", [P, 6], F32, s4)
            cw2 = sb("cw2", [P, 32, 5], F32, s4)
            dskip = sb("dskip", [P, 16], F32, s4)
            ssdg = sb("ssdg", [P, 16], F32, s4)
            mask2 = sb("mask2", [P, T], BF16, s4)
            tolast = sb("tolast", [P, NC, 32], F32, s4)
            cdall = sb("cdall", [P, 32, NC], F32, s4)
            with ExitStack() as s5:
                qh = sb("qh", [P, T * 16], F32, s5)
                r1 = sb("r1", [P, T], F32, s5)
                kvf = sb("kvf", [P, T], F32, s5)
                kvt = sb("kvt", [P, NC, P], F32, s5)
                ki = sb("ki", [P, T], F32, s5)
                madd = sb("madd", [P, NC, T], BF16, s5)
                bkt = sb("bkt", [P, NC, T], BF16, s5)
                cs = sb("cs", [P, 2, T], F32, s5)
                qn_hi = sb("qn_hi", [P, 2, T], F32R, s5)
                qn_lo = sb("qn_lo", [P, 2, T], F32R, s5)
                wcol = sb("wcol", [P, NC, 16], F32, s5)
                m8 = sb("m8", [P, 2, 8], F32, s5)
                qpi = sb("qpi", [P, 4], I32, s5)
                qpc = sb("qpc", [P, 2, 4], F32, s5)
                bcol = sb("bcol", [P, 1], F32, s5)
                st2 = sb("st2", [P, 3, 4], F32, s5)
                wuv = sb("wuv", [P, 16 * 64], F32, s5)
            with ExitStack() as s6:
                qi = sb("qi", [P, 8, T], F32, s6)
                reset2 = sb("reset2", [P, T], F32, s6)
                relu = sb("relu", [P, 2, T], F32, s6)
                oneh = sb("oneh", [P, T], F32, s6)
                cs2 = sb("cs2", [P, T], F32, s6)
                diag = sb("diag", [P, 32, NC], F32, s6)
            with ExitStack() as s7:
                ma = sb("ma", [P, KT, T], F32, s7)
                grp = sb("grp", [P, 2, 4, T], F32, s7)
                zt = sb("zt", [P, 2, 2, T], F32, s7)
                ysq = sb("ysq", [P, 2, T], F32, s7)
                btok = sb("btok", [P, NC, P], F32, s7)
                xd = sb("xd", [P, NC, 2, P], F32, s7)
                xdk = sb("xdk", [P, NC - 1, 2, P], F32, s7)
                lb = sb("lb", [P, 2, T], F32, s7)
                mt = sb("mt", [P, 2, T], F32, s7)
                ea = sb("ea", [P, T], F32, s7)
                ysd = sb("ysd", [P, 2, T], F32, s7)
                sst = sb("sst", [P, 3, 2, P], F32, s7)

        spill = nc.dram_tensor("spill", [64, P, T], F32, kind="Internal").ap()

        w_land = [S("w_land0"), S("w_land1")]
        W3 = lambda ap, slot: ap[:, slot, :].rearrange("p (k c) -> p k c", k=KT)

        def prep_hi(act, u, i=0):
            if isinstance(i, int) and u + 2 + 2 * i >= NU:
                return
            slot = u % 2
            act.wait_ge(w_land[slot], (i + ((u + 2) // 2 + 1)) * 16)
            b, n = BANK["unit", u, LAST_TILE[u]]
            act.wait_ge(bank_full[b], i + (n + 1))
            act.activation(w_hi[:, slot, :], raw[:, slot, :], ACT.Copy).then_inc(S("w_hi"), 1)

        def unit_jobs(pe, u, i, xh, xl, nkt, n=T, ready=None):
            pe.wait_ge(S("w_lo"), i * 2 + (u + 1))
            hi, lo = W3(w_hi, u % 2), W3(w_lo, u % 2)
            for t in range(LAST_TILE[u] + 1):
                b, n0 = BANK["unit", u, t]
                if not (isinstance(i, int) and i + n0 == 0):
                    pe.wait_ge(bank_read[b], i + n0)
                out = psum[b][:, 0:n]
                for k in range(nkt):
                    if ready and t == 0:
                        ready(k)
                    wh, wl = hi[:, k, t * P:(t + 1) * P], lo[:, k, t * P:(t + 1) * P]
                    pe.matmul(out, wh, xh(k), start=(k == 0), stop=False)
                    pe.matmul(out, wh, xl(k), start=False, stop=False)
                    mm = pe.matmul(out, wl, xh(k), start=False, stop=(k == nkt - 1))
                mm.then_inc(bank_full[b], 1)

        def over_units(eng, name, body, first=0):
            n = COUNT[name]
            u0 = U[name, 0] + first
            pairs = (n - first) // 2
            if u0 + n - first + 2 > NU:
                pairs = 0
            if pairs >= 2:
                with eng.Fori(0, pairs) as i:
                    body(u0, i)
                    body(u0 + 1, i)
            else:
                pairs = 0
            for u in range(u0 + 2 * pairs, U[name, 0] + n):
                body(u, 0)

        hn_of = (lambda k: hn_hi[:, k, :], lambda k: hn_lo[:, k, :])

        def pe_linear(pe, name, nkt=KT, ready=None):
            first = 0
            if ready:
                unit_jobs(pe, U[name, 0], 0, *hn_of, nkt, ready=ready)
                first = 1
            if first < COUNT[name]:
                over_units(pe, name, lambda u, i: unit_jobs(pe, u, i, *hn_of, nkt), first)

        def act_norm(a, i, src, n, ready):
            for k in range(KT):
                ready(a, k)
                a.activation(tmp[:, k, 0:n], src(k), ACT.Square).then_inc(S("squared"), 1)
            full(a, ("norm", i))
            a.activation(rs[:, 0:n], bank(("norm", i))[:, 0:n], ACT.Sqrt, bias=eps[:, 0:1],
                         scale=1.0 / D).then_inc(reads(("norm", i)), 1)

        def act_norm_round(a, i, n=T):
            if i == 4:
                full(a, ("unit", U["kv", 0], 1))
            for k in range(KT):
                a.wait_ge(S("normed"), KT * i + k + 1)
                a.activation(hn_hi[:, k, 0:n], tmp[:, k, 0:n], ACT.Copy).then_inc(S("hn_hi"), 1)

        def pe_norm(pe, i, n, rank):
            open_bank(pe, ("norm", i))
            for k in range(KT):
                pe.wait_ge(S("squared"), KT * rank + k + 1)
                mm = pe.matmul(bank(("norm", i))[:, 0:n], ones[:, :], tmp[:, k, 0:n], start=(k == 0),
                               stop=(k == KT - 1))
            mm.then_inc(fills(("norm", i)), 1)

        def dve_rstd(v, i, n, rank):
            taken(v, ("norm", i))
            v.reciprocal(rs[:, 0:n], rs[:, 0:n]).then_inc(S("rstd"), 1)
            v.wait_ge(S("rstd"), rank + 1)

        def dve_norm(v, i, g, src, n=T):
            def low(k):
                v.wait_ge(S("hn_hi"), KT * i + k + 1)
                v.tensor_tensor(hn_lo[:, k, 0:n], tmp[:, k, 0:n], hn_hi[:, k, 0:n].bitcast(F32),
                                ALU.subtract).then_inc(S("hn_lo"), 1)
            for k in range(KT):
                v.scalar_tensor_tensor(out=tmp[:, k, 0:n], in0=src(k), scalar=gains[:, g, k:k + 1],
                                       in1=rs[:, 0:n], op0=ALU.mult, op1=ALU.mult).then_inc(S("normed"), 1)
                if k:
                    low(k - 1)
            low(KT - 1)

        def hn_ready(pe, i):
            return lambda k: pe.wait_ge(S("hn_lo"), KT * i + k + 1)

        x_of = lambda k: x[:, k, :]
        memx = qkv[:, 0:4, :].rearrange("p a (b t) -> p (a b) t", b=2)
        mem_of = lambda k: memx[:, k, :]

        def after_units(name):
            return lambda eng, k: taken(eng, ("unit", U[name, k // 2], k % 2))

        def over_ffn(f, gate_up, down):
            for kind, c in (("gu", 0), ("gu", 1), ("dn", 0), ("gu", 2), ("dn", 1), ("dn", 2)):
                (gate_up if kind == "gu" else down)(f"{kind}{f}{c}", c)

        def pe_ffn(pe, f, ready):
            def gate_up(name, c):
                pe_linear(pe, name, ready=ready if c == 0 else None)

            def down(name, c):
                pe.wait_ge(S("hid_lo"), FT * f + sum(CHUNKS[:c + 1]))
                over_units(pe, name, lambda u, j: unit_jobs(
                    pe, u, j, lambda k: hid_hi[:, c % 2, k, :], lambda k: hid_lo[:, c % 2, k, :], CHUNKS[c]))
            over_ffn(f, gate_up, down)

        def act_ffn(a, f):
            def gate_up(name, c):
                u0 = U[name, 0]

                def body(u, i):
                    q = (u - u0) % 2
                    bg_, ng = BANK["unit", u, 0]
                    a.wait_ge(bank_full[bg_], i + (ng + 1))
                    a.activation(sg[:, q, :], psum[bg_][:, :], ACT.Silu).then_inc(bank_read[bg_], 1)
                    prep_hi(a, u, i)
                    bu, nu = BANK["unit", u, 1]
                    a.wait_ge(bank_read[bu], i + (nu + 1))
                    a.activation(hid_hi[:, c % 2, i * 2 + (u - u0), :], prod[:, q, :], ACT.Copy)\
                        .then_inc(S("hid_hi"), 1)
                over_units(a, name, body)

            def down(name, c):
                over_units(a, name, lambda u, i: prep_hi(a, u, i))
            over_ffn(f, gate_up, down)

        def dve_ffn(v, f):
            def gate_up(name, c):
                u0 = U[name, 0]
                h0 = FT * f + sum(CHUNKS[:c])

                def body(u, i):
                    q = (u - u0) % 2
                    bu, nu = BANK["unit", u, 1]
                    bg_, ng = BANK["unit", u, 0]
                    v.wait_ge(bank_read[bg_], i + (ng + 1))
                    v.wait_ge(bank_full[bu], i + (nu + 1))
                    v.tensor_tensor(prod[:, q, :], sg[:, q, :], psum[bu][:, :], ALU.mult).then_inc(bank_read[bu], 1)
                    v.wait_ge(bank_read[bu], i + (nu + 1))
                    v.wait_ge(S("hid_hi"), i * 2 + (h0 + u - u0 + 1))
                    v.tensor_tensor(hid_lo[:, c % 2, i * 2 + (u - u0), :], prod[:, q, :],
                                    hid_hi[:, c % 2, i * 2 + (u - u0), :].bitcast(F32),
                                    ALU.subtract).then_inc(S("hid_lo"), 1)
                over_units(v, name, body)

            def down(name, c):
                if f == 2:
                    dve_gather(v, name, c > 0)
                else:
                    dve_residual(v, name)
            over_ffn(f, gate_up, down)

        def dve_residual(v, name):
            u0 = U[name, 0]

            def body(u, i):
                for t in range(2):
                    b, n = BANK["unit", u, t]
                    v.wait_ge(bank_full[b], i + (n + 1))
                    xk = x[:, i * 4 + (2 * (u - u0) + t), :]
                    v.tensor_tensor(xk, xk, psum[b][:, :], ALU.add).then_inc(bank_read[b], 1)
            over_units(v, name, body)

        def dve_gather(v, name, add):
            u0 = U[name, 0]

            def body(u, i):
                for t in range(2):
                    b, n = BANK["unit", u, t]
                    v.wait_ge(bank_full[b], i + (n + 1))
                    tk = tmp[:, i * 4 + (2 * (u - u0) + t), :]
                    if add:
                        v.tensor_tensor(tk, tk, psum[b][:, :], ALU.add).then_inc(bank_read[b], 1)
                    else:
                        v.tensor_copy(tk, psum[b][:, :]).then_inc(bank_read[b], 1)
            over_units(v, name, body)

        def pe_mem(pe):
            for layer in range(2):
                u = U["mem", 2 * layer]
                unit_jobs(pe, u, 0, lambda k: hn_hi[:, k, 0:MEM], lambda k: hn_lo[:, k, 0:MEM], KT, n=MEM,
                          ready=hn_ready(pe, 0))
                u += 1
                pe.wait_ge(S("w_lo"), u + 1)
                hi, lo = W3(w_hi, u % 2), W3(w_lo, u % 2)
                for t in range(2):
                    key = ("unit", u, t)
                    open_bank(pe, key)
                    for k in range(KT):
                        xh, xl = hn_hi[:, k, t * P:(t + 1) * P], hn_lo[:, k, t * P:(t + 1) * P]
                        pe.matmul(bank(key)[:, 0:MEM], xh, hi[:, k, :], start=(k == 0), stop=False)
                        pe.matmul(bank(key)[:, 0:MEM], xh, lo[:, k, :], start=False, stop=False)
                        mm = pe.matmul(bank(key)[:, 0:MEM], xl, hi[:, k, :], start=False, stop=(k == KT - 1))
                    mm.then_inc(fills(key), 1)

        def dve_mem(v):
            for layer in range(2):
                for what, u in ((mem_k, U["mem", 2 * layer]), (mem_v, U["mem", 2 * layer + 1])):
                    for t in range(2):
                        key = ("unit", u, t)
                        full(v, key)
                        v.tensor_copy(what[:, layer, t, :], bank(key)[:, 0:MEM]).then_inc(reads(key), 1)

        def att_args(layer, n):
            kind, t, b = attention_items(layer)[n]
            if kind == "mem":
                halves = [mem_v[:, layer, m, t * P:(t + 1) * P] for m in range(2)]
                return kind, t, b, mem_q, mem_k[:, layer, t, :], halves, 6 + t
            k0 = (b - 1) * P if b else 0
            halves = [vs[:, m, :] for m in ([b - 1, b] if b else [0])]
            return kind, t, b, qr, kr[:, k0:(b + 1) * P], halves, t

        ATT0 = len(attention_items(0))
        V0 = 2

        def pe_attention(pe, layer, ready):
            items = attention_items(layer)
            g0 = ATT0 * layer
            for n in range(len(items) + 2):
                if n < len(items):
                    kind, t, b, q, keys, halves, _ = att_args(layer, n)
                    w = P * len(halves)
                    key = [("score", layer, n, s_) for s_ in range(2)]
                    ready(pe, kind, t)
                    for s_ in range(2):
                        open_bank(pe, key[s_])
                        if kind == "swa":
                            pe.matmul(bank(key[s_])[:, 0:w], identb[:, :], band[:, 256 - w:256],
                                      start=True, stop=False)
                    for s_ in range(2):
                        h = slice(64 * s_, 64 * s_ + 64)
                        pe.matmul(bank(key[s_])[:, 0:w], q[h, t, b * P:(b + 1) * P], keys[h, :],
                                  start=(kind == "mem"), stop=True).then_inc(fills(key[s_]), 1)
                if 1 <= n <= len(items):
                    m = n - 1
                    kind, t, b, q, keys, halves, _ = att_args(layer, m)
                    key = ("turn", layer, m)
                    open_bank(pe, key)
                    pe.wait_ge(S("prob_normed"), 2 * (g0 + m) + 2)
                    nh = len(halves)
                    for j in range(2 * nh):
                        mm = pe.transpose(bank(key)[:, j * P:(j + 1) * P],
                                          pr[:, (g0 + m) % 2, j // nh, (j % nh) * P:(j % nh + 1) * P], ident[:, :])
                    mm.then_inc(fills(key), 1)
                if n >= 2:
                    m = n - 2
                    kind, t, b, q, keys, halves, _ = att_args(layer, m)
                    key = ("value", layer, m // NC)
                    if b == 0:
                        open_bank(pe, key)
                    taken(pe, ("turn", layer, m))
                    nh = len(halves)
                    for s_ in range(2):
                        for j, vh in enumerate(halves):
                            mm = pe.matmul(bank(key)[64 * s_:64 * s_ + 64, b * P:(b + 1) * P],
                                           vh[:, 64 * s_:64 * s_ + 64],
                                           pt[:, (g0 + m) % 2, (s_ * nh + j) * P:(s_ * nh + j + 1) * P],
                                           start=(j == 0), stop=(j == nh - 1), skip_group_check=True)
                    if b == NC - 1:
                        mm.then_inc(fills(key), 1)
                if layer == 1:
                    pe_ada(pe, n)

        def pe_ada(pe, n):
            if 1 <= n <= 24:
                key = ("ada_turn", n - 1)
                open_bank(pe, key)
                taken(pe, ("unit", U["ada", n - 1], 0))
                for t in range(2):
                    mm = pe.matmul(bank(key)[:, t:t + 1], arow[:, (n - 1) % 2, t * P:(t + 1) * P], ones[0:2, 0:1],
                                   start=True, stop=True)
                mm.then_inc(fills(key), 1)
            if n < 24:
                u = U["ada", n]
                key = ("unit", u, 0)
                open_bank(pe, key)
                pe.wait_ge(S("w_lo"), u + 1)
                pe.wait_ge(S("c_split"), 2)
                hi, lo = W3(w_hi, u % 2), W3(w_lo, u % 2)
                for k in range(KT):
                    pe.matmul(bank(key)[0:2, 0:256], c_pair[:, k, :], hi[:, k, :], start=(k == 0), stop=False)
                    mm = pe.matmul(bank(key)[0:2, 0:256], c_pair[:, k, :], lo[:, k, :], start=False,
                                   stop=(k == KT - 1))
                mm.then_inc(fills(key), 1)

        def sink_col(kind, t):
            return t if kind == "swa" else 6 + t

        def dve_attention(v, layer):
            items = attention_items(layer)
            g0 = ATT0 * layer
            for n in range(len(items) + 2):
                if n < len(items):
                    kind, t, b, q, keys, halves, _ = att_args(layer, n)
                    g, w, c = g0 + n, P * len(halves), sink_col(kind, t)
                    key = ("score", layer, n, 0)
                    st = stat[:, g % 2]
                    full(v, key)
                    full(v, ("score", layer, n, 1))
                    b0 = BANK[key][0]
                    v.tensor_reduce(st[:, 0, :], banks[:, b0:b0 + 2, 0:w], AX,
                                    ALU.max).then_inc(S("row_max"), 1)
                    v.wait_ge(S("row_max"), g + 1)
                    v.scalar_tensor_tensor(out=st[:, 1, :], in0=st[:, 0, :], scalar=-0.125, in1=nsinks[:, c, :],
                                           op0=ALU.mult, op1=ALU.min).then_inc(S("neg_max"), 1)
                    v.wait_ge(S("neg_max"), g + 1)
                    v.tensor_tensor(st[:, 2, :], st[:, 1, :], sinks[:, c, :], ALU.add).then_inc(S("sink_arg"), 1)
                if 1 <= n <= len(items):
                    dve_prob_norm(v, layer, n - 1)
                if n >= 2 and (n - 2) % NC == NC - 1:
                    dve_value(v, layer, (n - 2) // NC)
                if layer == 1 and 1 <= n <= 24:
                    key = ("ada_turn", n - 1)
                    full(v, key)
                    v.tensor_tensor(mod[:, 2 * n - 2:2 * n], bank(key)[:, 0:2], mod[:, 2 * n - 2:2 * n], ALU.add)\
                        .then_inc(reads(key), 1)

        def dve_prob_norm(v, layer, m):
            kind, t, b, q, keys, halves, _ = att_args(layer, m)
            g, w = ATT0 * layer + m, P * len(halves)
            st = stat[:, g % 2]
            v.wait_ge(S("exps"), g + 1)
            for s_ in range(2):
                taken(v, ("score", layer, m, s_))
            v.tensor_tensor(st[:, 3, :], st[:, 3, :], st[:, 4, :], ALU.add).then_inc(S("denominator"), 1)
            v.wait_ge(S("denominator"), g + 1)
            v.reciprocal(st[:, 4, :], st[:, 3, :]).then_inc(S("inverse"), 1)
            v.wait_ge(S("inverse"), g + 1)
            for s_ in range(2):
                v.tensor_scalar(pr[:, g % 2, s_, 0:w], pr[:, g % 2, s_, 0:w], st[:, 4, s_:s_ + 1], None,
                                ALU.mult).then_inc(S("prob_normed"), 1)

        def dve_value(v, layer, j):
            key = ("value", layer, j)
            tile = att_args(layer, NC * j)[-1]
            v.wait_ge(S("value_hi"), V0 * layer + j + 1)
            v.tensor_tensor(hn_lo[:, tile, :], bank(key)[:, :], hn_hi[:, tile, :].bitcast(F32),
                            ALU.subtract).then_inc(reads(key), 1)

        def act_attention(a, layer):
            items = attention_items(layer)
            g0 = ATT0 * layer
            for n in range(len(items) + 2):
                if n < len(items):
                    kind, t, b, q, keys, halves, _ = att_args(layer, n)
                    g, w = g0 + n, P * len(halves)
                    st = stat[:, g % 2]
                    a.wait_ge(S("sink_arg"), g + 1)
                    a.activation(st[:, 4, :], st[:, 2, :], ACT.Exp).then_inc(S("exps"), 1)
                    if g >= 2:
                        m = n - 2 if n >= 2 else len(attention_items(layer - 1)) + n - 2
                        full(a, ("turn", layer if n >= 2 else layer - 1, m))
                    for s_ in range(2):
                        a.activation(pr[:, g % 2, s_, 0:w], bank(("score", layer, n, s_))[:, 0:w], ACT.Exp,
                                     bias=st[:, 1, s_:s_ + 1], scale=0.125, accum_out=st[:, 3, s_:s_ + 1])\
                            .then_inc(reads(("score", layer, n, s_)), 1)
                if 1 <= n <= len(items):
                    m = n - 1
                    w = P * len(att_args(layer, m)[5])
                    key = ("turn", layer, m)
                    full(a, key)
                    a.activation(pt[:, (g0 + m) % 2, 0:2 * w], bank(key)[:, 0:2 * w], ACT.Copy)\
                        .then_inc(reads(key), 1)
                if n >= 2 and (n - 2) % NC == NC - 1:
                    act_value(a, layer, (n - 2) // NC)
                if layer == 1 and n < 24:
                    key = ("unit", U["ada", n], 0)
                    full(a, key)
                    if n >= 2:
                        full(a, ("ada_turn", n - 2))
                    a.activation(arow[:, n % 2, :], bank(key)[0:2, 0:256], ACT.Copy).then_inc(reads(key), 1)
                    prep_hi(a, U["ada", n])

        def act_value(a, layer, j):
            key = ("value", layer, j)
            full(a, key)
            tile = att_args(layer, NC * j)[-1]
            a.activation(hn_hi[:, tile, :], bank(key)[:, :], ACT.Copy).then_inc(S("value_hi"), 1)

        QK = 2 * HG

        def row_of(j):
            return j if j < HG else 32 + j - HG

        def chunked(ap):
            return ap.rearrange("p (c t) -> p c t", c=NC)

        def dve_gates(v):
            key = ("unit", U["ba", 0], 0)
            lo, hi = slice(0, HG), slice(32, 32 + HG)
            v.wait_ge(S("bg_zero"), 1)
            v.wait_ge(S("neg_b_exp"), 1)
            v.tensor_scalar(bt[lo, 0, :], bt[lo, 0, :], 1.0, None, ALU.add).then_inc(S("gates"), 1)
            v.wait_ge(S("gates"), 1)
            v.reciprocal(bg[lo, :], bt[lo, 0, :]).then_inc(S("gates"), 1)
            full(v, key)
            v.tensor_scalar(bt[hi, 1, :], bank(key)[hi, :], gcst[hi, 0:1], None, ALU.add).then_inc(reads(key), 1)
            v.wait_ge(S("softplus_ln"), 4)
            taken(v, key)
            v.scalar_tensor_tensor(out=bt[hi, 1, :], in0=bt[hi, 1, :], scalar=0.0, in1=bt[hi, 2, :],
                                   op0=ALU.max, op1=ALU.add).then_inc(S("gates"), 1)
            v.wait_ge(S("gates"), 3)
            v.tensor_scalar(bt[hi, 1, :], bt[hi, 1, :], gcst[hi, 1:2], -1.0, ALU.mult, ALU.mult)\
                .then_inc(S("gates"), 1)
            v.wait_ge(S("gates"), 4)
            v.tensor_tensor_scan(bg[hi, :], reset[hi, :], bt[hi, 1, :], 0.0, ALU.mult, ALU.add)\
                .then_inc(S("gates"), 1)
            full(v, ("cols",))
            v.tensor_copy(cols[:, :, :], bank(("cols",))[:, 0:256].rearrange("p (c h) -> p c h", c=NC))\
                .then_inc(reads(("cols",)), 1)
            taken(v, ("cols",))
            v.wait_ge(S("exp_gc"), 1)
            v.scalar_tensor_tensor(out=nbe[:, :, :], in0=nbe[:, :, :], scalar=-1.0, in1=cols[:, :, 0:HG],
                                   op0=ALU.mult, op1=ALU.mult).then_inc(S("gates"), 1)

        def act_gates(a):
            key = ("unit", U["ba", 0], 0)
            lo, hi = slice(0, HG), slice(32, 32 + HG)
            full(a, key)
            a.activation(bt[lo, 0, :], bank(key)[lo, :], ACT.Exp, scale=-1.0).then_inc(S("neg_b_exp"), 1)
            prep_hi(a, U["ba", 0])
            a.activation(gcst[hi, 1:2], gcst[hi, 1:2], ACT.Exp).then_inc(S("softplus_ln"), 1)
            taken(a, key)
            a.activation(bt[hi, 2, :], bt[hi, 1, :], ACT.Abs).then_inc(S("softplus_ln"), 1)
            a.wait_ge(S("softplus_ln"), 2)
            a.activation(bt[hi, 2, :], bt[hi, 2, :], ACT.Exp, scale=-1.0).then_inc(S("softplus_ln"), 1)
            a.wait_ge(S("softplus_ln"), 3)
            a.activation(bt[hi, 2, :], bt[hi, 2, :], ACT.Ln, bias=1.0).then_inc(S("softplus_ln"), 1)
            taken(a, ("cols",))
            a.activation(nbe[:, :, :], cols[:, :, 32:32 + HG], ACT.Exp).then_inc(S("exp_gc"), 1)

        def pe_gate_cols(pe):
            pe.wait_ge(S("gates"), 5)
            open_bank(pe, ("cols",))
            for c in range(NC):
                mm = pe.transpose(bank(("cols",))[:, c * 64:(c + 1) * 64], bg[:, c * P:(c + 1) * P],
                                  ident[0:64, 0:64])
            mm.then_inc(fills(("cols",)), 1)

        def act_qkv(a):
            for i in range(9):
                u = U["qkv", i]
                for t in range(2):
                    j, key = 2 * i + t, ("unit", u, t)
                    full(a, key)
                    a.activation(qkv[:, j, :], bank(key)[:, :], ACT.Copy, scale=cw[:, j, 3:4])\
                        .then_inc(S("tap_last"), 1)
                prep_hi(a, u)
                for t in range(2):
                    j, key = 2 * i + t, ("unit", u, t)
                    taken(a, key)
                    a.activation(qkv[:, j, :], qkv[:, j, :], ACT.Silu).then_inc(S("conv_silu"), 1)
                for t in range(2):
                    j = 2 * i + t
                    if j < QK:
                        a.wait_ge(S("conv_silu"), j + 1)
                        if j >= 2:
                            a.wait_ge(S("l2_summed"), j - 1)
                        a.activation(sq[:, t, :], qkv[:, j, :], ACT.Square).then_inc(S("qk_squared"), 1)

        def dve_qkv(v):
            for i in range(9):
                for t in range(2):
                    j, key = 2 * i + t, ("unit", U["qkv", i], t)
                    v.wait_ge(S("tap_last"), j + 1)
                    for d in (1, 2, 3):
                        if d > 1:
                            v.wait_ge(S("taps"), 2 * j + d - 1)
                        ins = v.scalar_tensor_tensor(
                            out=qkv[:, j, d:T], in0=bank(key)[:, 0:T - d], scalar=cw[:, j, 3 - d:4 - d],
                            in1=qkv[:, j, d:T], op0=ALU.mult, op1=ALU.add)
                        ins.then_inc(S("taps") if d < 3 else reads(key), 1)

        def pe_l2(pe, j):
            if j == 0:
                open_bank(pe, ("l2",))
            pe.wait_ge(S("qk_squared"), j + 1)
            r = row_of(j)
            pe.matmul(bank(("l2",))[0:64, :], col1[:, 63 - r:127 - r], sq[:, j % 2, :], start=(j == 0),
                      stop=(j == QK - 1), skip_group_check=True)\
                .then_inc(S("l2_summed") if j < QK - 1 else fills(("l2",)), 1)

        def pe_gdn_in(pe):
            pe_linear(pe, "ba", ready=hn_ready(pe, 1))
            unit_jobs(pe, U["qkv", 0], 0, *hn_of, KT)
            pe_gate_cols(pe)
            for i in range(1, 9):
                unit_jobs(pe, U["qkv", i], 0, *hn_of, KT)
                for j in (2 * i - 2, 2 * i - 1):
                    if j < QK:
                        pe_l2(pe, j)
            over_units(pe, "z", lambda u, i: unit_jobs(pe, u, i, *hn_of, KT))
            over_units(pe, "memq", lambda u, i: unit_jobs(pe, u, i, *hn_of, KT))

        def act_z(a):
            def body(u, i):
                j = 2 * (u - U["z", 0])
                for t in range(2):
                    b, n = BANK["unit", u, t]
                    a.wait_ge(bank_full[b], i + (n + 1))
                    a.activation(zs[:, i * 4 + (j + t), :], psum[b][:, :], ACT.Silu).then_inc(bank_read[b], 1)
                prep_hi(a, u, i)
            over_units(a, "z", body)
            over_units(a, "memq", lambda u, i: prep_hi(a, u, i))
            full(a, ("l2",))
            a.activation(rows[:, :], bank(("l2",))[0:64, :], ACT.Sqrt, bias=eps[0:64, 0:1])\
                .then_inc(reads(("l2",)), 1)

        def dve_memq(v, src):
            for t in range(2):
                key = ("unit", src, t)
                full(v, key)
                v.tensor_copy(mem_q[:, t, :], bank(key)[:, :]).then_inc(reads(key), 1)

        def pe_heads(pe):
            pe.wait_ge(S("rows_inverse"), 1)
            for j in range(QK):
                key = ("l2b", j)
                open_bank(pe, key)
                pe.matmul(bank(key)[:, :], sel[:, j, :], rows[:, :], start=True, stop=True).then_inc(fills(key), 1)
            for h in range(HG):
                key = ("gm", h)
                open_bank(pe, key)
                pe.matmul(bank(key)[:, :], sel[:, HG + h, :], bg[:, :], start=True, stop=False)
                pe.matmul(bank(key)[:, :], identb[:, :], mask4[:, :], start=False, stop=True).then_inc(fills(key), 1)
                key = ("gp", h)
                open_bank(pe, key)
                pe.matmul(bank(key)[:, :], sel[:, HG + h, :], bg[:, :], start=True, stop=True)\
                    .then_inc(fills(key), 1)
                key = ("bb", h)
                open_bank(pe, key)
                pe.matmul(bank(key)[:, :], sel[:, h, :], bg[:, :], start=True, stop=True).then_inc(fills(key), 1)
                key = ("kk", h)
                open_bank(pe, key)
                taken(pe, ("bb", h))
                for c in range(NC):
                    cc = slice(c * P, (c + 1) * P)
                    mm = pe.matmul(bank(key)[:, cc], qkv[:, HG + h, cc], kb[:, h % 2, cc], start=True, stop=True)
                mm.then_inc(fills(key), 1)
                key = ("qk", h)
                open_bank(pe, key)
                taken(pe, ("l2b", h))
                for c in range(NC):
                    cc = slice(c * P, (c + 1) * P)
                    mm = pe.matmul(bank(key)[:, cc], qkv[:, HG + h, cc], qkv[:, h, cc], start=True, stop=True)
                mm.then_inc(fills(key), 1)

        def act_heads(a):
            for h in range(HG):
                taken(a, ("gm", h))
                a.activation(dec[:, h % 2, :], dec[:, h % 2, :], ACT.Exp).then_inc(S("decay"), 1)
                a.wait_ge(S("glast_diff"), h + 1)
                key = ("gp", h)
                full(a, key)
                a.activation(elast[:, h, :], elast[:, h, :], ACT.Exp).then_inc(S("elast"), 1)
                if h >= 2:
                    a.wait_ge(S("q_decayed"), h - 1)
                a.activation(eg[:, h % 2, :], bank(key)[:, :], ACT.Exp).then_inc(reads(key), 1)
                taken(a, key)
                a.activation(glast[:, h, :], chunked(eg[:, h % 2, :])[:, :, P - 1], ACT.Copy)\
                    .then_inc(S("glast"), 1)

        def dve_heads(v):
            taken(v, ("l2",))
            v.reciprocal(rows[:, :], rows[:, :]).then_inc(S("rows_inverse"), 1)
            for j in range(QK):
                key = ("l2b", j)
                full(v, key)
                v.scalar_tensor_tensor(out=qkv[:, j, :], in0=qkv[:, j, :], scalar=P ** -0.5 if j < HG else 1.0,
                                       in1=bank(key)[:, :], op0=ALU.mult, op1=ALU.mult).then_inc(reads(key), 1)
            for h in range(HG):
                key = ("gm", h)
                full(v, key)
                gcol = cols[:, :, 32 + h:33 + h]
                v.tensor_tensor(chunked(dec[:, h % 2, :]), chunked(bank(key)[:, :]), gcol.broadcast_to([P, NC, P]),
                                ALU.subtract).then_inc(reads(key), 1)
                key = ("gp", h)
                full(v, key)
                v.tensor_tensor(elast[:, h, :], chunked(bank(key)[:, :])[:, :, P - 1], cols[:, :, 32 + h],
                                ALU.subtract).then_inc(S("glast_diff"), 1)
                key = ("bb", h)
                full(v, key)
                taken(v, ("l2b", HG + h))
                v.tensor_tensor(kb[:, h % 2, :], qkv[:, HG + h, :], bank(key)[:, :], ALU.mult)\
                    .then_inc(reads(key), 1)
                key = ("kk", h)
                full(v, key)
                v.wait_ge(S("decay"), h + 1)
                v.tensor_tensor(lt[:, h, :], bank(key)[:, :], dec[:, h % 2, :], ALU.mult).then_inc(reads(key), 1)
                taken(v, key)
                v.tensor_tensor(chunked(lt[:, h, :]), chunked(lt[:, h, :]),
                                strict[:, None, :].broadcast_to([P, NC, P]), ALU.mult).then_inc(S("lt"), 1)
                key = ("qk", h)
                full(v, key)
                v.tensor_tensor(at[:, h, :], bank(key)[:, :], dec[:, h % 2, :], ALU.mult).then_inc(reads(key), 1)
                taken(v, ("gp", h))
                v.tensor_tensor(qkv[:, h, :], qkv[:, h, :], eg[:, h % 2, :], ALU.mult).then_inc(S("q_decayed"), 1)

        def pe_inverse(pe):
            for lv in range(7):
                for h in range(HG):
                    key = ("iz", lv, h)
                    open_bank(pe, key)
                    if lv:
                        taken(pe, ("iw", lv - 1, h))
                    else:
                        pe.wait_ge(S("lt"), h + 1)
                    for c in range(NC):
                        cc = slice(c * P, (c + 1) * P)
                        mm = pe.matmul(bank(key)[:, cc], lt[:, h, cc], xi[:, h, cc] if lv else ident[:, :],
                                       start=True, stop=True)
                    mm.then_inc(fills(key), 1)
                for h in range(HG):
                    taken(pe, ("iz", lv, h))
                    if lv:
                        taken(pe, ("iv", lv - 1, h))
                    for x_ in ("iw", "iv"):
                        key = (x_, lv, h)
                        if key not in BANK:
                            continue
                        open_bank(pe, key)
                        for c in range(NC):
                            cc = slice(c * P, (c + 1) * P)
                            xtc = xt[:, h, cc] if lv else ident[:, :]
                            z_ = zm[:, h, cc]
                            lhs, rhs = (xtc, z_) if x_ == "iw" else (z_, xtc)
                            mm = pe.matmul(bank(key)[:, cc], lhs, rhs, start=True, stop=True)
                        mm.then_inc(fills(key), 1)

        def dve_inverse(v):
            iall = ident[:, None, :].broadcast_to([P, NC, P])
            v.wait_ge(S("glast"), HG)
            v.wait_ge(S("q_decayed"), HG)
            taken(v, ("qk", HG - 1))
            for lv in range(7):
                for h in range(HG):
                    key = ("iz", lv, h)
                    full(v, key)
                    v.tensor_tensor(chunked(zm[:, h, :]), chunked(bank(key)[:, :]),
                                    levels[:, lv:lv + 1, :].broadcast_to([P, NC, P]), ALU.mult)\
                        .then_inc(reads(key), 1)
                for h in range(HG):
                    for x_, what in (("iw", xi), ("iv", xt)):
                        key = (x_, lv, h)
                        if key not in BANK:
                            continue
                        full(v, key)
                        old = chunked(what[:, h, :]) if lv else iall
                        v.tensor_tensor(chunked(what[:, h, :]), old, chunked(bank(key)[:, :]), ALU.subtract)\
                            .then_inc(reads(key), 1)

        def pe_turned(pe):
            for h in range(HG):
                for name, j in (("vt", 2 * HG + h), ("kt", HG + h)):
                    key = (name, h)
                    open_bank(pe, key)
                    for c in range(NC):
                        cc = slice(c * P, (c + 1) * P)
                        mm = pe.transpose(bank(key)[:, cc], qkv[:, j, cc], ident[:, :])
                    mm.then_inc(fills(key), 1)

        def dve_turned(v):
            for h in range(HG):
                key = ("vt", h)
                full(v, key)
                v.tensor_tensor(chunked(qkv[:, 2 * HG + h, :]), chunked(bank(key)[:, :]),
                                cols[:, :, h:h + 1].broadcast_to([P, NC, P]), ALU.mult).then_inc(reads(key), 1)
                key = ("kt", h)
                full(v, key)
                v.wait_ge(S("elast"), h + 1)
                v.tensor_tensor(chunked(lt[:, h, :]), chunked(bank(key)[:, :]),
                                elast[:, h, :, None].broadcast_to([P, NC, P]), ALU.mult).then_inc(reads(key), 1)

        def pe_recurrence(pe):
            for c in range(NC):
                cc = slice(c * P, (c + 1) * P)
                if c:
                    for h in range(HG):
                        key = ("ks", c, h)
                        open_bank(pe, key)
                        taken(pe, ("su", c - 1, h))
                        pe.matmul(bank(key)[:, 0:P], qkv[:, HG + h, cc], state[:, h, :], start=True, stop=True)\
                            .then_inc(fills(key), 1)
                for h in range(HG):
                    key = ("vn", c, h)
                    open_bank(pe, key)
                    if c:
                        taken(pe, ("ks", c, h))
                        right = rr[:, h, :]
                    else:
                        taken(pe, ("vt", h))
                        taken(pe, ("iv", 6, h))
                        right = qkv[:, 2 * HG + h, 0:P]
                    pe.matmul(bank(key)[:, 0:P], xt[:, h, cc], right, start=True, stop=True).then_inc(fills(key), 1)
                for h in range(HG):
                    key = ("oo", c, h)
                    open_bank(pe, key)
                    taken(pe, ("vn", c, h))
                    if c:
                        pe.matmul(bank(key)[:, 0:P], state[:, h, :], qkv[:, h, cc], start=True, stop=False)
                    else:
                        pe.wait_ge(S("q_decayed"), h + 1)
                    pe.matmul(bank(key)[:, 0:P], vn[:, h, :], at[:, h, cc], start=(c == 0), stop=True)\
                        .then_inc(fills(key), 1)
                    if c < NC - 1:
                        key = ("su", c, h)
                        open_bank(pe, key)
                        taken(pe, ("kt", h))
                        pe.matmul(bank(key)[:, 0:P], lt[:, h, cc], vn[:, h, :], start=True, stop=True)\
                            .then_inc(fills(key), 1)

        def dve_recurrence(v):
            for c in range(NC):
                cc = slice(c * P, (c + 1) * P)
                if c:
                    for h in range(HG):
                        key = ("ks", c, h)
                        full(v, key)
                        v.scalar_tensor_tensor(out=rr[:, h, :], in0=bank(key)[:, 0:P], scalar=nbe[:, c, h:h + 1],
                                               in1=qkv[:, 2 * HG + h, cc], op0=ALU.mult, op1=ALU.add)\
                            .then_inc(reads(key), 1)
                if c < NC - 1:
                    for h in range(HG):
                        key = ("su", c, h)
                        full(v, key)
                        if c:
                            v.wait_ge(S("glast"), h + 1)
                            v.scalar_tensor_tensor(out=state[:, h, :], in0=state[:, h, :],
                                                   scalar=glast[:, h, c:c + 1], in1=bank(key)[:, 0:P],
                                                   op0=ALU.mult, op1=ALU.add).then_inc(reads(key), 1)
                        else:
                            v.tensor_copy(state[:, h, :], bank(key)[:, 0:P]).then_inc(reads(key), 1)

        def act_recurrence(a):
            for c in range(NC):
                cc = slice(c * P, (c + 1) * P)
                for h in range(HG):
                    key = ("vn", c, h)
                    full(a, key)
                    a.activation(vn[:, h, :], bank(key)[:, 0:P], ACT.Copy).then_inc(reads(key), 1)
                for h in range(HG):
                    key = ("oo", c, h)
                    full(a, key)
                    a.activation(qkv[:, h, cc], bank(key)[:, 0:P], ACT.Copy).then_inc(reads(key), 1)
            for h in range(HG):
                taken(a, ("oo", NC - 1, h))
                if h:
                    a.wait_ge(S("o_summed"), h)
                a.activation(osq[:, :], qkv[:, h, :], ACT.Square).then_inc(S("o_squared"), 1)
            full(a, ("onorm",))
            a.activation(rows[:, :], bank(("onorm",))[0:64, :], ACT.Sqrt, bias=eps[0:64, 0:1], scale=1.0 / P)\
                .then_inc(reads(("onorm",)), 1)
            for h in range(HG):
                a.wait_ge(S("o_gated"), h + 1)
                a.activation(hn_hi[:, h, :], tmp[:, h, :], ACT.Copy).then_inc(S("mix_hi"), 1)

        def pe_onorm(pe):
            open_bank(pe, ("onorm",))
            for h in range(HG):
                pe.wait_ge(S("o_squared"), h + 1)
                pe.matmul(bank(("onorm",))[0:64, :], col1[:, 63 - h:127 - h], osq[:, :], start=(h == 0),
                          stop=(h == HG - 1), skip_group_check=True)\
                    .then_inc(S("o_summed") if h < HG - 1 else fills(("onorm",)), 1)
            pe.wait_ge(S("rows_inverse"), 2)
            for h in range(HG):
                key = ("ob", h)
                open_bank(pe, key)
                pe.matmul(bank(key)[:, :], sel[:, h, :], rows[:, :], start=True, stop=True).then_inc(fills(key), 1)

        def dve_onorm(v):
            taken(v, ("onorm",))
            v.reciprocal(rows[:, :], rows[:, :]).then_inc(S("rows_inverse"), 1)
            for h in range(HG + 1):
                if h < HG:
                    key = ("ob", h)
                    full(v, key)
                    v.scalar_tensor_tensor(out=tmp[:, h, :], in0=qkv[:, h, :], scalar=gng[:, 0:1],
                                           in1=bank(key)[:, :], op0=ALU.mult, op1=ALU.mult)\
                        .then_inc(reads(key), 1)
                    taken(v, key)
                    v.tensor_tensor(tmp[:, h, :], tmp[:, h, :], zs[:, h, :], ALU.mult).then_inc(S("o_gated"), 1)
                if h:
                    v.wait_ge(S("mix_hi"), h)
                    v.tensor_tensor(hn_lo[:, h - 1, :], tmp[:, h - 1, :], hn_hi[:, h - 1, :].bitcast(F32),
                                    ALU.subtract).then_inc(S("mix_lo"), 1)

        def rope_tables_dve(v):
            def step(ins):
                ins.then_inc(S("angle"), 1)
                count["angle"] += 1
                v.wait_ge(S("angle"), count["angle"])
            count = {"angle": 0}
            v.wait_ge(S("land_rope"), 16 * ROPE_LOADS)
            a0, kk_, r, _ = (ang[:, m, :] for m in range(4))
            step(v.tensor_copy(a0, posi[:, :]))
            step(v.tensor_scalar(a0, a0, rcol[:, 0:1], None, ALU.mult))
            for quarter, dst in ((0.0, sinv), (0.25, cosv)):
                step(v.tensor_scalar(kk_, a0, 1 / (2 * math.pi), quarter, ALU.mult, ALU.add))
                step(v.tensor_scalar(kk_, kk_, ROUND, ROUND, ALU.add, ALU.subtract))
                step(v.scalar_tensor_tensor(out=r, in0=kk_, scalar=-PI2[0], in1=a0, op0=ALU.mult, op1=ALU.add))
                step(v.scalar_tensor_tensor(out=r, in0=kk_, scalar=-PI2[1], in1=r, op0=ALU.mult, op1=ALU.add))
                step(v.scalar_tensor_tensor(out=r, in0=kk_, scalar=-PI2[2], in1=r, op0=ALU.mult, op1=ALU.add))
                step(v.tensor_scalar(r, r, quarter * 2 * math.pi, PI_IN, ALU.add, ALU.min))
                step(v.tensor_scalar(dst[:, :], r, -PI_IN, None, ALU.max))
            v.wait_ge(S("sines"), 2)
            step(v.tensor_scalar(sinv[:, :], sinv[:, :], rcol[:, 1:2], None, ALU.mult))

        def rope_tables_act(a):
            a.wait_ge(S("angle"), 16)
            a.activation(sinv[:, :], sinv[:, :], ACT.Sin).then_inc(S("sines"), 1)
            a.activation(cosv[:, :], cosv[:, :], ACT.Sin).then_inc(S("sines"), 1)

        def pe_kv(pe):
            u = U["kv", 0]
            pe.wait_ge(S("w_lo"), u + 1)
            hi, lo = W3(w_hi, u % 2), W3(w_lo, u % 2)
            key = ("unit", u, 0)
            open_bank(pe, key)
            for k in range(KT):
                hn_ready(pe, 3)(k)
                pe.matmul(bank(key)[:, :], hi[:, k, 0:P], hn_hi[:, k, :], start=(k == 0), stop=False)
                pe.matmul(bank(key)[:, :], hi[:, k, 0:P], hn_lo[:, k, :], start=False, stop=False)
                mm = pe.matmul(bank(key)[:, :], lo[:, k, 0:P], hn_hi[:, k, :], start=False, stop=(k == KT - 1))
            mm.then_inc(fills(key), 1)
            key = ("unit", u, 1)
            open_bank(pe, key)
            for b in range(NC):
                bb = slice(b * P, (b + 1) * P)
                for k in range(KT):
                    pe.matmul(bank(key)[:, bb], hn_hi[:, k, bb], hi[:, k, P:2 * P], start=(k == 0), stop=False)
                    pe.matmul(bank(key)[:, bb], hn_hi[:, k, bb], lo[:, k, P:2 * P], start=False, stop=False)
                    mm = pe.matmul(bank(key)[:, bb], hn_lo[:, k, bb], hi[:, k, P:2 * P], start=False,
                                   stop=(k == KT - 1))
            mm.then_inc(fills(key), 1)

        def dve_kv(v):
            u = U["kv", 0]
            full(v, ("unit", u, 0))
            v.tensor_copy(qraw[:, 6, :], bank(("unit", u, 0))[:, :]).then_inc(reads(("unit", u, 0)), 1)
            full(v, ("unit", u, 1))
            v.tensor_copy(vs[:, :, :], chunked(bank(("unit", u, 1))[:, :])).then_inc(reads(("unit", u, 1)), 1)

        def pe_rope(pe, j):
            key = ("rope", j)
            open_bank(pe, key)
            taken(pe, ("unit", U["kv", 0], 0) if j == 6 else ("unit", U["swaq", j // 2], j % 2))
            pe.matmul(bank(key)[:, :], perm[:, :], qraw[:, j, :], start=True, stop=True).then_inc(fills(key), 1)

        def dve_rope(v, j):
            key = ("rope", j)
            n = (j + 1) % 7
            dst = kr if j == 6 else qr[:, j, :]
            v.tensor_tensor(dst[:, :], qraw[:, j, :], cosv[:, :], ALU.mult).then_inc(S("rope_cos"), 1)
            full(v, key)
            v.wait_ge(S("rope_cos"), n + 1)
            v.tensor_tensor(qraw[:, j, :], bank(key)[:, :], sinv[:, :], ALU.mult).then_inc(reads(key), 1)
            taken(v, key)
            v.tensor_tensor(dst[:, :], dst[:, :], qraw[:, j, :], ALU.add).then_inc(S("roped"), 1)

        def act_round2(a, idx):
            for k in range(KT):
                a.wait_ge(S("shifted"), KT * idx + k + 1)
                a.activation(hn_hi[:, k, :], tmp[:, k, :], ACT.Copy).then_inc(S("ada_hi"), 1)

        def dve_ada_norm(v, i, idx):
            def low(k):
                v.wait_ge(S("ada_hi"), KT * idx + k + 1)
                v.tensor_tensor(hn_lo[:, k, :], tmp[:, k, :], hn_hi[:, k, :].bitcast(F32),
                                ALU.subtract).then_inc(S("ada_lo"), 1)
            for k in range(KT):
                v.scalar_tensor_tensor(out=tmp[:, k, :], in0=x[:, k, :], scalar=gain2[:, 2 * idx, k:k + 1],
                                       in1=rs[:, :], op0=ALU.mult, op1=ALU.mult).then_inc(S("scaled"), 1)
                v.wait_ge(S("scaled"), KT * idx + k + 1)
                c = 24 * idx + k
                v.tensor_scalar(tmp[:, k, :], tmp[:, k, :], mod[:, c:c + 1], None, ALU.add)\
                    .then_inc(S("shifted"), 1)
                if k:
                    low(k - 1)
            low(KT - 1)

        def ada_ready(pe, idx):
            return lambda k: pe.wait_ge(S("ada_lo"), KT * idx + k + 1)

        def dve_modulation(v):
            taken(v, ("ada_turn", 23))
            for m, c in ((0, 8), (2, 32)):
                v.scalar_tensor_tensor(out=gain2[:, m, :], in0=mod[:, c:c + 8], scalar=1.0, in1=gain2[:, m, :],
                                       op0=ALU.add, op1=ALU.mult).then_inc(S("modulated"), 1)
            for m, c in ((1, 16), (3, 40)):
                v.tensor_tensor(gain2[:, m, :], gain2[:, m, :], mod[:, c:c + 8], ALU.mult)\
                    .then_inc(S("modulated"), 1)
            v.wait_ge(S("modulated"), 4)

        def act_post(a, i, ring, ready):
            for k in range(KT):
                ready(a, k)
                if k >= 2:
                    a.wait_ge(S("post_summed"), (KT - 1) * i + k - 1)
                a.activation(ring[:, k % 2, :], tmp[:, k, :], ACT.Square).then_inc(S("post_squared"), 1)
            full(a, ("post", i))
            a.activation(rs[:, :], bank(("post", i))[:, :], ACT.Sqrt, bias=eps[:, 0:1], scale=1.0 / D)\
                .then_inc(reads(("post", i)), 1)

        def pe_post(pe, i, ring):
            key = ("post", i)
            open_bank(pe, key)
            for k in range(KT):
                pe.wait_ge(S("post_squared"), KT * i + k + 1)
                pe.matmul(bank(key)[:, :], ones[:, :], ring[:, k % 2, :], start=(k == 0), stop=(k == KT - 1))\
                    .then_inc(S("post_summed") if k < KT - 1 else fills(key), 1)

        def dve_post(v, i):
            taken(v, ("post", i))
            v.reciprocal(rs[:, :], rs[:, :]).then_inc(S("post_rstd"), 1)
            v.wait_ge(S("post_rstd"), i + 1)
            for k in range(KT):
                v.scalar_tensor_tensor(out=tmp[:, k, :], in0=tmp[:, k, :], scalar=gain2[:, 1 + 2 * i, k:k + 1],
                                       in1=rs[:, :], op0=ALU.mult, op1=ALU.mult).then_inc(S("post_scaled"), 1)
                v.wait_ge(S("post_scaled"), KT * i + k + 1)
                v.tensor_tensor(x[:, k, :], x[:, k, :], tmp[:, k, :], ALU.add).then_inc(S("post_added"), 1)

        HB = slice(96, 128)
        IK = slice(0, 64)

        def act_small(a):
            prep_hi(a, U["qlat", 0])
            for t in range(2):
                taken(a, ("unit", U["qlat", 0], t))
                a.activation(tmp[:, 2 + t, :], tmp[:, t, :], ACT.Square).then_inc(S("latent_sq"), 1)
            prep_hi(a, U["misc", 0])
            taken(a, ("unit", U["misc", 0], 0))
            a.activation(tmp[:, 4, :], kvf[:, :], ACT.Square).then_inc(S("latent_sq"), 1)
            taken(a, ("unit", U["misc", 0], 1))
            a.activation(tmp[IK, 5, :], r1[IK, :], ACT.Square).then_inc(S("latent_sq"), 1)

        def act_small_late(a):
            for name, dst, n in (("qn", rs[:, :], 256), ("kvn", tmp[:, 6, :], 128), ("kin", tmp[IK, 7, :], 64)):
                full(a, (name,))
                m = dst.shape[0]
                a.activation(dst, bank((name,))[0:m, :], ACT.Sqrt, bias=eps[0:m, 0:1], scale=1.0 / n)\
                    .then_inc(reads((name,)), 1)
            a.wait_ge(S("dt_arg"), 1)
            a.activation(small2[HB, 5:6], small2[HB, 5:6], ACT.Exp).then_inc(S("dt_exp"), 1)
            a.activation(tmp[HB, 2, :], r1[HB, :], ACT.Abs).then_inc(S("dt_exp"), 1)
            a.wait_ge(S("dt_exp"), 2)
            a.activation(tmp[HB, 2, :], tmp[HB, 2, :], ACT.Exp, scale=-1.0).then_inc(S("dt_exp"), 1)
            a.wait_ge(S("dt_exp"), 3)
            a.activation(tmp[HB, 2, :], tmp[HB, 2, :], ACT.Ln, bias=1.0).then_inc(S("dt_exp"), 1)
            for t in range(2):
                a.wait_ge(S("qn_scaled"), t + 1)
                a.activation(qn_hi[:, t, :], tmp[:, t, :], ACT.Copy).then_inc(S("qn_hi"), 1)
            a.dma_start(tmp[:, 4, :].bitcast(I32), I["posi2"]).then_inc(S("land_pos"), 16)

        def act_decays(a):
            a.wait_ge(S("last_diff"), 1)
            a.activation(tolast[:, :, :], tolast[:, :, :], ACT.Exp).then_inc(S("chunk_decays"), 1)
            a.activation(cdall[:, :, :], bank(("cl",))[:, 0:P].rearrange("p (h c) -> p h c", c=NC), ACT.Exp)\
                .then_inc(reads(("cl",)), 1)

        def dve_small(v):
            for t in range(2):
                key = ("unit", U["qlat", 0], t)
                full(v, key)
                v.tensor_copy(tmp[:, t, :], bank(key)[:, :]).then_inc(reads(key), 1)
            for t, dst in ((0, kvf), (1, r1)):
                key = ("unit", U["misc", 0], t)
                full(v, key)
                v.tensor_copy(dst[:, :], bank(key)[:, :]).then_inc(reads(key), 1)
            taken(v, key)
            v.wait_ge(S("land_second"), 16 * len(SECOND))
            v.wait_ge(S("latent_sq"), 4)
            v.tensor_scalar(r1[HB, :], r1[HB, :], small2[HB, 4:5], None, ALU.add).then_inc(S("dt_arg"), 1)
            for n, (name, dst) in enumerate((("qn", rs[:, :]), ("kvn", tmp[:, 6, :]), ("kin", tmp[IK, 7, :]))):
                taken(v, (name,))
                v.reciprocal(dst, dst).then_inc(S("latent_rstd"), 1)
            v.wait_ge(S("latent_rstd"), 3)
            for t in range(2):
                v.scalar_tensor_tensor(out=tmp[:, t, :], in0=tmp[:, t, :], scalar=small2[:, t:t + 1], in1=rs[:, :],
                                       op0=ALU.mult, op1=ALU.mult).then_inc(S("qn_scaled"), 1)
            v.scalar_tensor_tensor(out=kvf[:, :], in0=kvf[:, :], scalar=small2[:, 2:3], in1=tmp[:, 6, :],
                                   op0=ALU.mult, op1=ALU.mult).then_inc(S("keys_scaled"), 1)
            v.scalar_tensor_tensor(out=r1[IK, :], in0=r1[IK, :], scalar=small2[IK, 3:4], in1=tmp[IK, 7, :],
                                   op0=ALU.mult, op1=ALU.mult).then_inc(S("keys_scaled"), 1)
            for t in range(2):
                v.wait_ge(S("qn_hi"), t + 1)
                v.tensor_tensor(qn_lo[:, t, :], tmp[:, t, :], qn_hi[:, t, :].bitcast(F32), ALU.subtract)\
                    .then_inc(S("qn_lo"), 1)
            v.wait_ge(S("dt_exp"), 4)
            v.scalar_tensor_tensor(out=r1[HB, :], in0=r1[HB, :], scalar=0.0, in1=tmp[HB, 2, :],
                                   op0=ALU.max, op1=ALU.add).then_inc(S("dt"), 1)
            v.wait_ge(S("dt"), 1)
            v.tensor_scalar(tmp[HB, 3, :], r1[HB, :], small2[HB, 5:6], -1.0, ALU.mult, ALU.mult)\
                .then_inc(S("dt"), 1)
            v.memset(r2[:, :], 0.0).then_inc(S("dt"), 1)
            v.wait_ge(S("dt"), 3)
            v.tensor_tensor_scan(r2[HB, :], reset2[HB, :], tmp[HB, 3, :], 0.0, ALU.mult, ALU.add)\
                .then_inc(S("dt"), 1)
            v.wait_ge(S("dt"), 4)
            v.tensor_tensor(diag[HB, :, :], ident[HB, 96:128, None].broadcast_to([32, 32, NC]),
                            chunked(r2[HB, :])[:, None, :, P - 1].broadcast_to([32, 32, NC]), ALU.mult)\
                .then_inc(S("dt"), 1)
            full(v, ("kid",))
            v.tensor_copy(ki[:, :], bank(("kid",))[:, :]).then_inc(reads(("kid",)), 1)
            full(v, ("kvt",))
            v.tensor_copy(kvt[:, :, :], chunked(bank(("kvt",))[:, :])).then_inc(reads(("kvt",)), 1)
            full(v, ("c1",))
            v.tensor_copy(c1[:, :, :], chunked(bank(("c1",))[:, :])).then_inc(reads(("c1",)), 1)
            full(v, ("c2",))
            v.tensor_copy(c2[:, :, :], chunked(bank(("c2",))[:, :])[:, :, 96:128]).then_inc(reads(("c2",)), 1)
            taken(v, ("c2",))
            full(v, ("cl",))
            v.tensor_tensor(tolast[:, :, :], bank(("cl",))[:, 0:P].rearrange("p (h c) -> p c h", c=NC), c2[:, :, :],
                            ALU.subtract).then_inc(S("last_diff"), 1)
            taken(v, ("c1",))
            v.tensor_scalar(wcol[:, :, :], c1[:, :, 64:80], 1.0 / 32, None, ALU.mult).then_inc(S("wcol"), 1)
            ipos = tmp[:, 4, :].bitcast(I32)
            v.wait_ge(S("land_pos"), 16)
            v.wait_ge(S("keys_scaled"), 2)
            v.tensor_copy(tmp[:, 7, :], ipos).then_inc(S("positions"), 1)
            v.tensor_copy(qpc[:, 0, :], qpi[:, :]).then_inc(S("positions"), 1)
            v.wait_ge(S("positions"), 2)
            v.tensor_scalar(ipos, ipos, 6, None, ALU.arith_shift_right).then_inc(S("positions"), 1)
            v.tensor_scalar(qpi[:, :], qpi[:, :], 6, None, ALU.arith_shift_right).then_inc(S("positions"), 1)
            v.wait_ge(S("positions"), 4)
            v.tensor_copy(tmp[:, 6, :], ipos).then_inc(S("positions"), 1)
            v.tensor_copy(qpc[:, 1, :], qpi[:, :]).then_inc(S("positions"), 1)
            v.wait_ge(S("positions"), 6)

        def pe_small(pe):
            pe.wait_ge(S("latent_sq"), 2)
            open_bank(pe, ("qn",))
            pe.matmul(bank(("qn",))[:, :], ones[:, :], tmp[:, 2, :], start=True, stop=False)
            pe.matmul(bank(("qn",))[:, :], ones[:, :], tmp[:, 3, :], start=False, stop=True)\
                .then_inc(fills(("qn",)), 1)
            pe.wait_ge(S("latent_sq"), 4)
            open_bank(pe, ("kvn",))
            pe.matmul(bank(("kvn",))[:, :], ones[:, :], tmp[:, 4, :], start=True, stop=True)\
                .then_inc(fills(("kvn",)), 1)
            open_bank(pe, ("kin",))
            pe.matmul(bank(("kin",))[0:64, :], ones[IK, 0:64], tmp[IK, 5, :], start=True, stop=True)\
                .then_inc(fills(("kin",)), 1)

        def pe_small_late(pe):
            pe.wait_ge(S("keys_scaled"), 2)
            key = ("kid",)
            open_bank(pe, key)
            for s_ in range(2):
                mm = pe.matmul(bank(key)[64 * s_:64 * s_ + 64, :], ident[IK, 0:64], r1[IK, :], start=True, stop=True)
            mm.then_inc(fills(key), 1)
            pe.wait_ge(S("dt"), 4)
            for name, src in (("kvt", kvf), ("c1", r1), ("c2", r2)):
                open_bank(pe, (name,))
                for c in range(NC):
                    cc = slice(c * P, (c + 1) * P)
                    mm = pe.transpose(bank((name,))[:, cc], src[:, cc], ident[:, :])
                mm.then_inc(fills((name,)), 1)
            pe.wait_ge(S("dt"), 5)
            open_bank(pe, ("cl",))
            pe.matmul(bank(("cl",))[:, 0:P], ones[HB, :], diag[HB, :, :], start=True, stop=True)\
                .then_inc(fills(("cl",)), 1)

        def spill_out(a, j, src):
            a.dma_start(spill[j], src).then_inc(S(f"spilled{j % 2}"), 16)

        def slot_stored(eng, j):
            if j >= 2:
                eng.wait_ge(S(f"spilled{j % 2}"), 16 * (j // 2))

        def act_zed(a, lo, hi_):
            for u in range(U["zed", lo], U["zed", 0] + hi_):
                for t in range(2):
                    j = 2 * (u - U["zed", 0]) + t
                    full(a, ("unit", u, t))
                    slot_stored(a, j)
                    a.activation(cs[:, t, :], bank(("unit", u, t))[:, :], ACT.Silu)\
                        .then_inc(reads(("unit", u, t)), 1)
                prep_hi(a, u)
                for t in range(2):
                    taken(a, ("unit", u, t))
                    spill_out(a, 2 * (u - U["zed", 0]) + t, cs[:, t, :])

        def multi_unit(pe, u, jobs):
            pe.wait_ge(S("w_lo"), u + 1)
            hi = w_hi[:, u % 2, :].rearrange("p (k c) -> p k c", k=2)
            lo = w_lo[:, u % 2, :].rearrange("p (k c) -> p k c", k=2)
            for t in jobs:
                key = ("unit", u, t)
                open_bank(pe, key)
                for k in range(2):
                    cc = slice(t * P, (t + 1) * P)
                    pe.matmul(bank(key)[:, :], hi[:, k, cc], qn_hi[:, k, :], start=(k == 0), stop=False)
                    pe.matmul(bank(key)[:, :], hi[:, k, cc], qn_lo[:, k, :], start=False, stop=False)
                    mm = pe.matmul(bank(key)[:, :], lo[:, k, cc], qn_hi[:, k, :], start=False, stop=(k == 1))
                mm.then_inc(fills(key), 1)

        isc = lambda b: tmp[:, b, :]
        kc, kp = tmp[:, 6, :], tmp[:, 7, :]

        def pe_index(pe, n):
            b, t = n // 8, n % 8
            for s_ in range(2):
                key, h = ("index", n, s_), slice(64 * s_, 64 * s_ + 64)
                open_bank(pe, key)
                pe.matmul(bank(key)[:, :], qi[h, t, b * P:(b + 1) * P], ki[h, :], start=True, stop=True)\
                    .then_inc(fills(key), 1)

        def act_index(a, n):
            for s_ in range(2):
                key, m = ("index", n, s_), 2 * n + s_
                full(a, key)
                if m >= 2:
                    a.wait_ge(S("index_added"), m - 1)
                a.activation(relu[:, s_, :], bank(key)[:, :], ACT.Relu).then_inc(reads(key), 1)

        def dve_index(v, n):
            b, t = n // 8, n % 8
            for s_ in range(2):
                key, h, m = ("index", n, s_), 2 * t + s_, 2 * n + s_
                taken(v, key)
                w = wcol[:, b, h:h + 1]
                if h == 0:
                    v.tensor_scalar(isc(b), relu[:, s_, :], w, None, ALU.mult).then_inc(S("index_added"), 1)
                else:
                    v.wait_ge(S("index_added"), m)
                    v.scalar_tensor_tensor(out=isc(b), in0=relu[:, s_, :], scalar=w, in1=isc(b), op0=ALU.mult,
                                           op1=ALU.add).then_inc(S("index_added"), 1)

        def dve_topk(v, b, part):
            n0 = b * (2 * RD + 5)

            def step(ins, n):
                ins.then_inc(S("topk"), 1)
                v.wait_ge(S("topk"), n0 + n + 1)
            if part == 0:
                v.wait_ge(S("index_added"), 16 * (b + 1))
                step(v.tensor_scalar(oneh[:, :], kc, qpc[:, 1, b:b + 1], FILL, ALU.is_gt, ALU.mult), 0)
                step(v.tensor_tensor(isc(b), isc(b), oneh[:, :], ALU.add), 1)
            for r in range(4 * part, 4 * part + 4):
                step(v.max(m8[:, r % 2, :], isc(b)), 2 + 2 * r)
                step(v.match_replace(isc(b), m8[:, r % 2, :], isc(b), MARK), 3 + 2 * r)
            if part == 3:
                step(v.tensor_scalar(oneh[:, :], isc(b), -3.39e38, None, ALU.is_gt), 2 * RD + 2)
                step(v.scalar_tensor_tensor(out=isc(b), in0=kc, scalar=qpc[:, 1, b:b + 1], in1=oneh[:, :],
                                            op0=ALU.is_gt, op1=ALU.max), 2 * RD + 3)
                step(v.tensor_scalar(madd[:, b, :], isc(b), NEG, None, ALU.mult), 2 * RD + 4)

        def dve_buckets(v, b):
            NB_ = 5 + len(BUCKET_STEPS)

            def step(ins, n):
                ins.then_inc(S("bucket"), 1)
                v.wait_ge(S("bucket"), b * NB_ + n + 1)
            rel, dist, acc = isc(b), oneh[:, :], cs2[:, :]
            step(v.tensor_scalar(rel, kp, qpc[:, 0, b:b + 1], None, ALU.subtract), 0)
            step(v.tensor_scalar(acc, rel, 0.0, 16.0, ALU.is_gt, ALU.mult), 1)
            step(v.tensor_scalar(dist, rel, -1.0, None, ALU.mult), 2)
            step(v.tensor_tensor(dist, dist, rel, ALU.max), 3)
            step(v.scalar_tensor_tensor(out=acc, in0=dist, scalar=8.0, in1=acc, op0=ALU.min, op1=ALU.add), 4)
            for n, d in enumerate(BUCKET_STEPS):
                out = bkt[:, b, :] if n == len(BUCKET_STEPS) - 1 else acc
                step(v.scalar_tensor_tensor(out=out, in0=dist, scalar=float(d), in1=acc, op0=ALU.is_ge,
                                            op1=ALU.add), 5 + n)

        def pe_steps(pe):
            for i in range(24):
                u = U["xbc", i] if i < 16 else U["gab", i - 16]
                unit_jobs(pe, u, 0, *hn_of, KT)
                for n in (2 * i, 2 * i + 1):
                    if n < 32:
                        pe_index(pe, n)

        def act_steps(a):
            for i in range(24):
                u = U["xbc", i] if i < 16 else U["gab", i - 16]
                j0 = 16 + 2 * i
                for t in range(2):
                    key = ("unit", u, t)
                    full(a, key)
                    slot_stored(a, j0 + t)
                    if i < 16:
                        a.activation(cs[:, t, :], bank(key)[:, :], ACT.Identity, scale=cw2[:, 2 * i + t, 3:4],
                                     bias=cw2[:, 2 * i + t, 4:5]).then_inc(S("tap_last2"), 1)
                    else:
                        a.activation(cs[:, t, :], bank(key)[:, :], ACT.Sigmoid).then_inc(reads(key), 1)
                prep_hi(a, u)
                for t in range(2):
                    taken(a, ("unit", u, t))
                    if i < 16:
                        a.activation(cs[:, t, :], cs[:, t, :], ACT.Silu).then_inc(S("conv_silu2"), 1)
                for n in (2 * i, 2 * i + 1):
                    if n < 32:
                        act_index(a, n)
                for t in range(2):
                    if i < 16:
                        a.wait_ge(S("conv_silu2"), 2 * i + t + 1)
                    spill_out(a, j0 + t, cs[:, t, :])

        def dve_steps(v):
            for i in range(24):
                if i < 16:
                    for t in range(2):
                        j, key = 2 * i + t, ("unit", U["xbc", i], t)
                        v.wait_ge(S("tap_last2"), j + 1)
                        for d in (1, 2, 3):
                            if d > 1:
                                v.wait_ge(S("taps2"), 2 * j + d - 1)
                            v.scalar_tensor_tensor(
                                out=cs[:, t, d:T], in0=bank(key)[:, 0:T - d], scalar=cw2[:, j, 3 - d:4 - d],
                                in1=cs[:, t, d:T], op0=ALU.mult, op1=ALU.add)\
                                .then_inc(S("taps2") if d < 3 else reads(key), 1)
                    for n in (2 * i, 2 * i + 1):
                        dve_index(v, n)
                if 4 <= i < 20:
                    dve_topk(v, i // 4 - 1, i % 4)
                if i >= 20:
                    dve_buckets(v, i - 20)

        def queries(eng, which):
            by_head = qh[:, :].rearrange("p (q h) -> p q h", h=16)
            eng.wait_ge(S("bucket"), 4 * (5 + len(BUCKET_STEPS)))
            for i in range(2):
                for t in range(8):
                    key, h = ("unit", U["uq", i], t), 8 * i + t
                    if h % 2 != which:
                        continue
                    full(eng, key)
                    if which:
                        eng.tensor_scalar(by_head[:, :, h], bank(key)[:, :], P ** -0.5, None, ALU.mult)\
                            .then_inc(reads(key), 1)
                    else:
                        eng.activation(by_head[:, :, h], bank(key)[:, :], ACT.Copy, scale=P ** -0.5)\
                            .then_inc(reads(key), 1)
                if not which:
                    full(eng, ("unit", U["uq", i], 7))
                    prep_hi(eng, U["uq", i])

        def pe_latent(pe):
            pe.wait_ge(S("land_latent"), 16 * 3)
            pe.wait_ge(S("tbl_split"), 2)
            pe.wait_ge(S("bucket"), 4 * (5 + len(BUCKET_STEPS)))
            for n in range(NG + 5):
                if n < NG:
                    for e in range(2):
                        key = ("ohb", n, e)
                        open_bank(pe, key)
                        w = (2 * (n % 16) + e) * P
                        pe.matmul(bank(key)[:, :], qsel4[:, w:w + P], bkt[:, n // 16, :], start=True, stop=True)\
                            .then_inc(fills(key), 1)
                if 1 <= n <= NG:
                    m = n - 1
                    key = ("logit", m)
                    open_bank(pe, key)
                    out = bank(key)[:, :]
                    pe.matmul(out, qsel8[:, (m % 16) * P:(m % 16 + 1) * P], madd[:, m // 16, :], start=True, stop=False)
                    pe.matmul(out, qh[:, m * P:(m + 1) * P], kvf[:, :], start=False, stop=False)
                    for e in range(2):
                        taken(pe, ("ohb", m, e))
                        ee = slice(e * P, (e + 1) * P)
                        pe.matmul(out, tbl_hi[:, ee], oh[:, m % 2, e, :], start=False, stop=False)
                        mm = pe.matmul(out, tbl_lo[:, ee], oh[:, m % 2, e, :], start=False, stop=(e == 1))
                    mm.then_inc(fills(key), 1)
                if 3 <= n < NG + 3:
                    m = n - 3
                    key = ("ptp", m)
                    open_bank(pe, key)
                    pe.wait_ge(S("p_scaled"), m + 1)
                    for c in range(NC):
                        mm = pe.transpose(bank(key)[:, c * P:(c + 1) * P], pr2[:, m % 3, c * P:(c + 1) * P], ident[:, :])
                    mm.then_inc(fills(key), 1)
                if n >= 4 and (n - 4) % 4 == 3:
                    G = (n - 4) // 4
                    key = ("latent", G)
                    open_bank(pe, key)
                    taken(pe, ("ptp", 4 * G + 3))
                    for c in range(NC):
                        mm = pe.matmul(bank(key)[:, :], kvt[:, c, :], ptt[:, G % 2, c, :], start=(c == 0),
                                       stop=(c == NC - 1))
                    mm.then_inc(fills(key), 1)

        def dve_latent(v):
            v.wait_ge(S("tbl_split"), 1)
            v.wait_ge(S("land_latent"), 16 * 3)
            v.tensor_tensor(tbl_lo[:, :], tbl[:, :], tbl_hi[:, :].bitcast(F32), ALU.subtract)\
                .then_inc(S("tbl_split"), 1)
            for n in range(NG + 2):
                if n < NG:
                    for e in range(2):
                        key = ("ohb", n, e)
                        full(v, key)
                        if n >= 2:
                            full(v, ("logit", n - 2))
                        v.tensor_scalar(oh[:, n % 2, e, :], bank(key)[:, :], bcol[:, 0:1], None, ALU.is_equal)\
                            .then_inc(reads(key), 1)
                if 1 <= n <= NG:
                    m = n - 1
                    key = ("logit", m)
                    full(v, key)
                    v.tensor_reduce(st2[:, 0, m % 3:m % 3 + 1], bank(key)[:, :], AX, ALU.max)\
                        .then_inc(S("logit_max"), 1)
                    v.wait_ge(S("logit_max"), m + 1)
                    v.tensor_scalar(st2[:, 0, m % 3:m % 3 + 1], st2[:, 0, m % 3:m % 3 + 1], -1.0, None, ALU.mult)\
                        .then_inc(S("neg_logit_max"), 1)
                if n >= 2:
                    m = n - 2
                    taken(v, ("logit", m))
                    v.reciprocal(st2[:, 2, m % 3:m % 3 + 1], st2[:, 1, m % 3:m % 3 + 1]).then_inc(S("p_inverse"), 1)
                    v.wait_ge(S("p_inverse"), m + 1)
                    v.tensor_scalar(pr2[:, m % 3, :], pr2[:, m % 3, :], st2[:, 2, m % 3:m % 3 + 1], None,
                                    ALU.mult).then_inc(S("p_scaled"), 1)

        def act_latent(a):
            a.wait_ge(S("land_latent"), 16 * 3)
            a.activation(tbl_hi[:, :], tbl[:, :], ACT.Copy).then_inc(S("tbl_split"), 1)
            for n in range(1, NG + 6):
                if n <= NG:
                    m = n - 1
                    key = ("logit", m)
                    a.wait_ge(S("neg_logit_max"), m + 1)
                    if m >= 3:
                        full(a, ("ptp", m - 3))
                    a.activation(pr2[:, m % 3, :], bank(key)[:, :], ACT.Exp, bias=st2[:, 0, m % 3:m % 3 + 1],
                                 accum_out=st2[:, 1, m % 3:m % 3 + 1]).then_inc(reads(key), 1)
                if 3 <= n < NG + 3:
                    m = n - 3
                    key = ("ptp", m)
                    full(a, key)
                    g = m % 4
                    a.activation(ptt[:, m // 4 % 2, :, g * P:(g + 1) * P], chunked(bank(key)[:, :]), ACT.Copy)\
                        .then_inc(reads(key), 1)
                if n >= 5 and (n - 5) % 4 == 3:
                    G = (n - 5) // 4
                    key = ("latent", G)
                    full(a, key)
                    a.activation(qh[:, G * T:(G + 1) * T], bank(key)[:, :], ACT.Copy).then_inc(reads(key), 1)

        def pe_values(pe):
            by_head = qh[:, :].rearrange("p (q h) -> p q h", h=16)
            for t in range(8):
                key = ("uv", t)
                open_bank(pe, key)
                taken(pe, ("latent", NG // 4 - 1))
                for s_ in range(2):
                    h = 2 * t + s_
                    mm = pe.matmul(bank(key)[64 * s_:64 * s_ + 64, :], wuv[:, h * 64:(h + 1) * 64], by_head[:, :, h],
                                   start=True, stop=True)
                mm.then_inc(fills(key), 1)

        def act_values(a):
            for t in range(8):
                full(a, ("uv", t))
                a.activation(hn_hi[:, t, :], bank(("uv", t))[:, :], ACT.Copy).then_inc(S("attn_hi"), 1)

        def dve_values(v):
            for t in range(8):
                v.wait_ge(S("attn_hi"), t + 1)
                v.tensor_tensor(hn_lo[:, t, :], bank(("uv", t))[:, :], hn_hi[:, t, :].bitcast(F32), ALU.subtract)\
                    .then_inc(reads(("uv", t)), 1)

        def pe_ssd(pe, g):
            gr = grp[:, g % 2]
            pe.wait_ge(S(f"land_group{g % 2}"), 64 * (g // 2 + 1))
            key = ("bt", g)
            open_bank(pe, key)
            for c in range(NC):
                cc = slice(c * P, (c + 1) * P)
                mm = pe.transpose(bank(key)[:, cc], gr[:, 2, cc], ident[:, :])
            mm.then_inc(fills(key), 1)
            for t in range(2):
                key = ("xt", g, t)
                open_bank(pe, key)
                for c in range(NC):
                    cc = slice(c * P, (c + 1) * P)
                    mm = pe.transpose(bank(key)[:, cc], gr[:, t, cc], ident[:, :])
                mm.then_inc(fills(key), 1)
            key = ("cb", g)
            open_bank(pe, key)
            for c in range(NC):
                cc = slice(c * P, (c + 1) * P)
                mm = pe.matmul(bank(key)[:, cc], gr[:, 2, cc], gr[:, 3, cc], start=True, stop=True)
            mm.then_inc(fills(key), 1)
            for c in range(NC - 1):
                key = ("st", g, c)
                open_bank(pe, key)
                taken(pe, ("bt", g))
                pe.wait_ge(S("xdk"), 2 * g + 2)
                pe.matmul(bank(key)[:, 0:256], btok[:, c, :], xdk[:, c, :, :], start=True, stop=True)\
                    .then_inc(fills(key), 1)
            for t in range(2):
                for s_ in range(2):
                    h = 4 * g + 2 * t + s_
                    key = ("lm", g, t, s_)
                    open_bank(pe, key)
                    pe.matmul(bank(key)[:, :], ident[HB, 96 + h:97 + h].broadcast_to([32, P]), r2[HB, :],
                              start=True, stop=False)
                    pe.matmul(bank(key)[:, :], identb[:, :], mask2[:, :], start=False, stop=True)\
                        .then_inc(fills(key), 1)
                key = ("ea", g, t)
                h = 4 * g + 2 * t
                open_bank(pe, key)
                for s_ in range(2):
                    mm = pe.matmul(bank(key)[64 * s_:64 * s_ + 64, :],
                                   ident[HB, 96 + h + s_:97 + h + s_].broadcast_to([32, 64]), r2[HB, :],
                                   start=True, stop=True, skip_group_check=True)
                mm.then_inc(fills(key), 1)
                key = ("yd", g, t)
                open_bank(pe, key)
                if t:
                    taken(pe, ("cb", g))
                else:
                    pe.wait_ge(S("m_made"), 3 * g + 2)
                taken(pe, ("xt", g, t))
                for c in range(NC):
                    for s_ in range(2):
                        mm = pe.matmul(bank(key)[64 * s_:64 * s_ + 64, c * P:(c + 1) * P],
                                       xd[:, c, t, 64 * s_:64 * s_ + 64], mt[:, s_, c * P:(c + 1) * P],
                                       start=True, stop=True, skip_group_check=True)
                mm.then_inc(fills(key), 1)
                key = ("yo", g, t)
                open_bank(pe, key)
                taken(pe, ("st", g, NC - 2))
                for c in range(1, NC):
                    cc = slice(c * P, (c + 1) * P)
                    mm = pe.matmul(bank(key)[:, cc], sst[:, c - 1, t, :], gr[:, 3, cc], start=True, stop=True)
                mm.then_inc(fills(key), 1)
                if 2 * g + t:
                    pe_ssd_sum(pe, 2 * g + t - 1)
            if g == 7:
                pe_ssd_sum(pe, 15)

        def pe_ssd_sum(pe, i):
            key = ("ssn",)
            if i == 0:
                open_bank(pe, key)
            pe.wait_ge(S("y_squared"), i + 1)
            pe.matmul(bank(key)[:, :], ones[:, :], ysq[:, i % 2, :], start=(i == 0), stop=(i == 15),
                      skip_group_check=True).then_inc(S("y_summed") if i < 15 else fills(key), 1)

        def act_ssd(a, g):
            key = ("bt", g)
            full(a, key)
            if g:
                full(a, ("st", g - 1, NC - 2))
            a.activation(btok[:, :, :], chunked(bank(key)[:, :]), ACT.Copy).then_inc(reads(key), 1)
            for t in range(2):
                for s_ in range(2):
                    taken(a, ("lm", g, t, s_))
                    a.activation(lb[:, s_, :], lb[:, s_, :], ACT.Exp).then_inc(S("l_exp"), 1)
                key = ("ea", g, t)
                full(a, key)
                if 2 * g + t:
                    a.wait_ge(S("y_off"), 2 * g + t)
                a.activation(ea[:, :], bank(key)[:, :], ACT.Exp).then_inc(reads(key), 1)
                i = 2 * g + t
                a.wait_ge(S("y_gated"), i + 1)
                if i >= 2:
                    a.wait_ge(S("y_summed"), i - 1)
                a.activation(ysq[:, t, :], ysd[:, t, :], ACT.Square).then_inc(S("y_squared"), 1)
                full(a, ("unit", U["ossd0" if i >= 8 else "oattn", 3], 1))
                a.activation(hn_hi[:, i % 8, :], ysd[:, t, :], ACT.Copy, scale=ssdg[:, i:i + 1])\
                    .then_inc(S("y_hi"), 1)

        def dve_ssd(v, g):
            gr = grp[:, g % 2]
            v.wait_ge(S("chunk_decays"), 1)
            taken(v, ("cl",))
            v.wait_ge(S(f"land_group{g % 2}"), 64 * (g // 2 + 1))
            for t in range(2):
                key = ("xt", g, t)
                full(v, key)
                if g:
                    full(v, ("yd", g - 1, t))
                h = 96 + 4 * g + 2 * t
                dtc = c1[:, :, h:h + 2, None].broadcast_to([P, NC, 2, 64])
                v.tensor_tensor(xd[:, :, t, :].rearrange("p c (s d) -> p c s d", s=2),
                                chunked(bank(key)[:, :]).rearrange("p c (s d) -> p c s d", s=2), dtc, ALU.mult)\
                    .then_inc(reads(key), 1)
            for t in range(2):
                taken(v, ("xt", g, t))
                if g:
                    full(v, ("st", g - 1, NC - 2))
                h = 4 * g + 2 * t
                last = slice(0, NC - 1)
                v.tensor_tensor(xdk[:, :, t, :].rearrange("p c (s d) -> p c s d", s=2),
                                xd[:, last, t, :].rearrange("p c (s d) -> p c s d", s=2),
                                tolast[:, last, h:h + 2, None].broadcast_to([P, NC - 1, 2, 64]), ALU.mult)\
                    .then_inc(S("xdk"), 1)

            def decayed(t):
                for s_ in range(2):
                    n = 4 * g + 2 * t + s_
                    key = ("lm", g, t, s_)
                    full(v, key)
                    v.tensor_tensor(chunked(lb[:, s_, :]), chunked(bank(key)[:, :]),
                                    c2[:, :, 4 * g + 2 * t + s_, None].broadcast_to([P, NC, P]), ALU.subtract)\
                        .then_inc(reads(key), 1)
                for s_ in range(2):
                    n = 4 * g + 2 * t + s_
                    v.wait_ge(S("l_exp"), n + 1)
                    if n >= 2:
                        full(v, ("yd", (n - 2) // 4, (n - 2) // 2 % 2))
                    ins = v.tensor_tensor(mt[:, s_, :], lb[:, s_, :], bank(("cb", g))[:, :], ALU.mult)
                    ins.then_inc(reads(("cb", g)) if t and s_ else S("m_made"), 1)

            def output(t):
                i = 2 * g + t
                taken(v, ("ea", g, t))
                full(v, ("yd", g, t))
                if i >= 2:
                    v.wait_ge(S("y_lo"), i - 1)
                v.scalar_tensor_tensor(out=ysd[:, t, :], in0=gr[:, t, :], scalar=dskip[:, i:i + 1],
                                       in1=bank(("yd", g, t))[:, :], op0=ALU.mult, op1=ALU.add)\
                    .then_inc(reads(("yd", g, t)), 1)
                full(v, ("yo", g, t))
                v.tensor_tensor(ea[:, P:T], ea[:, P:T], bank(("yo", g, t))[:, P:T], ALU.mult)\
                    .then_inc(reads(("yo", g, t)), 1)
                taken(v, ("yo", g, t))
                taken(v, ("yd", g, t))
                v.tensor_tensor(ysd[:, t, P:T], ysd[:, t, P:T], ea[:, P:T], ALU.add).then_inc(S("y_off"), 1)
                v.wait_ge(S("y_off"), i + 1)
                v.tensor_tensor(ysd[:, t, :], ysd[:, t, :], zt[:, g % 2, t, :], ALU.mult).then_inc(S("y_gated"), 1)
                v.wait_ge(S("y_hi"), i + 1)
                v.scalar_tensor_tensor(out=hn_lo[:, i % 8, :], in0=ysd[:, t, :], scalar=ssdg[:, i:i + 1],
                                       in1=hn_hi[:, i % 8, :].bitcast(F32), op0=ALU.mult, op1=ALU.subtract)\
                    .then_inc(S("y_lo"), 1)

            for c in range(NC - 1):
                key = ("st", g, c)
                full(v, key)
                if c == 0:
                    if g:
                        full(v, ("yo", g - 1, 1))
                    v.tensor_copy(sst[:, 0, :, :], bank(key)[:, 0:256].rearrange("p (t d) -> p t d", t=2))\
                        .then_inc(reads(key), 1)
                    taken(v, key)
                else:
                    v.tensor_tensor(
                        sst[:, c, :, :].rearrange("p t (s d) -> p (t s) d", s=2),
                        sst[:, c - 1, :, :].rearrange("p t (s d) -> p (t s) d", s=2),
                        cdall[:, 4 * g:4 * g + 4, c:c + 1].broadcast_to([P, 4, 64]), ALU.mult)\
                        .then_inc(S("state_decayed"), 1)
                    v.wait_ge(S("state_decayed"), 2 * g + c)
                    v.tensor_tensor(sst[:, c, :, :], sst[:, c, :, :],
                                    bank(key)[:, 0:256].rearrange("p (t d) -> p t d", t=2), ALU.add)\
                        .then_inc(reads(key), 1)
                    taken(v, key)
            full(v, ("cb", g))
            decayed(0)
            output(0)
            decayed(1)
            output(1)
        def dve_attn_gate(v):
            v.wait_ge(S("land_gate"), 16)
            for i in range(4):
                for t in range(2):
                    key, j = ("unit", U["oattn", i], t), 2 * i + t
                    full(v, key)
                    v.tensor_tensor(ma[:, j, :], ma[:, j, :], bank(key)[:, :], ALU.mult).then_inc(reads(key), 1)

        def dve_mix(v):
            taken(v, ("ssn",))
            v.reciprocal(rs[:, :], rs[:, :]).then_inc(S("ssd_rstd"), 1)
            v.wait_ge(S("ssd_rstd"), 1)
            v.wait_ge(S("land_gate"), 32)
            gate = grp[:, :, :, :].rearrange("p a b t -> p (a b) t")

            def step(ins):
                ins.then_inc(S("mixed"), 1)
                count[0] += 1
                v.wait_ge(S("mixed"), count[0])
            count = [0]
            for i in range(4):
                for t in range(2):
                    key, j = ("unit", U["ossd1", i], t), 2 * i + t
                    step(v.tensor_tensor(gate[:, j, :], gate[:, j, :], rs[:, :], ALU.mult))
                    full(v, key)
                    v.tensor_tensor(tmp[:, j, :], tmp[:, j, :], bank(key)[:, :], ALU.add).then_inc(reads(key), 1)
                    taken(v, key)
                    step(v.tensor_tensor(tmp[:, j, :], tmp[:, j, :], gate[:, j, :], ALU.mult))
                    step(v.tensor_tensor(tmp[:, j, :], tmp[:, j, :], ma[:, j, :], ALU.add))
            for k in range(KT):
                v.wait_ge(S("blend_hi"), k + 1)
                v.tensor_tensor(hn_lo[:, k, :], tmp[:, k, :], hn_hi[:, k, :].bitcast(F32), ALU.subtract)\
                    .then_inc(S("blend_lo"), 1)

        def act_mix(a):
            full(a, ("ssn",))
            a.activation(rs[:, :], bank(("ssn",))[:, :], ACT.Sqrt, bias=eps[:, 0:1], scale=1.0 / 2048)\
                .then_inc(reads(("ssn",)), 1)
            over_units(a, "ossd1", lambda u, i: prep_hi(a, u, i))
            full(a, ("unit", U["ossd1", 3], 1))
            for k in range(KT):
                a.wait_ge(S("mixed"), 3 * k + 3)
                a.activation(hn_hi[:, k, :], tmp[:, k, :], ACT.Copy).then_inc(S("blend_hi"), 1)

        def sp_group(sp, g):
            land = S(f"land_group{g % 2}")
            if g >= 2:
                full(sp, ("yo", g - 2, 1))
                sp.wait_ge(S("y_gated"), 2 * g - 2)
            sp.dma_start(grp[:, g % 2, 0:2, :], spill[16 + 2 * g:18 + 2 * g].rearrange("n p t -> p n t"))\
                .then_inc(land, 16)
            sp.dma_start(grp[:, g % 2, 2, :], spill[32 + g]).then_inc(land, 16)
            sp.dma_start(grp[:, g % 2, 3, :], spill[40 + g]).then_inc(land, 16)
            sp.dma_start(zt[:, g % 2, :, :], spill[2 * g:2 * g + 2].rearrange("n p t -> p n t"))\
                .then_inc(land, 16)

        LOADS = [(ident, "ident"), (identb, "identb"), (ones, "ones"), (gains, "gains"), (sinks, "sinks"),
                 (cw, "cw"), (gng, "gng"), (col1, "col1"), (sel, "sel"), (mask4, "mask4"), (strict, "strict"),
                 (levels, "levels"), (mod, "mod"), (gain2, "gain2"), (c_col, "c_col")]
        SECOND = [(small2, "small2"), (cw2, "cw2"), (dskip, "dskip"), (ssdg, "ssdg"), (mask2, "mask2"),
                  (wuv, "wuv"), (bcol, "bcol"), (reset2, "reset2"), (qpi, "qpi")]
        block = ctx.enter_context(nc.Block())

        @block.sync
        def _(sp):
            sp.dma_start(memx, I["memT"]).then_inc(S("land_mem"), 16)
            for q in range(2):
                sp.dma_start(raw[:, q, :], I["W"][q]).then_inc(w_land[q], 16)
            sp.dma_start(x[:, :, :], I["xT"]).then_inc(S("land_x"), 16)

            def load_units(first, last):
                pairs = (last - first) // 2
                with sp.Fori(0, pairs) as i:
                    for q in range(2):
                        u = first + q
                        sp.wait_ge(S("w_lo"), i * 2 + (u - 1))
                        sp.dma_start(raw[:, u % 2, :], I["W"][i * 2 + u]).then_inc(w_land[u % 2], 16)
                for u in range(first + 2 * pairs, last):
                    sp.wait_ge(S("w_lo"), u - 1)
                    sp.dma_start(raw[:, u % 2, :], I["W"][u]).then_inc(w_land[u % 2], 16)

            u = U["oattn", 0]
            load_units(2, u + 2)
            full(sp, ("uv", 7))
            for q in range(2):
                sp.wait_ge(S(f"spilled{q}"), 16 * 32)
            sp.dma_start(ma[:, :, :], spill[48:56].rearrange("n p t -> p n t")).then_inc(S("land_gate"), 16)
            sp_group(sp, 0)
            sp_group(sp, 1)
            load_units(u + 2, u + 6)
            sp_group(sp, 2)
            sp_group(sp, 3)
            load_units(u + 6, u + 8)
            sp_group(sp, 4)
            sp_group(sp, 5)
            load_units(u + 8, u + 10)
            sp_group(sp, 6)
            sp_group(sp, 7)
            full(sp, ("yo", 7, 1))
            sp.wait_ge(S("y_gated"), 16)
            sp.dma_start(grp[:, :, :, :], spill[56:64].rearrange("(a b) p t -> p a b t", a=2))\
                .then_inc(S("land_gate"), 16)
            load_units(u + 10, NU)
            sp.wait_ge(S("post_added"), 2 * KT)
            sp.dma_start(O["out"], x[:, :, :]).then_inc(S("stored"), 16)
            sp.wait_ge(S("stored"), 16)

        @block.gpsimd
        def _(pool):
            pool.memset(eps[:, :], EPS).then_inc(S("eps_set"), 1)
            pool.memset(bg[:, :], 0.0).then_inc(S("bg_zero"), 1)
            with pool.Fori(0, NU // 2) as i:
                for q in range(2):
                    pool.wait_ge(S("w_hi"), i * 2 + (q + 1))
                    pool.tensor_tensor(w_lo[:, q, :], raw[:, q, :], w_hi[:, q, :].bitcast(F32), ALU.subtract)\
                        .then_inc(S("w_lo"), 1)
            for u in range(NU // 2 * 2, NU):
                pool.wait_ge(S("w_hi"), u + 1)
                pool.tensor_tensor(w_lo[:, u % 2, :], raw[:, u % 2, :], w_hi[:, u % 2, :].bitcast(F32),
                                   ALU.subtract).then_inc(S("w_lo"), 1)

        @block.scalar
        def _(a):
            for ap, name in LOADS:
                a.dma_start(ap[tuple(slice(None) for _ in ap.shape)], I[name]).then_inc(S("land_const"), 16)
            a.dma_start(gcst[32:32 + HG, :], I["gcst"]).then_inc(S("land_const"), 16)
            a.dma_start(reset[32:32 + HG, :], I["reset"]).then_inc(S("land_const"), 16)
            for q in range(2):
                a.wait_ge(w_land[q], 16)
                a.activation(w_hi[:, q, :], raw[:, q, :], ACT.Copy).then_inc(S("w_hi"), 1)
            a.wait_ge(S("land_const"), 16 * (len(LOADS) + 2))
            a.wait_ge(S("eps_set"), 1)
            a.activation(c_col[:, :], c_col[:, :], ACT.Silu).then_inc(S("c_silu"), 1)
            a.wait_ge(S("c_silu"), 1)
            a.activation(c_pair[:, :, 0], c_col[:, :], ACT.Copy).then_inc(S("c_split"), 1)
            act_norm(a, 0, lambda k: mem_of(k), MEM, lambda e, k: e.wait_ge(S("land_mem"), 16))
            act_norm_round(a, 0, MEM)
            for i in range(4):
                prep_hi(a, U["mem", i])
            act_norm(a, 1, x_of, T, lambda e, k: e.wait_ge(S("land_x"), 16))
            act_norm_round(a, 1)
            act_gates(a)
            act_qkv(a)
            act_z(a)
            act_heads(a)
            act_recurrence(a)
            act_attention(a, 0)
            over_units(a, "wout0", lambda u, i: prep_hi(a, u, i))
            act_norm(a, 2, x_of, T, after_units("wout0"))
            act_norm_round(a, 2)
            act_ffn(a, 0)
            taken(a, ("unit", U["dn02", 3], 1))
            for ap, name in ((rcol, "rcol"), (perm, "perm"), (band, "band"), (posi, "posi")):
                a.dma_start(ap[:, :], I[name]).then_inc(S("land_rope"), 16)
            act_norm(a, 3, x_of, T, after_units("dn02"))
            act_norm_round(a, 3)
            rope_tables_act(a)
            prep_hi(a, U["kv", 0])
            act_norm_round(a, 4)
            over_units(a, "swaq", lambda u, i: prep_hi(a, u, i))
            act_attention(a, 1)
            over_units(a, "wout1", lambda u, i: prep_hi(a, u, i))
            act_norm(a, 5, x_of, T, after_units("wout1"))
            act_norm_round(a, 5)
            act_ffn(a, 1)
            act_norm(a, 6, x_of, T, after_units("dn12"))
            full(a, ("unit", U["dn12", 3], 1))
            for ap, name in SECOND:
                a.dma_start(ap[tuple(slice(None) for _ in ap.shape)], I[name]).then_inc(S("land_second"), 16)
            act_norm(a, 7, x_of, T, lambda e, k: e.wait_ge(S("final"), k + 1))
            act_round2(a, 0)
            act_small(a)
            a.wait_ge(S("land_second"), 16 * len(SECOND))
            act_zed(a, 0, 1)
            act_small_late(a)
            act_zed(a, 1, 8)
            act_decays(a)
            full(a, ("unit", U["qidx", 0], 7))
            prep_hi(a, U["qidx", 0])
            act_steps(a)
            full(a, ("unit", U["gab", 7], 1))
            a.wait_ge(S("bucket"), 4 * (5 + len(BUCKET_STEPS)))
            for ap, name in ((qsel4, "qsel4"), (qsel8, "qsel8"), (tbl, "tbl")):
                a.dma_start(ap[:, :], I[name]).then_inc(S("land_latent"), 16)
            queries(a, 0)
            act_latent(a)
            act_values(a)
            over_units(a, "oattn", lambda u, i: prep_hi(a, u, i))
            for g in range(4):
                act_ssd(a, g)
            over_units(a, "ossd0", lambda u, i: prep_hi(a, u, i))
            for g in range(4, 8):
                act_ssd(a, g)
            act_mix(a)
            over_units(a, "wout2", lambda u, i: prep_hi(a, u, i))
            act_post(a, 0, ysq, after_units("wout2"))
            act_norm(a, 8, x_of, T, lambda e, k: e.wait_ge(S("post_added"), k + 1))
            act_round2(a, 1)
            act_ffn(a, 2)
            act_post(a, 1, sg, after_units("dn22"))

        @block.vector
        def _(v):
            v.wait_ge(S("land_const"), 16 * (len(LOADS) + 2))
            v.tensor_scalar(nsinks[:, :, :], sinks[:, :, :], -1.0, None, ALU.mult).then_inc(S("nsinks"), 1)
            v.wait_ge(S("nsinks"), 1)
            v.wait_ge(S("c_split"), 1)
            v.tensor_tensor(c_pair[:, :, 1], c_col[:, :], c_pair[:, :, 0].bitcast(F32), ALU.subtract)\
                .then_inc(S("c_split"), 1)
            dve_rstd(v, 0, MEM, 0)
            dve_norm(v, 0, 0, mem_of, MEM)
            dve_mem(v)
            dve_rstd(v, 1, T, 1)
            dve_norm(v, 1, 1, x_of)
            dve_gates(v)
            dve_qkv(v)
            dve_memq(v, U["memq", 0])
            dve_heads(v)
            dve_inverse(v)
            dve_turned(v)
            dve_recurrence(v)
            dve_onorm(v)
            dve_attention(v, 0)
            dve_residual(v, "wout0")
            dve_rstd(v, 2, T, 2)
            dve_norm(v, 2, 2, x_of)
            dve_ffn(v, 0)
            dve_rstd(v, 3, T, 3)
            dve_norm(v, 3, 3, x_of)
            rope_tables_dve(v)
            dve_kv(v)
            dve_norm(v, 4, 4, x_of)
            for i in range(4):
                for j in (2 * i, 2 * i + 1):
                    key = ("unit", U["swaq", i], j % 2)
                    full(v, key)
                    dst = qraw[:, j, :] if j < 6 else mem_q[:, j - 6, :]
                    v.tensor_copy(dst, bank(key)[:, :]).then_inc(reads(key), 1)
                for j in ROPE_AFTER[i]:
                    taken(v, ("unit", U["swaq", j // 2], j % 2) if j < 6 else ("unit", U["kv", 0], 0))
                    dve_rope(v, j)
            dve_attention(v, 1)
            dve_residual(v, "wout1")
            dve_rstd(v, 5, T, 4)
            dve_norm(v, 5, 5, x_of)
            dve_ffn(v, 1)
            dve_rstd(v, 6, T, 5)
            for k in range(KT):
                v.scalar_tensor_tensor(out=x[:, k, :], in0=x[:, k, :], scalar=gains[:, 6, k:k + 1],
                                       in1=rs[:, :], op0=ALU.mult, op1=ALU.mult).then_inc(S("final"), 1)
            dve_modulation(v)
            dve_rstd(v, 7, T, 6)
            dve_ada_norm(v, 7, 0)
            dve_small(v)
            for t in range(8):
                key = ("unit", U["qidx", 0], t)
                full(v, key)
                v.tensor_copy(qi[:, t, :], bank(key)[:, :]).then_inc(reads(key), 1)
            v.wait_ge(S("wcol"), 1)
            dve_steps(v)
            queries(v, 1)
            dve_latent(v)
            dve_values(v)
            dve_attn_gate(v)
            for g in range(4):
                dve_ssd(v, g)
            dve_gather(v, "ossd0", False)
            for g in range(4, 8):
                dve_ssd(v, g)
            dve_mix(v)
            dve_gather(v, "wout2", False)
            dve_post(v, 0)
            dve_rstd(v, 8, T, 7)
            dve_ada_norm(v, 8, 1)
            dve_ffn(v, 2)
            dve_post(v, 1)

        @block.tensor
        def _(pe):
            pe.wait_ge(S("land_const"), 16 * (len(LOADS) + 2))
            pe_norm(pe, 0, MEM, 0)
            pe_mem(pe)
            pe_norm(pe, 1, T, 1)
            pe_gdn_in(pe)
            pe_heads(pe)
            pe_inverse(pe)
            pe_turned(pe)
            pe_recurrence(pe)
            pe_onorm(pe)
            pe_attention(pe, 0, lambda e, kind, t: taken(e, ("unit", U["memq", 0], t)))
            pe.wait_ge(S("mix_lo"), HG)
            for j in range(2):
                taken(pe, ("value", 0, j))
            pe_linear(pe, "wout0")
            pe_norm(pe, 2, T, 2)
            pe_ffn(pe, 0, hn_ready(pe, 2))
            pe_norm(pe, 3, T, 3)
            pe_kv(pe)
            for i in range(4):
                unit_jobs(pe, U["swaq", i], 0, *hn_of, KT, ready=None if i else hn_ready(pe, 4))
                for j in ROPE_AFTER[i]:
                    pe_rope(pe, j)
            pe.wait_ge(S("roped"), 7)
            pe_attention(pe, 1, lambda e, kind, t: kind == "mem" and taken(e, ("unit", U["swaq", 3], t)))
            for j in range(8):
                taken(pe, ("value", 1, j))
            pe_linear(pe, "wout1")
            pe_norm(pe, 5, T, 4)
            pe_ffn(pe, 1, hn_ready(pe, 5))
            pe_norm(pe, 6, T, 5)
            pe_norm(pe, 7, T, 6)
            pe_linear(pe, "qlat", ready=ada_ready(pe, 0))
            pe_linear(pe, "misc")
            pe_small(pe)
            for i in range(8):
                unit_jobs(pe, U["zed", i], 0, *hn_of, KT)
                if i == 3:
                    pe_small_late(pe)
            pe.wait_ge(S("qn_lo"), 2)
            multi_unit(pe, U["qidx", 0], range(8))
            taken(pe, ("kid",))
            taken(pe, ("unit", U["qidx", 0], 7))
            pe_steps(pe)
            for i in range(2):
                multi_unit(pe, U["uq", i], range(8))
            for t in range(4, 8):
                taken(pe, ("unit", U["uq", 1], t))
            pe_latent(pe)
            pe_values(pe)
            pe_linear(pe, "oattn", ready=lambda k: taken(pe, ("uv", k)))
            for g in range(4):
                pe_ssd(pe, g)
            pe_linear(pe, "ossd0", ready=lambda k: pe.wait_ge(S("y_lo"), k + 1))
            for g in range(4, 8):
                pe_ssd(pe, g)
            pe_linear(pe, "ossd1", ready=lambda k: pe.wait_ge(S("y_lo"), k + 9))
            pe_linear(pe, "wout2", ready=lambda k: pe.wait_ge(S("blend_lo"), k + 1))
            pe_post(pe, 0, ysq)
            pe_norm(pe, 8, T, 7)
            pe_ffn(pe, 2, ada_ready(pe, 1))
            pe_post(pe, 1, sg)


def units_of(w):
    out = []
    for k0 in range(0, w.shape[0], D):
        part = w[k0:k0 + D]
        rows = np.zeros((D, w.shape[1]), np.float32)
        rows[:part.shape[0]] = part
        for c0 in range(0, w.shape[1], 2 * P):
            block = np.zeros((D, 2 * P), np.float32)
            block[:, :min(2 * P, w.shape[1] - c0)] = rows[:, c0:c0 + 2 * P]
            out.append(block.reshape(KT, P, 2 * P).transpose(1, 0, 2).reshape(P, UW))
    return out


def ffn_units(gate_up, down):
    pairs = np.stack([gate_up[:, :FF].reshape(D, FT, P), gate_up[:, FF:].reshape(D, FT, P)], 2)
    gu = units_of(pairs.reshape(D, 2 * FF))
    dn = units_of(down)
    return gu[0:16] + dn[0:4] + gu[16:22] + dn[4:12]


def short_units(w):
    return [w[:, c:c + D].reshape(2, P, D).transpose(1, 0, 2).reshape(P, UW) for c in range(0, w.shape[1], D)]


def tiles(a):
    return np.ascontiguousarray(a.reshape(-1, P, *a.shape[1:]).swapaxes(0, 1))


def layout(i):
    BF = mybir.dt.np(BF16)
    a = {}
    eye = np.eye(P, dtype=np.float32)
    w = []
    for layer in range(2):
        w += units_of(i["w_mem_kv"][layer])
    win = i["gdn_w_in"][0]
    ba = np.zeros((D, P), np.float32)
    ba[:, 0:HG] = win[:, 3072:3072 + HG]
    ba[:, 32:32 + HG] = win[:, 3072 + HG:3072 + 2 * HG]
    w += units_of(ba) + units_of(win[:, 0:3072]) + units_of(win[:, 3072 + 2 * HG:])
    w += units_of(i["w_out"][0]) + ffn_units(i["w_gate_up"][0], i["w_down"][0]) + units_of(i["w_kv"])
    order = np.arange(12 * 64).reshape(2, 6, 64).transpose(1, 0, 2).reshape(-1)
    order = np.concatenate([order, np.arange(12 * 64, D)])
    w += units_of(i["swa_w_q"][0][:, order]) + units_of(i["ada_w_2"]) + units_of(i["w_out"][1][order])
    w += ffn_units(i["w_gate_up"][1], i["w_down"][1])
    cuts = np.cumsum([0, 256, 128, 64, 16, 2048, 4096, 32, D, D])
    qlat, kvl, kid, wid, zed, xbc, dt, ga, gb = (i["w_in_2"][:, lo:hi] for lo, hi in zip(cuts[:-1], cuts[1:]))
    misc = np.concatenate([kvl, kid, wid, np.zeros((D, 16), np.float32), dt], 1)
    w += units_of(qlat) + units_of(misc) + units_of(zed) + short_units(i["w_qidx_2"])
    w += units_of(xbc) + units_of(ga) + units_of(gb) + short_units(i["w_uq_2"])
    w += units_of(i["w_o_attn_2"]) + units_of(i["w_o_ssd_2"]) + units_of(i["w_out_2"])
    w += ffn_units(i["w_ffn_in_2"], i["w_ffn_out_2"])
    a["W"] = np.stack(w)
    a["xT"] = tiles(i["x"][0].T)
    a["memT"] = tiles(i["mem"][0].T)
    a["ident"] = eye
    a["identb"] = eye.astype(BF)
    a["ones"] = np.ones((P, P), np.float32)
    a["gains"] = np.ascontiguousarray(np.stack([g.reshape(KT, P) for g in (
        i["ln_mem"], i["ln_mix"][0], i["ln_ffn"][0], i["ln_kv"], i["ln_mix"][1], i["ln_ffn"][1],
        i["ln_final"])]).transpose(2, 0, 1))
    sinks = np.full((8, 2), NEG, np.float32)
    sinks[0:6] = i["swa_sinks"][0].reshape(2, 6).T
    a["sinks"] = np.tile(sinks, (P, 1, 1))
    a["cw"] = tiles(i["gdn_conv"][0].T)
    a["gng"] = i["gdn_norm"][0].reshape(P, 1)
    a["gcst"] = np.ascontiguousarray(np.stack([i["gdn_dt_bias"][0], i["gdn_A_log"][0]], 1))
    a["col1"] = np.zeros((P, 127), np.float32)
    a["col1"][:, 63] = 1
    a["sel"] = np.zeros((64, 2 * HG, P), np.float32)
    for h in range(HG):
        a["sel"][h, h] = 1
        a["sel"][32 + h, HG + h] = 1
    s, c = np.arange(P)[:, None], np.arange(P)[None, :]
    a["mask4"] = np.tile(np.where(s > c, NEG, 0.0), (1, 4)).astype(BF)
    a["strict"] = (s < c).astype(np.float32)
    a["levels"] = np.stack([((s >> lv) % 2 == 1) & ((s >> lv) - 1 == (c >> lv)) for lv in range(7)], 1)\
        .astype(np.float32)
    reset = np.ones((HG, T), np.float32)
    reset[:, ::P] = 0
    a["reset"] = reset
    f = np.arange(P) % 64
    inv = (np.float32(500000.0) ** (-np.arange(0, 16, 2, dtype=np.float32) / np.float32(16))).astype(np.float32)
    a["rcol"] = np.zeros((P, 2), np.float32)
    a["rcol"][:, 0] = np.where(f < 16, inv[f % 8], 0)
    a["rcol"][:, 1] = np.where(f < 8, -1, np.where(f < 16, 1, 0))
    a["perm"] = np.zeros((P, P), np.float32)
    for r in np.flatnonzero(f < 16):
        a["perm"][r + 8 if f[r] < 8 else r - 8, r] = 1
    k = np.arange(256)[None, :]
    a["band"] = np.where((k > s) & (k <= s + P), 0.0, NEG).astype(BF)
    a["posi"] = np.tile(i["positions"].astype(np.int32), (P, 1))
    a["mod"] = tiles(i["ada_b_2"])
    a["c_col"] = tiles(i["c_2"][0])
    a["gain2"] = np.ascontiguousarray(np.stack([i[g + "_2"].reshape(KT, P) for g in (
        "pre_norm_mix", "post_norm_mix", "pre_norm_ffn", "post_norm_ffn")]).transpose(2, 0, 1))
    small = np.zeros((P, 6), np.float32)
    small[:, 0:2] = tiles(i["q_norm_2"])
    small[:, 2] = i["kv_norm_2"]
    small[0:64, 3] = i["kidx_norm_2"]
    small[96:128, 4] = i["dt_bias_2"]
    small[96:128, 5] = i["a_log_2"]
    a["small2"] = small
    a["cw2"] = np.concatenate([tiles(i["conv_w_2"].T), tiles(i["conv_b_2"])[:, :, None]], 2)
    a["dskip"] = tiles(np.repeat(i["d_skip_2"], 64))
    a["ssdg"] = tiles(i["ssd_norm_2"])
    a["mask2"] = a["mask4"]
    a["reset2"] = np.tile(reset[0], (P, 1))
    a["wuv"] = np.ascontiguousarray(i["w_uv_2"].transpose(1, 0, 2).reshape(P, 16 * 64))
    a["bcol"] = (np.arange(P) % 32).astype(np.float32)[:, None]
    a["qpi"] = tiles(i["positions_2"][0].astype(np.int32))
    a["posi2"] = np.tile(i["positions_2"].astype(np.int32), (P, 1))
    a["qsel4"] = (s == np.arange(32 * P)[None, :] // 32).astype(BF)
    a["qsel8"] = (s == np.arange(16 * P)[None, :] // 16).astype(BF)
    tbl = np.zeros((4, 32, 2, 8, 16), np.float32)
    for q in range(8):
        tbl[q % 4, :, q // 4, q, :] = i["rel_bias_2"]
    a["tbl"] = tbl.reshape(P, 2 * P)
    return a


def kernel(**inputs):
    import concourse.bacc as bacc
    from concourse.bass_utils import run_bass_kernel_spmd

    arrays = layout({name: np.asarray(value) for name, value in inputs.items()})
    nc = bacc.Bacc("TRN2", target_bir_lowering=False, num_devices=1)
    I = {k: nc.dram_tensor("in_" + k, v.shape, mybir.dt.from_np(v.dtype), kind="ExternalInput").ap()
         for k, v in arrays.items()}
    O = {"out": nc.dram_tensor("out_x", (P, KT, T), F32, kind="ExternalOutput").ap()}
    build(nc, I, O)
    result = run_bass_kernel_spmd(nc, [{"in_" + k: v for k, v in arrays.items()}], core_ids=[0])
    out = result.results[0]["out_x"]
    return np.ascontiguousarray(out.transpose(1, 0, 2).reshape(1, D, T).transpose(0, 2, 1))
```

```python
import math
from contextlib import ExitStack

import numpy as np

import concourse.bass as bass
from concourse import mybir

F32 = mybir.dt.float32
F32R = mybir.dt.float32r
BF16 = mybir.dt.bfloat16
I32 = mybir.dt.int32
ALU = mybir.AluOpType
ACT = mybir.ActivationFunctionType
AX = mybir.AxisListType.X

P = 128
T = 512
D = 1024
KT = D // P
MEM = 256
HG = 6
NC = T // P
FF = 2816
FT = FF // P
CHUNKS = [8, 8, 6]
EPS = 1e-6
NEG = -1e30
ROUND = 12582912.0
PI2 = (6.28125, 0.0019340515136718750, 1.2556659146e-06)
PI_IN = 3.14159250
ROPE_LOADS = 4
ROPE_AFTER = [(), (6, 0, 1), (2, 3), (4, 5)]
NG = 64
RD = 16
FILL, MARK = -3.0e38, -3.4e38
BUCKET_STEPS = (12, 16, 23, 32, 46, 64, 91)
UW = 2048


def unit_list():
    units = []

    def add(name, n):
        units.extend((name, i) for i in range(n))

    def ffn(f):
        for name, c in (("gu", 0), ("gu", 1), ("dn", 0), ("gu", 2), ("dn", 1), ("dn", 2)):
            add(f"{name}{f}{c}", CHUNKS[c] if name == "gu" else 4)

    add("mem", 4)
    add("ba", 1)
    add("qkv", 9)
    add("z", 3)
    add("memq", 1)
    add("wout0", 4)
    ffn(0)
    add("kv", 1)
    add("swaq", 4)
    add("ada", 24)
    add("wout1", 4)
    ffn(1)
    add("qlat", 1)
    add("misc", 1)
    add("zed", 8)
    add("qidx", 1)
    add("xbc", 16)
    add("gab", 8)
    add("uq", 2)
    add("oattn", 4)
    add("ossd0", 4)
    add("ossd1", 4)
    add("wout2", 4)
    ffn(2)
    return units


UNITS = unit_list()
NU = len(UNITS)
U = {}
for _u, (_name, _i) in enumerate(UNITS):
    U[_name, _i] = _u


def attention_items(layer):
    items = []
    if layer == 1:
        items += [("swa", t, b) for t in range(6) for b in range(NC)]
    items += [("mem", t, b) for t in range(2) for b in range(NC)]
    return items


class Banks:

    def __init__(self):
        self.uses = [0] * 8
        self.at = {}

    def add(self, key, bank):
        assert key not in self.at, key
        self.at[key] = (bank, self.uses[bank])
        self.uses[bank] += 1

    def rotate(self, keys, banks):
        for i, key in enumerate(keys):
            self.add(key, banks[i % len(banks)])


def bank_plan():
    k = Banks()

    def units(name, tiles=2):
        i = 0
        while (name, i) in U:
            u = U[name, i]
            for t in range(tiles):
                k.add(("unit", u, t), 2 * (u % 2) + t % 2 if tiles < 8 else t % 4)
            i += 1

    def ffn(f):
        for name in ("gu", 0), ("gu", 1), ("dn", 0), ("gu", 2), ("dn", 1), ("dn", 2):
            units(f"{name[0]}{f}{name[1]}")

    def attention(layer):
        items = attention_items(layer)
        for n in range(len(items) + 3):
            if n < len(items):
                for s in range(2):
                    k.add(("score", layer, n, s), (4, 2)[n % 2] + s)
            if 2 <= n < len(items) + 2:
                k.add(("turn", layer, n - 2), 6 + n % 2)
            if n >= 3 and items[n - 3][2] == 0:
                k.add(("value", layer, (n - 3) // NC), 0)
            if layer == 1:
                if 1 <= n <= 24:
                    k.add(("ada_turn", n - 1), 1)
                if n < 24:
                    k.add(("unit", U["ada", n], 0), 1)

    k.add(("norm", 0), 4)
    units("mem")
    k.add(("norm", 1), 4)
    units("ba", 1)
    k.add(("cols",), 6)
    k.add(("l2",), 4)
    units("qkv")
    units("z")
    units("memq")
    k.rotate([("l2b", j) for j in range(2 * HG)], [5, 6, 7])
    k.rotate([(x, h) for h in range(HG) for x in ("gm", "gp", "bb", "kk", "qk")], range(8))
    k.rotate([(x, lv, h) for lv in range(7) for x in ("iz", "iw") for h in range(HG)
              for x in ([x] if x == "iz" else ["iw", "iv"]) if not (x == "iw" and lv == 6)], range(8))
    k.rotate([(x, h) for h in range(HG) for x in ("vt", "kt")], range(8))
    for c in range(NC):
        k.rotate([(x, c, h) for x in ("ks", "vn") for h in range(HG) if c or x == "vn"], range(8))
        k.rotate([(x, c, h) for h in range(HG) for x in ("oo", "su") if c < NC - 1 or x == "oo"], range(8))
    k.add(("onorm",), 0)
    k.rotate([("ob", h) for h in range(HG)], [1, 2, 3])
    attention(0)
    units("wout0")
    k.add(("norm", 2), 4)
    ffn(0)
    k.add(("norm", 3), 4)
    units("kv")
    units("swaq")
    k.rotate([("rope", j) for j in (6, 0, 1, 2, 3, 4, 5)], [4, 5, 6, 7])
    attention(1)
    units("wout1")
    k.add(("norm", 5), 4)
    ffn(1)
    k.add(("norm", 6), 4)
    k.add(("norm", 7), 4)
    units("qlat")
    units("misc")
    units("zed")
    for i, name in enumerate(("qn", "kvn", "kin", "kid", "kvt", "c1", "c2", "cl")):
        k.add((name,), 4 + i % 4)
    units("qidx", 8)
    for i in range(24):
        name, j = ("xbc", i) if i < 16 else ("gab", i - 16)
        for t in range(2):
            k.add(("unit", U[name, j], t), 2 * (U[name, j] % 2) + t)
        for n in (2 * i, 2 * i + 1):
            if n < 32:
                for s in range(2):
                    k.add(("index", n, s), 4 + 2 * (n % 2) + s)
    units("uq", 8)
    for n in range(NG + 5):
        if n < NG:
            for e in range(2):
                k.add(("ohb", n, e), e)
        if 1 <= n <= NG:
            k.add(("logit", n - 1), 2 + (n - 1) % 2)
        if 3 <= n < NG + 3:
            k.add(("ptp", n - 3), 4 + (n - 3) % 2)
        if n >= 4 and (n - 4) % 4 == 3:
            k.add(("latent", (n - 4) // 4), 6 + (n - 4) // 4 % 2)
    k.rotate([("uv", t) for t in range(8)], [0, 1, 2, 3])
    units("oattn")
    for part in range(2):
        def turned(g):
            one, two = ((0, 1), (7, 2))[g % 2]
            for name, b in (("xt", g, 0), one), (("xt", g, 1), two), (("bt", g), 6), (("cb", g), 3):
                k.add(name, b)

        turned(4 * part)
        for g in range(4 * part, 4 * part + 4):
            one, two = ((0, 1), (7, 2))[g % 2]
            other, another = ((0, 1), (7, 2))[1 - g % 2]
            for t in range(2):
                for s in range(2):
                    k.add(("lm", g, t, s), ((4, 5), (6, 3))[t][s])
            for c in range(2):
                k.add(("st", g, c), another)
            k.add(("yd", g, 0), other)
            k.add(("yo", g, 0), another)
            k.add(("yd", g, 1), one)
            k.add(("yo", g, 1), two)
            if g % 4 < 3:
                turned(g + 1)
        units(f"ossd{part}")
    k.add(("ssn",), 7)
    units("wout2")
    k.add(("post", 0), 4)
    k.add(("norm", 8), 4)
    ffn(2)
    k.add(("post", 1), 4)
    return k.at


BANK = bank_plan()
COUNT = {name: sum(n == name for n, _ in UNITS) for name, _ in UNITS}
LAST_TILE = [{"ba": 0, "ada": 0, "qidx": 7, "uq": 7}.get(name, 1) for name, _ in UNITS]


def build(nc, I, O):
    ctx = ExitStack()
    with ctx:
        names = {}

        def S(name):
            if name not in names:
                names[name] = ctx.enter_context(nc.semaphore(name))
            return names[name]

        def sb(name, shape, dt, scope=ctx):
            return scope.enter_context(nc.sbuf_tensor(name, shape, dt))

        banks = ctx.enter_context(nc.psum_tensor("banks", [P, 8, T], F32))
        psum = [banks[:, b, :] for b in range(8)]
        bank_full = [S(f"bank_full{b}") for b in range(8)]
        bank_read = [S(f"bank_read{b}") for b in range(8)]

        def bank(key):
            return psum[BANK[key][0]]

        def open_bank(pe, key):
            b, n = BANK[key]
            if n:
                pe.wait_ge(bank_read[b], n)

        def fills(key):
            return bank_full[BANK[key][0]]

        def full(eng, key):
            b, n = BANK[key]
            eng.wait_ge(bank_full[b], n + 1)

        def reads(key):
            return bank_read[BANK[key][0]]

        def taken(eng, key):
            b, n = BANK[key]
            eng.wait_ge(bank_read[b], n + 1)

        x = sb("x", [P, KT, T], F32)
        raw = sb("raw", [P, 2, UW], F32)
        w_hi = sb("w_hi", [P, 2, UW], F32R)
        w_lo = sb("w_lo", [P, 2, UW], F32R)
        rs = sb("rs", [P, T], F32)
        ident = sb("ident", [P, P], F32)
        identb = sb("identb", [P, P], BF16)
        ones = sb("ones", [P, P], F32)
        eps = sb("eps", [P, 1], F32)
        gains = sb("gains", [P, 7, KT], F32)
        mem_k = sb("mem_k", [P, 2, 2, MEM], F32)
        mem_v = sb("mem_v", [P, 2, 2, MEM], F32)
        mem_q = sb("mem_q", [P, 2, T], F32)
        stat = sb("stat", [P, 2, 5, 2], F32)
        sinks = sb("sinks", [P, 8, 2], F32)
        nsinks = sb("nsinks", [P, 8, 2], F32)
        mod = sb("mod", [P, 48], F32)
        gain2 = sb("gain2", [P, 4, KT], F32)
        c_col = sb("c_col", [P, KT], F32)
        c_pair = sb("c_pair", [P, KT, 2], F32R)
        arow = sb("arow", [2, 2, 256], F32)

        with ExitStack() as core:
            lt = sb("lt", [P, HG, T], F32, core)
            at = sb("at", [P, HG, T], F32, core)
            xi = sb("xi", [P, HG, T], F32, core)
            xt = sb("xt", [P, HG, T], F32, core)
        with ExitStack() as lat:
            qsel4 = sb("qsel4", [P, 32 * P], BF16, lat)
            qsel8 = sb("qsel8", [P, 16 * P], BF16, lat)
            oh = sb("oh", [P, 2, 2, T], BF16, lat)
            pr2 = sb("pr2", [P, 3, T], F32, lat)
            ptt = sb("ptt", [P, 2, NC, T], F32, lat)
            tbl = sb("tbl", [P, 2 * P], F32, lat)
            tbl3 = sb("tbl3", [P, 3, 2 * P], BF16, lat)
        hn_hi = sb("hn_hi", [P, KT, T], F32R)
        hn_lo = sb("hn_lo", [P, KT, T], F32R)
        tmp = sb("tmp", [P, KT, T], F32)
        with ExitStack() as s1:
            qkv = sb("qkv", [P, 3 * HG, T], F32, s1)
            zs = sb("zs", [P, HG, T], F32, s1)
            bg = sb("bg", [64, T], F32, s1)
            rows = sb("rows", [64, T], F32, s1)
            cols = sb("cols", [P, NC, 64], F32, s1)
            nbe = sb("nbe", [P, NC, HG], F32, s1)
            elast = sb("elast", [P, HG, NC], F32, s1)
            glast = sb("glast", [P, HG, NC], F32, s1)
            cw = sb("cw", [P, 3 * HG, 4], F32, s1)
            gcst = sb("gcst", [64, 2], F32, s1)
            gng = sb("gng", [P, 1], F32, s1)
            col1 = sb("col1", [P, 127], F32, s1)
            sel = sb("sel", [64, 2 * HG, P], F32, s1)
            mask4 = sb("mask4", [P, T], BF16, s1)
            strict = sb("strict", [P, P], F32, s1)
            levels = sb("levels", [P, 7, P], F32, s1)
            with ExitStack() as z1:
                bt = sb("bt", [64, 3, T], F32, z1)
                reset = sb("reset", [64, T], F32, z1)
                sq = sb("sq", [P, 2, T], F32, z1)
            with ExitStack() as z2:
                kb = sb("kb", [P, 2, T], F32, z2)
                dec = sb("dec", [P, 2, T], F32, z2)
                eg = sb("eg", [P, 2, T], F32, z2)
            with ExitStack() as z3:
                zm = sb("zm", [P, HG, T], F32, z3)
            with ExitStack() as z4:
                state = sb("state", [P, HG, P], F32, z4)
                vn = sb("vn", [P, HG, P], F32, z4)
                rr = sb("rr", [P, HG, P], F32, z4)
                osq = sb("osq", [P, T], F32, z4)
        with ExitStack() as s2:
            pr = sb("pr", [P, 3, 2, 256], F32, s2)
            pt = sb("pt", [P, 2, T], F32, s2)
            qr = sb("qr", [P, 6, T], F32, s2)
            kr = sb("kr", [P, T], F32, s2)
            qraw = sb("qraw", [P, 7, T], F32, s2)
            vs = sb("vs", [P, NC, P], F32, s2)
            cosv = sb("cosv", [P, T], F32, s2)
            sinv = sb("sinv", [P, T], F32, s2)
            ang = sb("ang", [P, 4, T], F32, s2)
            posi = sb("posi", [P, T], I32, s2)
            rcol = sb("rcol", [P, 2], F32, s2)
            perm = sb("perm", [P, P], F32, s2)
            band = sb("band", [P, 256], BF16, s2)
        with ExitStack() as s3:
            hid_hi = sb("hid_hi", [P, 2, 8, T], F32R, s3)
            hid_lo = sb("hid_lo", [P, 2, 8, T], F32R, s3)
            sg = sb("sg", [P, 2, T], F32, s3)
            prod = sb("prod", [P, 2, T], F32, s3)
        with ExitStack() as s4:
            c1 = sb("c1", [P, NC, P], F32, s4)
            c2 = sb("c2", [P, NC, 32], F32, s4)
            r2_hi = sb("r2_hi", [P, T], F32R, s4)
            r2_lo = sb("r2_lo", [P, T], F32R, s4)
            pick = sb("pick", [P, 32], F32R, s4)
            small2 = sb("small2", [P, 6], F32, s4)
            cw2 = sb("cw2", [P, 32, 5], F32, s4)
            dskip = sb("dskip", [P, 16], F32, s4)
            ssdg = sb("ssdg", [P, 16], F32, s4)
            causal = sb("causal", [P, P], F32, s4)
            tolast = sb("tolast", [P, NC, 32], F32, s4)
            cdall = sb("cdall", [P, 32, NC], F32, s4)
            with ExitStack() as s5:
                qh = sb("qh", [P, T * 16], F32, s5)
                r1 = sb("r1", [P, T], F32, s5)
                kvf = sb("kvf", [P, T], F32, s5)
                kvt = sb("kvt", [P, NC, P], F32, s5)
                ki = sb("ki", [P, T], F32, s5)
                madd = sb("madd", [P, NC, T], BF16, s5)
                bkt = sb("bkt", [P, NC, T], BF16, s5)
                cs = sb("cs", [P, 2, T], F32, s5)
                qn_hi = sb("qn_hi", [P, 2, T], F32R, s5)
                qn_lo = sb("qn_lo", [P, 2, T], F32R, s5)
                wcol = sb("wcol", [P, NC, 16], F32, s5)
                m8 = sb("m8", [P, 2, 8], F32, s5)
                qpi = sb("qpi", [P, 4], I32, s5)
                qpc = sb("qpc", [P, 2, 4], F32, s5)
                bcol = sb("bcol", [P, 1], F32, s5)
                st2 = sb("st2", [P, 3, 4], F32, s5)
                wuv = sb("wuv", [P, 16 * 64], F32, s5)
            with ExitStack() as s6:
                qi = sb("qi", [P, 8, T], F32, s6)
                reset2 = sb("reset2", [P, T], F32, s6)
                relu = sb("relu", [P, 2, T], F32, s6)
                oneh = sb("oneh", [P, T], F32, s6)
                cs2 = sb("cs2", [P, T], F32, s6)
                diag = sb("diag", [P, 32, NC], F32, s6)
            with ExitStack() as s7:
                ma = sb("ma", [P, KT, T], F32, s7)
                grp = sb("grp", [P, 2, 4, T], F32, s7)
                zt = sb("zt", [P, 2, T], F32, s7)
                ysq = sb("ysq", [P, 2, T], F32, s7)
                btok = sb("btok", [P, NC - 1, P], F32, s7)
                xd = sb("xd", [P, NC, 2, P], F32, s7)
                xdk = sb("xdk", [P, NC - 1, 2, P], F32, s7)
                lb = sb("lb", [P, 2, 2, T], F32, s7)
                cbm = sb("cbm", [P, T], F32, s7)
                ea = sb("ea", [P, T], F32, s7)
                ysd = sb("ysd", [P, 2, T], F32, s7)
                sst = sb("sst", [P, 3, 2, P], F32, s7)

        r2 = tmp[:, 5, :]
        spill = nc.dram_tensor("spill", [64, P, T], F32, kind="Internal").ap()

        w_land = [S("w_land0"), S("w_land1")]
        W3 = lambda ap, slot: ap[:, slot, :].rearrange("p (k c) -> p k c", k=KT)

        def prep_hi(act, u, i=0):
            if isinstance(i, int) and u + 2 + 2 * i >= NU:
                return
            slot = u % 2
            act.wait_ge(w_land[slot], (i + ((u + 2) // 2 + 1)) * 16)
            b, n = BANK["unit", u, LAST_TILE[u]]
            act.wait_ge(bank_full[b], i + (n + 1))
            act.activation(w_hi[:, slot, :], raw[:, slot, :], ACT.Copy).then_inc(S("w_hi"), 1)

        def unit_jobs(pe, u, i, xh, xl, nkt, n=T, ready=None):
            pe.wait_ge(S("w_lo"), i * 2 + (u + 1))
            hi, lo = W3(w_hi, u % 2), W3(w_lo, u % 2)
            tiles_ = range(LAST_TILE[u] + 1)
            for t in tiles_:
                b, n0 = BANK["unit", u, t]
                assert isinstance(i, int) or n0 > 0
                if not (isinstance(i, int) and i + n0 == 0):
                    pe.wait_ge(bank_read[b], i + n0)
            order = [(k, t) for k in range(nkt) for t in tiles_] if ready else \
                [(k, t) for t in tiles_ for k in range(nkt)]
            for k, t in order:
                if ready and t == 0:
                    ready(k)
                b = BANK["unit", u, t][0]
                out = psum[b][:, 0:n]
                wh, wl = hi[:, k, t * P:(t + 1) * P], lo[:, k, t * P:(t + 1) * P]
                pe.matmul(out, wh, xh(k), start=(k == 0), stop=False)
                pe.matmul(out, wh, xl(k), start=False, stop=False)
                mm = pe.matmul(out, wl, xh(k), start=False, stop=(k == nkt - 1))
                if k == nkt - 1:
                    mm.then_inc(bank_full[b], 1)

        def over_units(eng, name, body, first=0):
            n = COUNT[name]
            u0 = U[name, 0] + first
            pairs = (n - first) // 2
            if u0 + n - first + 2 > NU:
                pairs = 0
            if pairs >= 2:
                with eng.Fori(0, pairs) as i:
                    body(u0, i)
                    body(u0 + 1, i)
            else:
                pairs = 0
            for u in range(u0 + 2 * pairs, U[name, 0] + n):
                body(u, 0)

        hn_of = (lambda k: hn_hi[:, k, :], lambda k: hn_lo[:, k, :])

        def pe_linear(pe, name, nkt=KT, ready=None):
            first = 0
            if ready:
                unit_jobs(pe, U[name, 0], 0, *hn_of, nkt, ready=ready)
                first = 1
            if first < COUNT[name]:
                over_units(pe, name, lambda u, i: unit_jobs(pe, u, i, *hn_of, nkt), first)

        def act_norm(a, i, src, n, ready, between=None):
            for k in range(KT):
                ready(a, k)
                a.activation(tmp[:, k, 0:n], src(k), ACT.Square).then_inc(S("squared"), 1)
            if between:
                between()
            full(a, ("norm", i))
            a.activation(rs[:, 0:n], bank(("norm", i))[:, 0:n], ACT.Sqrt, bias=eps[:, 0:1],
                         scale=1.0 / D).then_inc(reads(("norm", i)), 1)

        def act_norm_round(a, i, n=T):
            if i == 4:
                full(a, ("unit", U["kv", 0], 1))
            for k in range(KT):
                a.wait_ge(S("normed"), KT * i + k + 1)
                a.activation(hn_hi[:, k, 0:n], tmp[:, k, 0:n], ACT.Copy).then_inc(S("hn_hi"), 1)

        def pe_norm(pe, i, n, rank):
            open_bank(pe, ("norm", i))
            for k in range(KT):
                pe.wait_ge(S("squared"), KT * rank + k + 1)
                mm = pe.matmul(bank(("norm", i))[:, 0:n], ones[:, :], tmp[:, k, 0:n], start=(k == 0),
                               stop=(k == KT - 1))
            mm.then_inc(fills(("norm", i)), 1)

        def dve_rstd(v, i, n, rank):
            taken(v, ("norm", i))
            v.reciprocal(rs[:, 0:n], rs[:, 0:n]).then_inc(S("rstd"), 1)
            v.wait_ge(S("rstd"), rank + 1)

        def dve_norm(v, i, g, src, n=T):
            def low(k):
                v.wait_ge(S("hn_hi"), KT * i + k + 1)
                v.tensor_tensor(hn_lo[:, k, 0:n], tmp[:, k, 0:n], hn_hi[:, k, 0:n].bitcast(F32),
                                ALU.subtract).then_inc(S("hn_lo"), 1)
            for k in range(KT):
                v.scalar_tensor_tensor(out=tmp[:, k, 0:n], in0=src(k), scalar=gains[:, g, k:k + 1],
                                       in1=rs[:, 0:n], op0=ALU.mult, op1=ALU.mult).then_inc(S("normed"), 1)
                if k:
                    low(k - 1)
            low(KT - 1)

        def hn_ready(pe, i):
            return lambda k: pe.wait_ge(S("hn_lo"), KT * i + k + 1)

        x_of = lambda k: x[:, k, :]
        memx = qkv[:, 0:4, :].rearrange("p a (b t) -> p (a b) t", b=2)
        mem_of = lambda k: memx[:, k, :]

        SUMS = {"wout0": 0, "dn02": 1, "wout1": 2, "dn12": 3, "wout2": 4, "dn22": 5}
        sq_tmp = lambda k: tmp[:, k, :]

        def act_squares(a, name, key, src, sq):
            r = SUMS[name]
            for i in range(4):
                for t in range(2):
                    k = 2 * i + t
                    taken(a, ("unit", U[name, i], t))
                    if k >= 2:
                        a.wait_ge(S("square_added"), 6 * r + k - 1)
                    a.activation(sq(k), src(k), ACT.Square).then_inc(S("tile_squared"), 1)
                prep_hi(a, U[name, i])
            full(a, key)
            a.activation(rs[:, :], bank(key)[:, :], ACT.Sqrt, bias=eps[:, 0:1], scale=1.0 / D)\
                .then_inc(reads(key), 1)

        def dve_squares(v, name, evacuate, sq):
            r = SUMS[name]
            for k in range(KT):
                key = ("unit", U[name, k // 2], k % 2)
                full(v, key)
                evacuate(k, bank(key)[:, :]).then_inc(reads(key), 1)
                if 1 <= k <= KT - 2:
                    v.wait_ge(S("tile_squared"), KT * r + k + 1)
                    if k > 1:
                        v.wait_ge(S("square_added"), 6 * r + k - 1)
                    v.tensor_tensor(sq(0), sq(0), sq(k), ALU.add).then_inc(S("square_added"), 1)

        def pe_squares(pe, name, key, sq):
            r = SUMS[name]
            open_bank(pe, key)
            pe.wait_ge(S("square_added"), 6 * r + 6)
            pe.matmul(bank(key)[:, :], ones[:, :], sq(0), start=True, stop=False)
            pe.wait_ge(S("tile_squared"), KT * r + KT)
            pe.matmul(bank(key)[:, :], ones[:, :], sq(KT - 1), start=False, stop=True).then_inc(fills(key), 1)

        def to_x(v):
            return lambda k, out: v.tensor_tensor(x[:, k, :], x[:, k, :], out, ALU.add)

        def to_tmp(v, add):
            return lambda k, out: (v.tensor_tensor(tmp[:, k, :], tmp[:, k, :], out, ALU.add) if add
                                   else v.tensor_copy(tmp[:, k, :], out))

        def over_ffn(f, gate_up, down):
            for kind, c in (("gu", 0), ("gu", 1), ("dn", 0), ("gu", 2), ("dn", 1), ("dn", 2)):
                (gate_up if kind == "gu" else down)(f"{kind}{f}{c}", c)

        def pe_ffn(pe, f, ready):
            def gate_up(name, c):
                pe_linear(pe, name, ready=ready if c == 0 else None)

            def down(name, c):
                pe.wait_ge(S("hid_lo"), FT * f + sum(CHUNKS[:c + 1]))
                over_units(pe, name, lambda u, j: unit_jobs(
                    pe, u, j, lambda k: hid_hi[:, c % 2, k, :], lambda k: hid_lo[:, c % 2, k, :], CHUNKS[c]))
            over_ffn(f, gate_up, down)

        def act_ffn(a, f):
            def gate_up(name, c):
                u0 = U[name, 0]

                def body(u, i):
                    q = (u - u0) % 2
                    bg_, ng = BANK["unit", u, 0]
                    a.wait_ge(bank_full[bg_], i + (ng + 1))
                    a.activation(sg[:, q, :], psum[bg_][:, :], ACT.Silu).then_inc(bank_read[bg_], 1)
                    prep_hi(a, u, i)
                    bu, nu = BANK["unit", u, 1]
                    a.wait_ge(bank_read[bu], i + (nu + 1))
                    a.activation(hid_hi[:, c % 2, i * 2 + (u - u0), :], prod[:, q, :], ACT.Copy)\
                        .then_inc(S("hid_hi"), 1)
                over_units(a, name, body)

            def down(name, c):
                if c < 2:
                    over_units(a, name, lambda u, i: prep_hi(a, u, i))
                elif f == 2:
                    act_squares(a, name, ("post", 1), sq_tmp, lambda k: sg[:, min(k, 1), :])
                else:
                    act_squares(a, name, ("norm", 3 + 3 * f), x_of, sq_tmp)
            over_ffn(f, gate_up, down)

        def dve_ffn(v, f):
            def gate_up(name, c):
                u0 = U[name, 0]
                h0 = FT * f + sum(CHUNKS[:c])

                def body(u, i):
                    q = (u - u0) % 2
                    bu, nu = BANK["unit", u, 1]
                    bg_, ng = BANK["unit", u, 0]
                    v.wait_ge(bank_read[bg_], i + (ng + 1))
                    v.wait_ge(bank_full[bu], i + (nu + 1))
                    v.tensor_tensor(prod[:, q, :], sg[:, q, :], psum[bu][:, :], ALU.mult).then_inc(bank_read[bu], 1)
                    v.wait_ge(bank_read[bu], i + (nu + 1))
                    v.wait_ge(S("hid_hi"), i * 2 + (h0 + u - u0 + 1))
                    v.tensor_tensor(hid_lo[:, c % 2, i * 2 + (u - u0), :], prod[:, q, :],
                                    hid_hi[:, c % 2, i * 2 + (u - u0), :].bitcast(F32),
                                    ALU.subtract).then_inc(S("hid_lo"), 1)
                over_units(v, name, body)

            def down(name, c):
                if c == 2 and f == 2:
                    dve_squares(v, name, to_tmp(v, True), lambda k: sg[:, min(k, 1), :])
                elif c == 2:
                    dve_squares(v, name, to_x(v), sq_tmp)
                elif f == 2:
                    dve_gather(v, name, c > 0)
                else:
                    dve_residual(v, name)
            over_ffn(f, gate_up, down)

        def dve_residual(v, name):
            u0 = U[name, 0]

            def body(u, i):
                for t in range(2):
                    b, n = BANK["unit", u, t]
                    v.wait_ge(bank_full[b], i + (n + 1))
                    xk = x[:, i * 4 + (2 * (u - u0) + t), :]
                    v.tensor_tensor(xk, xk, psum[b][:, :], ALU.add).then_inc(bank_read[b], 1)
            over_units(v, name, body)

        def dve_gather(v, name, add):
            u0 = U[name, 0]

            def body(u, i):
                for t in range(2):
                    b, n = BANK["unit", u, t]
                    v.wait_ge(bank_full[b], i + (n + 1))
                    tk = tmp[:, i * 4 + (2 * (u - u0) + t), :]
                    if add:
                        v.tensor_tensor(tk, tk, psum[b][:, :], ALU.add).then_inc(bank_read[b], 1)
                    else:
                        v.tensor_copy(tk, psum[b][:, :]).then_inc(bank_read[b], 1)
            over_units(v, name, body)

        def pe_mem(pe):
            for layer in range(2):
                u = U["mem", 2 * layer]
                unit_jobs(pe, u, 0, lambda k: hn_hi[:, k, 0:MEM], lambda k: hn_lo[:, k, 0:MEM], KT, n=MEM,
                          ready=hn_ready(pe, 0))
                u += 1
                pe.wait_ge(S("w_lo"), u + 1)
                hi, lo = W3(w_hi, u % 2), W3(w_lo, u % 2)
                for t in range(2):
                    key = ("unit", u, t)
                    open_bank(pe, key)
                    for k in range(KT):
                        xh, xl = hn_hi[:, k, t * P:(t + 1) * P], hn_lo[:, k, t * P:(t + 1) * P]
                        pe.matmul(bank(key)[:, 0:MEM], xh, hi[:, k, :], start=(k == 0), stop=False)
                        pe.matmul(bank(key)[:, 0:MEM], xh, lo[:, k, :], start=False, stop=False)
                        mm = pe.matmul(bank(key)[:, 0:MEM], xl, hi[:, k, :], start=False, stop=(k == KT - 1))
                    mm.then_inc(fills(key), 1)

        def dve_mem(v):
            for layer in range(2):
                for what, u in ((mem_k, U["mem", 2 * layer]), (mem_v, U["mem", 2 * layer + 1])):
                    for t in range(2):
                        key = ("unit", u, t)
                        full(v, key)
                        v.tensor_copy(what[:, layer, t, :], bank(key)[:, 0:MEM]).then_inc(reads(key), 1)

        def att_args(layer, n):
            kind, t, b = attention_items(layer)[n]
            if kind == "mem":
                halves = [mem_v[:, layer, m, t * P:(t + 1) * P] for m in range(2)]
                return kind, t, b, mem_q, mem_k[:, layer, t, :], halves, 6 + t
            k0 = (b - 1) * P if b else 0
            halves = [vs[:, m, :] for m in ([b - 1, b] if b else [0])]
            return kind, t, b, qr, kr[:, k0:(b + 1) * P], halves, t

        ATT0 = len(attention_items(0))
        V0 = 2

        def pe_attention(pe, layer, ready):
            items = attention_items(layer)
            g0 = ATT0 * layer
            for n in range(len(items) + 3):
                if n < len(items):
                    kind, t, b, q, keys, halves, _ = att_args(layer, n)
                    w = P * len(halves)
                    key = [("score", layer, n, s_) for s_ in range(2)]
                    ready(pe, kind, t)
                    for s_ in range(2):
                        open_bank(pe, key[s_])
                        if kind == "swa":
                            pe.matmul(bank(key[s_])[:, 0:w], identb[:, :], band[:, 256 - w:256],
                                      start=True, stop=False)
                    for s_ in range(2):
                        h = slice(64 * s_, 64 * s_ + 64)
                        pe.matmul(bank(key[s_])[:, 0:w], q[h, t, b * P:(b + 1) * P], keys[h, :],
                                  start=(kind == "mem"), stop=True).then_inc(fills(key[s_]), 1)
                if 2 <= n < len(items) + 2:
                    m = n - 2
                    kind, t, b, q, keys, halves, _ = att_args(layer, m)
                    key = ("turn", layer, m)
                    open_bank(pe, key)
                    pe.wait_ge(S("prob_normed"), 2 * (g0 + m) + 2)
                    nh = len(halves)
                    for j in range(2 * nh):
                        mm = pe.transpose(bank(key)[:, j * P:(j + 1) * P],
                                          pr[:, (g0 + m) % 3, j // nh, (j % nh) * P:(j % nh + 1) * P], ident[:, :])
                    mm.then_inc(fills(key), 1)
                if n >= 3:
                    m = n - 3
                    kind, t, b, q, keys, halves, _ = att_args(layer, m)
                    key = ("value", layer, m // NC)
                    if b == 0:
                        open_bank(pe, key)
                    taken(pe, ("turn", layer, m))
                    nh = len(halves)
                    for s_ in range(2):
                        for j, vh in enumerate(halves):
                            mm = pe.matmul(bank(key)[64 * s_:64 * s_ + 64, b * P:(b + 1) * P],
                                           vh[:, 64 * s_:64 * s_ + 64],
                                           pt[:, (g0 + m) % 2, (s_ * nh + j) * P:(s_ * nh + j + 1) * P],
                                           start=(j == 0), stop=(j == nh - 1), skip_group_check=True)
                    if b == NC - 1:
                        mm.then_inc(fills(key), 1)
                if layer == 1:
                    pe_ada(pe, n)

        def pe_ada(pe, n):
            if 1 <= n <= 24:
                key = ("ada_turn", n - 1)
                open_bank(pe, key)
                taken(pe, ("unit", U["ada", n - 1], 0))
                for t in range(2):
                    mm = pe.matmul(bank(key)[:, t:t + 1], arow[:, (n - 1) % 2, t * P:(t + 1) * P], ones[0:2, 0:1],
                                   start=True, stop=True)
                mm.then_inc(fills(key), 1)
            if n < 24:
                u = U["ada", n]
                key = ("unit", u, 0)
                open_bank(pe, key)
                pe.wait_ge(S("w_lo"), u + 1)
                pe.wait_ge(S("c_split"), 2)
                hi, lo = W3(w_hi, u % 2), W3(w_lo, u % 2)
                for k in range(KT):
                    pe.matmul(bank(key)[0:2, 0:256], c_pair[:, k, :], hi[:, k, :], start=(k == 0), stop=False)
                    mm = pe.matmul(bank(key)[0:2, 0:256], c_pair[:, k, :], lo[:, k, :], start=False,
                                   stop=(k == KT - 1))
                mm.then_inc(fills(key), 1)

        def sink_col(kind, t):
            return t if kind == "swa" else 6 + t

        def dve_attention(v, layer):
            items = attention_items(layer)
            g0 = ATT0 * layer
            for n in range(len(items) + 3):
                if n < len(items):
                    kind, t, b, q, keys, halves, _ = att_args(layer, n)
                    g, w, c = g0 + n, P * len(halves), sink_col(kind, t)
                    key = ("score", layer, n, 0)
                    st = stat[:, g % 2]
                    full(v, key)
                    full(v, ("score", layer, n, 1))
                    b0 = BANK[key][0]
                    v.tensor_reduce(st[:, 0, :], banks[:, b0:b0 + 2, 0:w], AX,
                                    ALU.max).then_inc(S("row_max"), 1)
                    v.wait_ge(S("row_max"), g + 1)
                    v.scalar_tensor_tensor(out=st[:, 1, :], in0=st[:, 0, :], scalar=-0.125, in1=nsinks[:, c, :],
                                           op0=ALU.mult, op1=ALU.min).then_inc(S("neg_max"), 1)
                    v.wait_ge(S("neg_max"), g + 1)
                    v.tensor_tensor(st[:, 2, :], st[:, 1, :], sinks[:, c, :], ALU.add).then_inc(S("sink_arg"), 1)
                if 1 <= n <= len(items):
                    dve_prob_norm(v, layer, n - 1)
                if n >= 3 and (n - 3) % NC == NC - 1:
                    dve_value(v, layer, (n - 3) // NC)
                if layer == 1 and 1 <= n <= 24:
                    key = ("ada_turn", n - 1)
                    full(v, key)
                    v.tensor_tensor(mod[:, 2 * n - 2:2 * n], bank(key)[:, 0:2], mod[:, 2 * n - 2:2 * n], ALU.add)\
                        .then_inc(reads(key), 1)

        def dve_prob_norm(v, layer, m):
            kind, t, b, q, keys, halves, _ = att_args(layer, m)
            g, w = ATT0 * layer + m, P * len(halves)
            st = stat[:, g % 2]
            v.wait_ge(S("exps"), g + 1)
            for s_ in range(2):
                taken(v, ("score", layer, m, s_))
            v.tensor_tensor(st[:, 3, :], st[:, 3, :], st[:, 4, :], ALU.add).then_inc(S("denominator"), 1)
            v.wait_ge(S("denominator"), g + 1)
            v.reciprocal(st[:, 4, :], st[:, 3, :]).then_inc(S("inverse"), 1)
            v.wait_ge(S("inverse"), g + 1)
            for s_ in range(2):
                v.tensor_scalar(pr[:, g % 3, s_, 0:w], pr[:, g % 3, s_, 0:w], st[:, 4, s_:s_ + 1], None,
                                ALU.mult).then_inc(S("prob_normed"), 1)

        def dve_value(v, layer, j):
            key = ("value", layer, j)
            tile = att_args(layer, NC * j)[-1]
            v.wait_ge(S("value_hi"), V0 * layer + j + 1)
            v.tensor_tensor(hn_lo[:, tile, :], bank(key)[:, :], hn_hi[:, tile, :].bitcast(F32),
                            ALU.subtract).then_inc(reads(key), 1)

        def act_attention(a, layer):
            items = attention_items(layer)
            g0 = ATT0 * layer
            for n in range(len(items) + 3):
                if n < len(items):
                    kind, t, b, q, keys, halves, _ = att_args(layer, n)
                    g, w = g0 + n, P * len(halves)
                    st = stat[:, g % 2]
                    a.wait_ge(S("sink_arg"), g + 1)
                    a.activation(st[:, 4, :], st[:, 2, :], ACT.Exp).then_inc(S("exps"), 1)
                    if g >= 3:
                        m = n - 3 if n >= 3 else len(attention_items(layer - 1)) + n - 3
                        full(a, ("turn", layer if n >= 3 else layer - 1, m))
                    for s_ in range(2):
                        a.activation(pr[:, g % 3, s_, 0:w], bank(("score", layer, n, s_))[:, 0:w], ACT.Exp,
                                     bias=st[:, 1, s_:s_ + 1], scale=0.125, accum_out=st[:, 3, s_:s_ + 1])\
                            .then_inc(reads(("score", layer, n, s_)), 1)
                if 2 <= n < len(items) + 2:
                    m = n - 2
                    w = P * len(att_args(layer, m)[5])
                    key = ("turn", layer, m)
                    full(a, key)
                    a.activation(pt[:, (g0 + m) % 2, 0:2 * w], bank(key)[:, 0:2 * w], ACT.Copy)\
                        .then_inc(reads(key), 1)
                if n >= 3 and (n - 3) % NC == NC - 1:
                    act_value(a, layer, (n - 3) // NC)
                if layer == 1 and n < 24:
                    key = ("unit", U["ada", n], 0)
                    full(a, key)
                    if n >= 2:
                        full(a, ("ada_turn", n - 2))
                    a.activation(arow[:, n % 2, :], bank(key)[0:2, 0:256], ACT.Copy).then_inc(reads(key), 1)
                    prep_hi(a, U["ada", n])

        def act_value(a, layer, j):
            key = ("value", layer, j)
            full(a, key)
            tile = att_args(layer, NC * j)[-1]
            a.activation(hn_hi[:, tile, :], bank(key)[:, :], ACT.Copy).then_inc(S("value_hi"), 1)

        QK = 2 * HG

        def row_of(j):
            return j if j < HG else 32 + j - HG

        def chunked(ap):
            return ap.rearrange("p (c t) -> p c t", c=NC)

        def dve_gates(v):
            key = ("unit", U["ba", 0], 0)
            lo, hi = slice(0, HG), slice(32, 32 + HG)
            v.wait_ge(S("bg_zero"), 1)
            v.wait_ge(S("neg_b_exp"), 1)
            v.tensor_scalar(bt[lo, 0, :], bt[lo, 0, :], 1.0, None, ALU.add).then_inc(S("gates"), 1)
            v.wait_ge(S("gates"), 1)
            v.reciprocal(bg[lo, :], bt[lo, 0, :]).then_inc(S("gates"), 1)
            full(v, key)
            v.tensor_scalar(bt[hi, 1, :], bank(key)[hi, :], gcst[hi, 0:1], None, ALU.add).then_inc(reads(key), 1)
            v.wait_ge(S("softplus_ln"), 4)
            taken(v, key)
            v.scalar_tensor_tensor(out=bt[hi, 1, :], in0=bt[hi, 1, :], scalar=0.0, in1=bt[hi, 2, :],
                                   op0=ALU.max, op1=ALU.add).then_inc(S("gates"), 1)
            v.wait_ge(S("gates"), 3)
            v.tensor_scalar(bt[hi, 1, :], bt[hi, 1, :], gcst[hi, 1:2], -1.0, ALU.mult, ALU.mult)\
                .then_inc(S("gates"), 1)
            v.wait_ge(S("gates"), 4)
            v.tensor_tensor_scan(bg[hi, :], reset[hi, :], bt[hi, 1, :], 0.0, ALU.mult, ALU.add)\
                .then_inc(S("gates"), 1)
            full(v, ("cols",))
            v.tensor_copy(cols[:, :, :], bank(("cols",))[:, 0:256].rearrange("p (c h) -> p c h", c=NC))\
                .then_inc(reads(("cols",)), 1)
            taken(v, ("cols",))
            v.wait_ge(S("exp_gc"), 1)
            v.scalar_tensor_tensor(out=nbe[:, :, :], in0=nbe[:, :, :], scalar=-1.0, in1=cols[:, :, 0:HG],
                                   op0=ALU.mult, op1=ALU.mult).then_inc(S("gates"), 1)

        def act_gates(a):
            key = ("unit", U["ba", 0], 0)
            lo, hi = slice(0, HG), slice(32, 32 + HG)
            full(a, key)
            a.activation(bt[lo, 0, :], bank(key)[lo, :], ACT.Exp, scale=-1.0).then_inc(S("neg_b_exp"), 1)
            prep_hi(a, U["ba", 0])
            a.activation(gcst[hi, 1:2], gcst[hi, 1:2], ACT.Exp).then_inc(S("softplus_ln"), 1)
            taken(a, key)
            a.activation(bt[hi, 2, :], bt[hi, 1, :], ACT.Abs).then_inc(S("softplus_ln"), 1)
            a.wait_ge(S("softplus_ln"), 2)
            a.activation(bt[hi, 2, :], bt[hi, 2, :], ACT.Exp, scale=-1.0).then_inc(S("softplus_ln"), 1)
            a.wait_ge(S("softplus_ln"), 3)
            a.activation(bt[hi, 2, :], bt[hi, 2, :], ACT.Ln, bias=1.0).then_inc(S("softplus_ln"), 1)
            taken(a, ("cols",))
            a.activation(nbe[:, :, :], cols[:, :, 32:32 + HG], ACT.Exp).then_inc(S("exp_gc"), 1)

        def pe_gate_cols(pe):
            pe.wait_ge(S("gates"), 5)
            open_bank(pe, ("cols",))
            for c in range(NC):
                mm = pe.transpose(bank(("cols",))[:, c * 64:(c + 1) * 64], bg[:, c * P:(c + 1) * P],
                                  ident[0:64, 0:64])
            mm.then_inc(fills(("cols",)), 1)

        def act_qkv(a):
            for i in range(9):
                u = U["qkv", i]
                for t in range(2):
                    j, key = 2 * i + t, ("unit", u, t)
                    full(a, key)
                    a.activation(qkv[:, j, :], bank(key)[:, :], ACT.Copy, scale=cw[:, j, 3:4])\
                        .then_inc(S("tap_last"), 1)
                prep_hi(a, u)
                for t in range(2):
                    j, key = 2 * i + t, ("unit", u, t)
                    taken(a, key)
                    a.activation(qkv[:, j, :], qkv[:, j, :], ACT.Silu).then_inc(S("conv_silu"), 1)
                for t in range(2):
                    j = 2 * i + t
                    if j < QK:
                        a.wait_ge(S("conv_silu"), j + 1)
                        if j >= 2:
                            a.wait_ge(S("l2_summed"), j - 1)
                        a.activation(sq[:, t, :], qkv[:, j, :], ACT.Square).then_inc(S("qk_squared"), 1)

        def dve_qkv(v):
            for i in range(9):
                for t in range(2):
                    j, key = 2 * i + t, ("unit", U["qkv", i], t)
                    v.wait_ge(S("tap_last"), j + 1)
                    for d in (1, 2, 3):
                        if d > 1:
                            v.wait_ge(S("taps"), 2 * j + d - 1)
                        ins = v.scalar_tensor_tensor(
                            out=qkv[:, j, d:T], in0=bank(key)[:, 0:T - d], scalar=cw[:, j, 3 - d:4 - d],
                            in1=qkv[:, j, d:T], op0=ALU.mult, op1=ALU.add)
                        ins.then_inc(S("taps") if d < 3 else reads(key), 1)

        def pe_l2(pe, j):
            if j == 0:
                open_bank(pe, ("l2",))
            pe.wait_ge(S("qk_squared"), j + 1)
            r = row_of(j)
            pe.matmul(bank(("l2",))[0:64, :], col1[:, 63 - r:127 - r], sq[:, j % 2, :], start=(j == 0),
                      stop=(j == QK - 1), skip_group_check=True)\
                .then_inc(S("l2_summed") if j < QK - 1 else fills(("l2",)), 1)

        def pe_gdn_in(pe):
            pe_linear(pe, "ba", ready=hn_ready(pe, 1))
            unit_jobs(pe, U["qkv", 0], 0, *hn_of, KT)
            pe_gate_cols(pe)
            for i in range(1, 9):
                unit_jobs(pe, U["qkv", i], 0, *hn_of, KT)
                for j in (2 * i - 2, 2 * i - 1):
                    if j < QK:
                        pe_l2(pe, j)
            over_units(pe, "z", lambda u, i: unit_jobs(pe, u, i, *hn_of, KT))
            over_units(pe, "memq", lambda u, i: unit_jobs(pe, u, i, *hn_of, KT))

        def act_z(a):
            def body(u, i):
                j = 2 * (u - U["z", 0])
                for t in range(2):
                    b, n = BANK["unit", u, t]
                    a.wait_ge(bank_full[b], i + (n + 1))
                    a.activation(zs[:, i * 4 + (j + t), :], psum[b][:, :], ACT.Silu).then_inc(bank_read[b], 1)
                prep_hi(a, u, i)
            over_units(a, "z", body)
            over_units(a, "memq", lambda u, i: prep_hi(a, u, i))
            full(a, ("l2",))
            a.activation(rows[:, :], bank(("l2",))[0:64, :], ACT.Sqrt, bias=eps[0:64, 0:1])\
                .then_inc(reads(("l2",)), 1)

        def dve_memq(v, src):
            for t in range(2):
                key = ("unit", src, t)
                full(v, key)
                v.tensor_copy(mem_q[:, t, :], bank(key)[:, :]).then_inc(reads(key), 1)

        def pe_heads(pe):
            pe.wait_ge(S("rows_inverse"), 1)
            for j in range(QK):
                key = ("l2b", j)
                open_bank(pe, key)
                pe.matmul(bank(key)[:, :], sel[:, j, :], rows[:, :], start=True, stop=True).then_inc(fills(key), 1)
            for h in range(HG):
                key = ("gm", h)
                open_bank(pe, key)
                pe.matmul(bank(key)[:, :], sel[:, HG + h, :], bg[:, :], start=True, stop=False)
                pe.matmul(bank(key)[:, :], identb[:, :], mask4[:, :], start=False, stop=True).then_inc(fills(key), 1)
                key = ("gp", h)
                open_bank(pe, key)
                pe.matmul(bank(key)[:, :], sel[:, HG + h, :], bg[:, :], start=True, stop=True)\
                    .then_inc(fills(key), 1)
                key = ("bb", h)
                open_bank(pe, key)
                pe.matmul(bank(key)[:, :], sel[:, h, :], bg[:, :], start=True, stop=True).then_inc(fills(key), 1)
                key = ("kk", h)
                open_bank(pe, key)
                taken(pe, ("bb", h))
                for c in range(NC):
                    cc = slice(c * P, (c + 1) * P)
                    mm = pe.matmul(bank(key)[:, cc], qkv[:, HG + h, cc], kb[:, h % 2, cc], start=True, stop=True)
                mm.then_inc(fills(key), 1)
                key = ("qk", h)
                open_bank(pe, key)
                taken(pe, ("l2b", h))
                for c in range(NC):
                    cc = slice(c * P, (c + 1) * P)
                    mm = pe.matmul(bank(key)[:, cc], qkv[:, HG + h, cc], qkv[:, h, cc], start=True, stop=True)
                mm.then_inc(fills(key), 1)

        def act_heads(a):
            for h in range(HG):
                taken(a, ("gm", h))
                a.activation(dec[:, h % 2, :], dec[:, h % 2, :], ACT.Exp).then_inc(S("decay"), 1)
                a.wait_ge(S("glast_diff"), h + 1)
                key = ("gp", h)
                full(a, key)
                a.activation(elast[:, h, :], elast[:, h, :], ACT.Exp).then_inc(S("elast"), 1)
                if h >= 2:
                    a.wait_ge(S("q_decayed"), h - 1)
                a.activation(eg[:, h % 2, :], bank(key)[:, :], ACT.Exp).then_inc(reads(key), 1)
                taken(a, key)
                a.activation(glast[:, h, :], chunked(eg[:, h % 2, :])[:, :, P - 1], ACT.Copy)\
                    .then_inc(S("glast"), 1)

        def dve_heads(v):
            taken(v, ("l2",))
            v.reciprocal(rows[:, :], rows[:, :]).then_inc(S("rows_inverse"), 1)
            for j in range(QK):
                key = ("l2b", j)
                full(v, key)
                v.scalar_tensor_tensor(out=qkv[:, j, :], in0=qkv[:, j, :], scalar=P ** -0.5 if j < HG else 1.0,
                                       in1=bank(key)[:, :], op0=ALU.mult, op1=ALU.mult).then_inc(reads(key), 1)
            for h in range(HG):
                key = ("gm", h)
                full(v, key)
                gcol = cols[:, :, 32 + h:33 + h]
                v.tensor_tensor(chunked(dec[:, h % 2, :]), chunked(bank(key)[:, :]), gcol.broadcast_to([P, NC, P]),
                                ALU.subtract).then_inc(reads(key), 1)
                key = ("gp", h)
                full(v, key)
                v.tensor_tensor(elast[:, h, :], chunked(bank(key)[:, :])[:, :, P - 1], cols[:, :, 32 + h],
                                ALU.subtract).then_inc(S("glast_diff"), 1)
                key = ("bb", h)
                full(v, key)
                taken(v, ("l2b", HG + h))
                v.tensor_tensor(kb[:, h % 2, :], qkv[:, HG + h, :], bank(key)[:, :], ALU.mult)\
                    .then_inc(reads(key), 1)
                key = ("kk", h)
                full(v, key)
                v.wait_ge(S("decay"), h + 1)
                v.tensor_tensor(lt[:, h, :], bank(key)[:, :], dec[:, h % 2, :], ALU.mult).then_inc(reads(key), 1)
                taken(v, key)
                v.tensor_tensor(chunked(lt[:, h, :]), chunked(lt[:, h, :]),
                                strict[:, None, :].broadcast_to([P, NC, P]), ALU.mult).then_inc(S("lt"), 1)
                key = ("qk", h)
                full(v, key)
                v.tensor_tensor(at[:, h, :], bank(key)[:, :], dec[:, h % 2, :], ALU.mult).then_inc(reads(key), 1)
                taken(v, ("gp", h))
                v.tensor_tensor(qkv[:, h, :], qkv[:, h, :], eg[:, h % 2, :], ALU.mult).then_inc(S("q_decayed"), 1)

        def pe_inverse(pe):
            for lv in range(7):
                for h in range(HG):
                    key = ("iz", lv, h)
                    open_bank(pe, key)
                    if lv:
                        taken(pe, ("iw", lv - 1, h))
                    else:
                        pe.wait_ge(S("lt"), h + 1)
                    for c in range(NC):
                        cc = slice(c * P, (c + 1) * P)
                        mm = pe.matmul(bank(key)[:, cc], lt[:, h, cc], xi[:, h, cc] if lv else ident[:, :],
                                       start=True, stop=True)
                    mm.then_inc(fills(key), 1)
                for h in range(HG):
                    taken(pe, ("iz", lv, h))
                    if lv:
                        taken(pe, ("iv", lv - 1, h))
                    for x_ in ("iw", "iv"):
                        key = (x_, lv, h)
                        if key not in BANK:
                            continue
                        open_bank(pe, key)
                        for c in range(NC):
                            cc = slice(c * P, (c + 1) * P)
                            xtc = xt[:, h, cc] if lv else ident[:, :]
                            z_ = zm[:, h, cc]
                            lhs, rhs = (xtc, z_) if x_ == "iw" else (z_, xtc)
                            mm = pe.matmul(bank(key)[:, cc], lhs, rhs, start=True, stop=True)
                        mm.then_inc(fills(key), 1)

        def dve_inverse(v):
            iall = ident[:, None, :].broadcast_to([P, NC, P])
            v.wait_ge(S("glast"), HG)
            v.wait_ge(S("q_decayed"), HG)
            taken(v, ("qk", HG - 1))
            for lv in range(7):
                for h in range(HG):
                    key = ("iz", lv, h)
                    full(v, key)
                    v.tensor_tensor(chunked(zm[:, h, :]), chunked(bank(key)[:, :]),
                                    levels[:, lv:lv + 1, :].broadcast_to([P, NC, P]), ALU.mult)\
                        .then_inc(reads(key), 1)
                for h in range(HG):
                    for x_, what in (("iw", xi), ("iv", xt)):
                        key = (x_, lv, h)
                        if key not in BANK:
                            continue
                        full(v, key)
                        old = chunked(what[:, h, :]) if lv else iall
                        v.tensor_tensor(chunked(what[:, h, :]), old, chunked(bank(key)[:, :]), ALU.subtract)\
                            .then_inc(reads(key), 1)

        def pe_turned(pe):
            for h in range(HG):
                for name, j in (("vt", 2 * HG + h), ("kt", HG + h)):
                    key = (name, h)
                    open_bank(pe, key)
                    for c in range(NC):
                        cc = slice(c * P, (c + 1) * P)
                        mm = pe.transpose(bank(key)[:, cc], qkv[:, j, cc], ident[:, :])
                    mm.then_inc(fills(key), 1)

        def dve_turned(v):
            for h in range(HG):
                key = ("vt", h)
                full(v, key)
                v.tensor_tensor(chunked(qkv[:, 2 * HG + h, :]), chunked(bank(key)[:, :]),
                                cols[:, :, h:h + 1].broadcast_to([P, NC, P]), ALU.mult).then_inc(reads(key), 1)
                key = ("kt", h)
                full(v, key)
                v.wait_ge(S("elast"), h + 1)
                v.tensor_tensor(chunked(lt[:, h, :]), chunked(bank(key)[:, :]),
                                elast[:, h, :, None].broadcast_to([P, NC, P]), ALU.mult).then_inc(reads(key), 1)

        def pe_recurrence(pe):
            for c in range(NC):
                cc = slice(c * P, (c + 1) * P)
                if c:
                    for h in range(HG):
                        key = ("ks", c, h)
                        open_bank(pe, key)
                        taken(pe, ("su", c - 1, h))
                        pe.matmul(bank(key)[:, 0:P], qkv[:, HG + h, cc], state[:, h, :], start=True, stop=True)\
                            .then_inc(fills(key), 1)
                for h in range(HG):
                    key = ("vn", c, h)
                    open_bank(pe, key)
                    if c:
                        taken(pe, ("ks", c, h))
                        right = rr[:, h, :]
                    else:
                        taken(pe, ("vt", h))
                        taken(pe, ("iv", 6, h))
                        right = qkv[:, 2 * HG + h, 0:P]
                    pe.matmul(bank(key)[:, 0:P], xt[:, h, cc], right, start=True, stop=True).then_inc(fills(key), 1)
                for h in range(HG):
                    key = ("oo", c, h)
                    open_bank(pe, key)
                    taken(pe, ("vn", c, h))
                    if c:
                        pe.matmul(bank(key)[:, 0:P], state[:, h, :], qkv[:, h, cc], start=True, stop=False)
                    else:
                        pe.wait_ge(S("q_decayed"), h + 1)
                    pe.matmul(bank(key)[:, 0:P], vn[:, h, :], at[:, h, cc], start=(c == 0), stop=True)\
                        .then_inc(fills(key), 1)
                    if c < NC - 1:
                        key = ("su", c, h)
                        open_bank(pe, key)
                        taken(pe, ("kt", h))
                        pe.matmul(bank(key)[:, 0:P], lt[:, h, cc], vn[:, h, :], start=True, stop=True)\
                            .then_inc(fills(key), 1)

        def dve_recurrence(v):
            for c in range(NC):
                cc = slice(c * P, (c + 1) * P)
                if c:
                    for h in range(HG):
                        key = ("ks", c, h)
                        full(v, key)
                        v.scalar_tensor_tensor(out=rr[:, h, :], in0=bank(key)[:, 0:P], scalar=nbe[:, c, h:h + 1],
                                               in1=qkv[:, 2 * HG + h, cc], op0=ALU.mult, op1=ALU.add)\
                            .then_inc(reads(key), 1)
                if c < NC - 1:
                    for h in range(HG):
                        key = ("su", c, h)
                        full(v, key)
                        if c:
                            v.wait_ge(S("glast"), h + 1)
                            v.scalar_tensor_tensor(out=state[:, h, :], in0=state[:, h, :],
                                                   scalar=glast[:, h, c:c + 1], in1=bank(key)[:, 0:P],
                                                   op0=ALU.mult, op1=ALU.add).then_inc(reads(key), 1)
                        else:
                            v.tensor_copy(state[:, h, :], bank(key)[:, 0:P]).then_inc(reads(key), 1)

        def act_recurrence(a):
            for c in range(NC):
                cc = slice(c * P, (c + 1) * P)
                for h in range(HG):
                    key = ("vn", c, h)
                    full(a, key)
                    a.activation(vn[:, h, :], bank(key)[:, 0:P], ACT.Copy).then_inc(reads(key), 1)
                for h in range(HG):
                    key = ("oo", c, h)
                    full(a, key)
                    a.activation(qkv[:, h, cc], bank(key)[:, 0:P], ACT.Copy).then_inc(reads(key), 1)
            for h in range(HG):
                taken(a, ("oo", NC - 1, h))
                if h:
                    a.wait_ge(S("o_summed"), h)
                a.activation(osq[:, :], qkv[:, h, :], ACT.Square).then_inc(S("o_squared"), 1)
            full(a, ("onorm",))
            a.activation(rows[:, :], bank(("onorm",))[0:64, :], ACT.Sqrt, bias=eps[0:64, 0:1], scale=1.0 / P)\
                .then_inc(reads(("onorm",)), 1)
            for h in range(HG):
                a.wait_ge(S("o_gated"), h + 1)
                a.activation(hn_hi[:, h, :], tmp[:, h, :], ACT.Copy).then_inc(S("mix_hi"), 1)

        def pe_onorm(pe):
            open_bank(pe, ("onorm",))
            for h in range(HG):
                pe.wait_ge(S("o_squared"), h + 1)
                pe.matmul(bank(("onorm",))[0:64, :], col1[:, 63 - h:127 - h], osq[:, :], start=(h == 0),
                          stop=(h == HG - 1), skip_group_check=True)\
                    .then_inc(S("o_summed") if h < HG - 1 else fills(("onorm",)), 1)
            pe.wait_ge(S("rows_inverse"), 2)
            for h in range(HG):
                key = ("ob", h)
                open_bank(pe, key)
                pe.matmul(bank(key)[:, :], sel[:, h, :], rows[:, :], start=True, stop=True).then_inc(fills(key), 1)

        def dve_onorm(v):
            taken(v, ("onorm",))
            v.reciprocal(rows[:, :], rows[:, :]).then_inc(S("rows_inverse"), 1)
            for h in range(HG + 1):
                if h < HG:
                    key = ("ob", h)
                    full(v, key)
                    v.scalar_tensor_tensor(out=tmp[:, h, :], in0=qkv[:, h, :], scalar=gng[:, 0:1],
                                           in1=bank(key)[:, :], op0=ALU.mult, op1=ALU.mult)\
                        .then_inc(reads(key), 1)
                    taken(v, key)
                    v.tensor_tensor(tmp[:, h, :], tmp[:, h, :], zs[:, h, :], ALU.mult).then_inc(S("o_gated"), 1)
                if h:
                    v.wait_ge(S("mix_hi"), h)
                    v.tensor_tensor(hn_lo[:, h - 1, :], tmp[:, h - 1, :], hn_hi[:, h - 1, :].bitcast(F32),
                                    ALU.subtract).then_inc(S("mix_lo"), 1)

        def rope_tables_dve(v):
            def step(ins):
                ins.then_inc(S("angle"), 1)
                count["angle"] += 1
                v.wait_ge(S("angle"), count["angle"])
            count = {"angle": 0}
            v.wait_ge(S("land_rope"), 16 * ROPE_LOADS)
            a0, kk_, r, _ = (ang[:, m, :] for m in range(4))
            step(v.tensor_copy(a0, posi[:, :]))
            step(v.tensor_scalar(a0, a0, rcol[:, 0:1], None, ALU.mult))
            for quarter, dst in ((0.0, sinv), (0.25, cosv)):
                step(v.tensor_scalar(kk_, a0, 1 / (2 * math.pi), quarter, ALU.mult, ALU.add))
                step(v.tensor_scalar(kk_, kk_, ROUND, ROUND, ALU.add, ALU.subtract))
                step(v.scalar_tensor_tensor(out=r, in0=kk_, scalar=-PI2[0], in1=a0, op0=ALU.mult, op1=ALU.add))
                step(v.scalar_tensor_tensor(out=r, in0=kk_, scalar=-PI2[1], in1=r, op0=ALU.mult, op1=ALU.add))
                step(v.scalar_tensor_tensor(out=r, in0=kk_, scalar=-PI2[2], in1=r, op0=ALU.mult, op1=ALU.add))
                step(v.tensor_scalar(r, r, quarter * 2 * math.pi, PI_IN, ALU.add, ALU.min))
                step(v.tensor_scalar(dst[:, :], r, -PI_IN, None, ALU.max))
            v.wait_ge(S("sines"), 2)
            step(v.tensor_scalar(sinv[:, :], sinv[:, :], rcol[:, 1:2], None, ALU.mult))

        def rope_tables_act(a):
            a.wait_ge(S("angle"), 16)
            a.activation(sinv[:, :], sinv[:, :], ACT.Sin).then_inc(S("sines"), 1)
            a.activation(cosv[:, :], cosv[:, :], ACT.Sin).then_inc(S("sines"), 1)

        def pe_kv(pe):
            u = U["kv", 0]
            pe.wait_ge(S("w_lo"), u + 1)
            hi, lo = W3(w_hi, u % 2), W3(w_lo, u % 2)
            key = ("unit", u, 0)
            open_bank(pe, key)
            for k in range(KT):
                hn_ready(pe, 3)(k)
                pe.matmul(bank(key)[:, :], hi[:, k, 0:P], hn_hi[:, k, :], start=(k == 0), stop=False)
                pe.matmul(bank(key)[:, :], hi[:, k, 0:P], hn_lo[:, k, :], start=False, stop=False)
                mm = pe.matmul(bank(key)[:, :], lo[:, k, 0:P], hn_hi[:, k, :], start=False, stop=(k == KT - 1))
            mm.then_inc(fills(key), 1)
            key = ("unit", u, 1)
            open_bank(pe, key)
            for b in range(NC):
                bb = slice(b * P, (b + 1) * P)
                for k in range(KT):
                    pe.matmul(bank(key)[:, bb], hn_hi[:, k, bb], hi[:, k, P:2 * P], start=(k == 0), stop=False)
                    pe.matmul(bank(key)[:, bb], hn_hi[:, k, bb], lo[:, k, P:2 * P], start=False, stop=False)
                    mm = pe.matmul(bank(key)[:, bb], hn_lo[:, k, bb], hi[:, k, P:2 * P], start=False,
                                   stop=(k == KT - 1))
            mm.then_inc(fills(key), 1)

        def dve_kv(v):
            u = U["kv", 0]
            full(v, ("unit", u, 0))
            v.tensor_copy(qraw[:, 6, :], bank(("unit", u, 0))[:, :]).then_inc(reads(("unit", u, 0)), 1)
            full(v, ("unit", u, 1))
            v.tensor_copy(vs[:, :, :], chunked(bank(("unit", u, 1))[:, :])).then_inc(reads(("unit", u, 1)), 1)

        def pe_rope(pe, j):
            key = ("rope", j)
            open_bank(pe, key)
            taken(pe, ("unit", U["kv", 0], 0) if j == 6 else ("unit", U["swaq", j // 2], j % 2))
            pe.matmul(bank(key)[:, :], perm[:, :], qraw[:, j, :], start=True, stop=True).then_inc(fills(key), 1)

        def dve_rope(v, j):
            key = ("rope", j)
            n = (j + 1) % 7
            dst = kr if j == 6 else qr[:, j, :]
            v.tensor_tensor(dst[:, :], qraw[:, j, :], cosv[:, :], ALU.mult).then_inc(S("rope_cos"), 1)
            full(v, key)
            v.wait_ge(S("rope_cos"), n + 1)
            v.tensor_tensor(qraw[:, j, :], bank(key)[:, :], sinv[:, :], ALU.mult).then_inc(reads(key), 1)
            taken(v, key)
            v.tensor_tensor(dst[:, :], dst[:, :], qraw[:, j, :], ALU.add).then_inc(S("roped"), 1)

        def act_round2(a, idx):
            for k in range(KT):
                a.wait_ge(S("shifted"), KT * idx + k + 1)
                a.activation(hn_hi[:, k, :], tmp[:, k, :], ACT.Copy).then_inc(S("ada_hi"), 1)

        def dve_ada_norm(v, i, idx):
            def low(k):
                v.wait_ge(S("ada_hi"), KT * idx + k + 1)
                v.tensor_tensor(hn_lo[:, k, :], tmp[:, k, :], hn_hi[:, k, :].bitcast(F32),
                                ALU.subtract).then_inc(S("ada_lo"), 1)
            for k in range(KT):
                v.scalar_tensor_tensor(out=tmp[:, k, :], in0=x[:, k, :], scalar=gain2[:, 2 * idx, k:k + 1],
                                       in1=rs[:, :], op0=ALU.mult, op1=ALU.mult).then_inc(S("scaled"), 1)
                v.wait_ge(S("scaled"), KT * idx + k + 1)
                c = 24 * idx + k
                v.tensor_scalar(tmp[:, k, :], tmp[:, k, :], mod[:, c:c + 1], None, ALU.add)\
                    .then_inc(S("shifted"), 1)
                if k:
                    low(k - 1)
            low(KT - 1)

        def ada_ready(pe, idx):
            return lambda k: pe.wait_ge(S("ada_lo"), KT * idx + k + 1)

        def dve_modulation(v):
            taken(v, ("ada_turn", 23))
            for m, c in ((0, 8), (2, 32)):
                v.scalar_tensor_tensor(out=gain2[:, m, :], in0=mod[:, c:c + 8], scalar=1.0, in1=gain2[:, m, :],
                                       op0=ALU.add, op1=ALU.mult).then_inc(S("modulated"), 1)
            for m, c in ((1, 16), (3, 40)):
                v.tensor_tensor(gain2[:, m, :], gain2[:, m, :], mod[:, c:c + 8], ALU.mult)\
                    .then_inc(S("modulated"), 1)
            v.wait_ge(S("modulated"), 4)

        def dve_post(v, i):
            taken(v, ("post", i))
            v.reciprocal(rs[:, :], rs[:, :]).then_inc(S("post_rstd"), 1)
            v.wait_ge(S("post_rstd"), i + 1)
            for k in range(KT):
                v.scalar_tensor_tensor(out=tmp[:, k, :], in0=tmp[:, k, :], scalar=gain2[:, 1 + 2 * i, k:k + 1],
                                       in1=rs[:, :], op0=ALU.mult, op1=ALU.mult).then_inc(S("post_scaled"), 1)
                v.wait_ge(S("post_scaled"), KT * i + k + 1)
                v.tensor_tensor(x[:, k, :], x[:, k, :], tmp[:, k, :], ALU.add).then_inc(S("post_added"), 1)

        HB = slice(96, 128)
        IK = slice(0, 64)

        def act_small(a):
            prep_hi(a, U["qlat", 0])
            for t in range(2):
                taken(a, ("unit", U["qlat", 0], t))
                a.activation(tmp[:, 2 + t, :], tmp[:, t, :], ACT.Square).then_inc(S("latent_sq"), 1)
            prep_hi(a, U["misc", 0])
            taken(a, ("unit", U["misc", 0], 0))
            a.activation(tmp[:, 4, :], kvf[:, :], ACT.Square).then_inc(S("latent_sq"), 1)
            taken(a, ("unit", U["misc", 0], 1))
            a.activation(tmp[IK, 5, :], r1[IK, :], ACT.Square).then_inc(S("latent_sq"), 1)

        def act_small_late(a):
            for name, dst, n in (("qn", rs[:, :], 256), ("kvn", tmp[:, 6, :], 128), ("kin", tmp[IK, 7, :], 64)):
                full(a, (name,))
                m = dst.shape[0]
                a.activation(dst, bank((name,))[0:m, :], ACT.Sqrt, bias=eps[0:m, 0:1], scale=1.0 / n)\
                    .then_inc(reads((name,)), 1)
            a.wait_ge(S("dt_arg"), 1)
            a.activation(small2[HB, 5:6], small2[HB, 5:6], ACT.Exp).then_inc(S("dt_exp"), 1)
            a.activation(tmp[HB, 2, :], r1[HB, :], ACT.Abs).then_inc(S("dt_exp"), 1)
            a.wait_ge(S("dt_exp"), 2)
            a.activation(tmp[HB, 2, :], tmp[HB, 2, :], ACT.Exp, scale=-1.0).then_inc(S("dt_exp"), 1)
            a.wait_ge(S("dt_exp"), 3)
            a.activation(tmp[HB, 2, :], tmp[HB, 2, :], ACT.Ln, bias=1.0).then_inc(S("dt_exp"), 1)
            for t in range(2):
                a.wait_ge(S("qn_scaled"), t + 1)
                a.activation(qn_hi[:, t, :], tmp[:, t, :], ACT.Copy).then_inc(S("qn_hi"), 1)
            a.dma_start(tmp[:, 4, :].bitcast(I32), I["posi2"]).then_inc(S("land_pos"), 16)

        def act_decays(a):
            a.wait_ge(S("last_diff"), 1)
            a.activation(tolast[:, :, :], tolast[:, :, :], ACT.Exp).then_inc(S("chunk_decays"), 1)
            a.activation(cdall[:, :, :], bank(("cl",))[:, 0:P].rearrange("p (h c) -> p h c", c=NC), ACT.Exp)\
                .then_inc(reads(("cl",)), 1)

        def dve_small(v):
            for t in range(2):
                key = ("unit", U["qlat", 0], t)
                full(v, key)
                v.tensor_copy(tmp[:, t, :], bank(key)[:, :]).then_inc(reads(key), 1)
            for t, dst in ((0, kvf), (1, r1)):
                key = ("unit", U["misc", 0], t)
                full(v, key)
                v.tensor_copy(dst[:, :], bank(key)[:, :]).then_inc(reads(key), 1)
            taken(v, key)
            v.wait_ge(S("land_second"), 16 * len(SECOND))
            v.wait_ge(S("latent_sq"), 4)
            v.tensor_scalar(r1[HB, :], r1[HB, :], small2[HB, 4:5], None, ALU.add).then_inc(S("dt_arg"), 1)
            for n, (name, dst) in enumerate((("qn", rs[:, :]), ("kvn", tmp[:, 6, :]), ("kin", tmp[IK, 7, :]))):
                taken(v, (name,))
                v.reciprocal(dst, dst).then_inc(S("latent_rstd"), 1)
            v.wait_ge(S("latent_rstd"), 3)
            for t in range(2):
                v.scalar_tensor_tensor(out=tmp[:, t, :], in0=tmp[:, t, :], scalar=small2[:, t:t + 1], in1=rs[:, :],
                                       op0=ALU.mult, op1=ALU.mult).then_inc(S("qn_scaled"), 1)
            v.scalar_tensor_tensor(out=kvf[:, :], in0=kvf[:, :], scalar=small2[:, 2:3], in1=tmp[:, 6, :],
                                   op0=ALU.mult, op1=ALU.mult).then_inc(S("keys_scaled"), 1)
            v.scalar_tensor_tensor(out=r1[IK, :], in0=r1[IK, :], scalar=small2[IK, 3:4], in1=tmp[IK, 7, :],
                                   op0=ALU.mult, op1=ALU.mult).then_inc(S("keys_scaled"), 1)
            for t in range(2):
                v.wait_ge(S("qn_hi"), t + 1)
                v.tensor_tensor(qn_lo[:, t, :], tmp[:, t, :], qn_hi[:, t, :].bitcast(F32), ALU.subtract)\
                    .then_inc(S("qn_lo"), 1)
            v.wait_ge(S("dt_exp"), 4)
            v.scalar_tensor_tensor(out=r1[HB, :], in0=r1[HB, :], scalar=0.0, in1=tmp[HB, 2, :],
                                   op0=ALU.max, op1=ALU.add).then_inc(S("dt"), 1)
            v.wait_ge(S("dt"), 1)
            v.tensor_scalar(tmp[HB, 3, :], r1[HB, :], small2[HB, 5:6], -1.0, ALU.mult, ALU.mult)\
                .then_inc(S("dt"), 1)
            v.memset(r2[:, :], 0.0).then_inc(S("dt"), 1)
            v.wait_ge(S("dt"), 3)
            v.tensor_tensor_scan(r2[HB, :], reset2[HB, :], tmp[HB, 3, :], 0.0, ALU.mult, ALU.add)\
                .then_inc(S("dt"), 1)
            v.wait_ge(S("dt"), 4)
            v.tensor_tensor(diag[HB, :, :], ident[HB, 96:128, None].broadcast_to([32, 32, NC]),
                            chunked(r2[HB, :])[:, None, :, P - 1].broadcast_to([32, 32, NC]), ALU.mult)\
                .then_inc(S("dt"), 1)
            v.tensor_copy(pick[HB, :], ident[HB, 96:128]).then_inc(S("r2_split"), 1)
            v.tensor_copy(r2_hi[HB, :], r2[HB, :]).then_inc(S("r2_split"), 1)
            v.wait_ge(S("r2_split"), 2)
            v.tensor_tensor(r2_lo[HB, :], r2[HB, :], r2_hi[HB, :].bitcast(F32), ALU.subtract)\
                .then_inc(S("r2_split"), 1)
            full(v, ("kid",))
            v.tensor_copy(ki[:, :], bank(("kid",))[:, :]).then_inc(reads(("kid",)), 1)
            full(v, ("kvt",))
            v.tensor_copy(kvt[:, :, :], chunked(bank(("kvt",))[:, :])).then_inc(reads(("kvt",)), 1)
            full(v, ("c1",))
            v.tensor_copy(c1[:, :, :], chunked(bank(("c1",))[:, :])).then_inc(reads(("c1",)), 1)
            full(v, ("c2",))
            v.tensor_copy(c2[:, :, :], chunked(bank(("c2",))[:, :])[:, :, 96:128]).then_inc(reads(("c2",)), 1)
            taken(v, ("c2",))
            full(v, ("cl",))
            v.tensor_tensor(tolast[:, :, :], bank(("cl",))[:, 0:P].rearrange("p (h c) -> p c h", c=NC), c2[:, :, :],
                            ALU.subtract).then_inc(S("last_diff"), 1)
            taken(v, ("c1",))
            v.tensor_scalar(wcol[:, :, :], c1[:, :, 64:80], 1.0 / 32, None, ALU.mult).then_inc(S("wcol"), 1)
            ipos = tmp[:, 4, :].bitcast(I32)
            v.wait_ge(S("land_pos"), 16)
            v.wait_ge(S("keys_scaled"), 2)
            v.tensor_copy(tmp[:, 7, :], ipos).then_inc(S("positions"), 1)
            v.tensor_copy(qpc[:, 0, :], qpi[:, :]).then_inc(S("positions"), 1)
            v.wait_ge(S("positions"), 2)
            v.tensor_scalar(ipos, ipos, 6, None, ALU.arith_shift_right).then_inc(S("positions"), 1)
            v.tensor_scalar(qpi[:, :], qpi[:, :], 6, None, ALU.arith_shift_right).then_inc(S("positions"), 1)
            v.wait_ge(S("positions"), 4)
            v.tensor_copy(tmp[:, 6, :], ipos).then_inc(S("positions"), 1)
            v.tensor_copy(qpc[:, 1, :], qpi[:, :]).then_inc(S("positions"), 1)
            v.wait_ge(S("positions"), 6)

        def pe_small(pe):
            pe.wait_ge(S("latent_sq"), 2)
            open_bank(pe, ("qn",))
            pe.matmul(bank(("qn",))[:, :], ones[:, :], tmp[:, 2, :], start=True, stop=False)
            pe.matmul(bank(("qn",))[:, :], ones[:, :], tmp[:, 3, :], start=False, stop=True)\
                .then_inc(fills(("qn",)), 1)
            pe.wait_ge(S("latent_sq"), 4)
            open_bank(pe, ("kvn",))
            pe.matmul(bank(("kvn",))[:, :], ones[:, :], tmp[:, 4, :], start=True, stop=True)\
                .then_inc(fills(("kvn",)), 1)
            open_bank(pe, ("kin",))
            pe.matmul(bank(("kin",))[0:64, :], ones[IK, 0:64], tmp[IK, 5, :], start=True, stop=True)\
                .then_inc(fills(("kin",)), 1)

        def pe_small_late(pe):
            pe.wait_ge(S("keys_scaled"), 2)
            key = ("kid",)
            open_bank(pe, key)
            for s_ in range(2):
                mm = pe.matmul(bank(key)[64 * s_:64 * s_ + 64, :], ident[IK, 0:64], r1[IK, :], start=True, stop=True)
            mm.then_inc(fills(key), 1)
            pe.wait_ge(S("dt"), 4)
            for name, src in (("kvt", kvf), ("c1", r1), ("c2", r2)):
                open_bank(pe, (name,))
                for c in range(NC):
                    cc = slice(c * P, (c + 1) * P)
                    mm = pe.transpose(bank((name,))[:, cc], src[:, cc], ident[:, :])
                mm.then_inc(fills((name,)), 1)
            pe.wait_ge(S("dt"), 5)
            open_bank(pe, ("cl",))
            pe.matmul(bank(("cl",))[:, 0:P], ones[HB, :], diag[HB, :, :], start=True, stop=True)\
                .then_inc(fills(("cl",)), 1)

        def spill_out(a, j, src):
            a.dma_start(spill[j], src).then_inc(S(f"spilled{j % 2}"), 16)

        def slot_stored(eng, j):
            if j >= 2:
                eng.wait_ge(S(f"spilled{j % 2}"), 16 * (j // 2))

        def act_zed(a, lo, hi_):
            for u in range(U["zed", lo], U["zed", 0] + hi_):
                for t in range(2):
                    j = 2 * (u - U["zed", 0]) + t
                    full(a, ("unit", u, t))
                    slot_stored(a, j)
                    a.activation(cs[:, t, :], bank(("unit", u, t))[:, :], ACT.Silu)\
                        .then_inc(reads(("unit", u, t)), 1)
                prep_hi(a, u)
                for t in range(2):
                    taken(a, ("unit", u, t))
                    spill_out(a, 2 * (u - U["zed", 0]) + t, cs[:, t, :])

        def multi_unit(pe, u, jobs):
            pe.wait_ge(S("w_lo"), u + 1)
            hi = w_hi[:, u % 2, :].rearrange("p (k c) -> p k c", k=2)
            lo = w_lo[:, u % 2, :].rearrange("p (k c) -> p k c", k=2)
            for t in jobs:
                key = ("unit", u, t)
                open_bank(pe, key)
                for k in range(2):
                    cc = slice(t * P, (t + 1) * P)
                    pe.matmul(bank(key)[:, :], hi[:, k, cc], qn_hi[:, k, :], start=(k == 0), stop=False)
                    pe.matmul(bank(key)[:, :], hi[:, k, cc], qn_lo[:, k, :], start=False, stop=False)
                    mm = pe.matmul(bank(key)[:, :], lo[:, k, cc], qn_hi[:, k, :], start=False, stop=(k == 1))
                mm.then_inc(fills(key), 1)

        isc = lambda b: tmp[:, b, :]
        kc, kp = tmp[:, 6, :], tmp[:, 7, :]

        def pe_index(pe, n):
            b, t = n // 8, n % 8
            for s_ in range(2):
                key, h = ("index", n, s_), slice(64 * s_, 64 * s_ + 64)
                open_bank(pe, key)
                pe.matmul(bank(key)[:, :], qi[h, t, b * P:(b + 1) * P], ki[h, :], start=True, stop=True)\
                    .then_inc(fills(key), 1)

        def act_index(a, n):
            for s_ in range(2):
                key, m = ("index", n, s_), 2 * n + s_
                full(a, key)
                if m >= 2:
                    a.wait_ge(S("index_added"), m - 1)
                a.activation(relu[:, s_, :], bank(key)[:, :], ACT.Relu).then_inc(reads(key), 1)

        def dve_index(v, n):
            b, t = n // 8, n % 8
            for s_ in range(2):
                key, h, m = ("index", n, s_), 2 * t + s_, 2 * n + s_
                taken(v, key)
                w = wcol[:, b, h:h + 1]
                if h == 0:
                    v.tensor_scalar(isc(b), relu[:, s_, :], w, None, ALU.mult).then_inc(S("index_added"), 1)
                else:
                    v.wait_ge(S("index_added"), m)
                    v.scalar_tensor_tensor(out=isc(b), in0=relu[:, s_, :], scalar=w, in1=isc(b), op0=ALU.mult,
                                           op1=ALU.add).then_inc(S("index_added"), 1)

        def dve_topk(v, b, part):
            n0 = b * (2 * RD + 5)

            def step(ins, n):
                ins.then_inc(S("topk"), 1)
                v.wait_ge(S("topk"), n0 + n + 1)
            if part == 0:
                v.wait_ge(S("index_added"), 16 * (b + 1))
                step(v.tensor_scalar(oneh[:, :], kc, qpc[:, 1, b:b + 1], FILL, ALU.is_gt, ALU.mult), 0)
                step(v.tensor_tensor(isc(b), isc(b), oneh[:, :], ALU.add), 1)
            for r in range(4 * part, 4 * part + 4):
                step(v.max(m8[:, r % 2, :], isc(b)), 2 + 2 * r)
                step(v.match_replace(isc(b), m8[:, r % 2, :], isc(b), MARK), 3 + 2 * r)
            if part == 3:
                step(v.tensor_scalar(oneh[:, :], isc(b), -3.39e38, None, ALU.is_gt), 2 * RD + 2)
                step(v.scalar_tensor_tensor(out=isc(b), in0=kc, scalar=qpc[:, 1, b:b + 1], in1=oneh[:, :],
                                            op0=ALU.is_gt, op1=ALU.max), 2 * RD + 3)
                step(v.tensor_scalar(madd[:, b, :], isc(b), NEG, None, ALU.mult), 2 * RD + 4)

        def dve_buckets(v, b):
            NB_ = 5 + len(BUCKET_STEPS)

            def step(ins, n):
                ins.then_inc(S("bucket"), 1)
                v.wait_ge(S("bucket"), b * NB_ + n + 1)
            rel, dist, acc = isc(b), oneh[:, :], cs2[:, :]
            step(v.tensor_scalar(rel, kp, qpc[:, 0, b:b + 1], None, ALU.subtract), 0)
            step(v.tensor_scalar(acc, rel, 0.0, 16.0, ALU.is_gt, ALU.mult), 1)
            step(v.tensor_scalar(dist, rel, -1.0, None, ALU.mult), 2)
            step(v.tensor_tensor(dist, dist, rel, ALU.max), 3)
            step(v.scalar_tensor_tensor(out=acc, in0=dist, scalar=8.0, in1=acc, op0=ALU.min, op1=ALU.add), 4)
            for n, d in enumerate(BUCKET_STEPS):
                out = bkt[:, b, :] if n == len(BUCKET_STEPS) - 1 else acc
                step(v.scalar_tensor_tensor(out=out, in0=dist, scalar=float(d), in1=acc, op0=ALU.is_ge,
                                            op1=ALU.add), 5 + n)

        def pe_steps(pe):
            for i in range(24):
                u = U["xbc", i] if i < 16 else U["gab", i - 16]
                unit_jobs(pe, u, 0, *hn_of, KT)
                for n in (2 * i, 2 * i + 1):
                    if n < 32:
                        pe_index(pe, n)

        def act_steps(a):
            for i in range(24):
                u = U["xbc", i] if i < 16 else U["gab", i - 16]
                j0 = 16 + 2 * i
                for t in range(2):
                    key = ("unit", u, t)
                    full(a, key)
                    slot_stored(a, j0 + t)
                    if i < 16:
                        a.activation(cs[:, t, :], bank(key)[:, :], ACT.Identity, scale=cw2[:, 2 * i + t, 3:4],
                                     bias=cw2[:, 2 * i + t, 4:5]).then_inc(S("tap_last2"), 1)
                    else:
                        a.activation(cs[:, t, :], bank(key)[:, :], ACT.Sigmoid).then_inc(reads(key), 1)
                prep_hi(a, u)
                for t in range(2):
                    taken(a, ("unit", u, t))
                    if i < 16:
                        a.activation(cs[:, t, :], cs[:, t, :], ACT.Silu).then_inc(S("conv_silu2"), 1)
                for n in (2 * i, 2 * i + 1):
                    if n < 32:
                        act_index(a, n)
                for t in range(2):
                    if i < 16:
                        a.wait_ge(S("conv_silu2"), 2 * i + t + 1)
                    spill_out(a, j0 + t, cs[:, t, :])

        def dve_steps(v):
            for i in range(24):
                if i < 16:
                    for t in range(2):
                        j, key = 2 * i + t, ("unit", U["xbc", i], t)
                        v.wait_ge(S("tap_last2"), j + 1)
                        for d in (1, 2, 3):
                            if d > 1:
                                v.wait_ge(S("taps2"), 2 * j + d - 1)
                            v.scalar_tensor_tensor(
                                out=cs[:, t, d:T], in0=bank(key)[:, 0:T - d], scalar=cw2[:, j, 3 - d:4 - d],
                                in1=cs[:, t, d:T], op0=ALU.mult, op1=ALU.add)\
                                .then_inc(S("taps2") if d < 3 else reads(key), 1)
                    for n in (2 * i, 2 * i + 1):
                        dve_index(v, n)
                if 4 <= i < 20:
                    dve_topk(v, i // 4 - 1, i % 4)
                if i >= 20:
                    dve_buckets(v, i - 20)

        def queries(eng, which):
            by_head = qh[:, :].rearrange("p (q h) -> p q h", h=16)
            eng.wait_ge(S("bucket"), 4 * (5 + len(BUCKET_STEPS)))
            for i in range(2):
                for t in range(8):
                    key, h = ("unit", U["uq", i], t), 8 * i + t
                    if h % 2 != which:
                        continue
                    full(eng, key)
                    if which:
                        eng.tensor_scalar(by_head[:, :, h], bank(key)[:, :], P ** -0.5, None, ALU.mult)\
                            .then_inc(reads(key), 1)
                    else:
                        eng.activation(by_head[:, :, h], bank(key)[:, :], ACT.Copy, scale=P ** -0.5)\
                            .then_inc(reads(key), 1)
                if not which:
                    full(eng, ("unit", U["uq", i], 7))
                    prep_hi(eng, U["uq", i])

        def pe_latent(pe):
            pe.wait_ge(S("land_latent"), 16 * 3)
            pe.wait_ge(S("tbl_split"), 5)
            pe.wait_ge(S("bucket"), 4 * (5 + len(BUCKET_STEPS)))
            for n in range(NG + 5):
                if n < NG:
                    for e in range(2):
                        key = ("ohb", n, e)
                        open_bank(pe, key)
                        w = (2 * (n % 16) + e) * P
                        pe.matmul(bank(key)[:, :], qsel4[:, w:w + P], bkt[:, n // 16, :], start=True, stop=True)\
                            .then_inc(fills(key), 1)
                if 1 <= n <= NG:
                    m = n - 1
                    key = ("logit", m)
                    open_bank(pe, key)
                    out = bank(key)[:, :]
                    pe.matmul(out, qsel8[:, (m % 16) * P:(m % 16 + 1) * P], madd[:, m // 16, :], start=True, stop=False,
                              skip_group_check=True)
                    pe.matmul(out, qh[:, m * P:(m + 1) * P], kvf[:, :], start=False, stop=False,
                              skip_group_check=True)
                    for e in range(2):
                        taken(pe, ("ohb", m, e))
                    for part in range(3):
                        for e in range(2):
                            mm = pe.matmul(bank(key)[64 * e:64 * e + 64, :], tbl3[:, part, 192 * e:192 * e + 64],
                                           oh[:, m % 2, e, :], start=False, stop=(part == 2), skip_group_check=True)
                    mm.then_inc(fills(key), 1)
                if 3 <= n < NG + 3:
                    m = n - 3
                    key = ("ptp", m)
                    open_bank(pe, key)
                    pe.wait_ge(S("p_scaled"), m + 1)
                    for c in range(NC):
                        mm = pe.transpose(bank(key)[:, c * P:(c + 1) * P], pr2[:, m % 3, c * P:(c + 1) * P], ident[:, :])
                    mm.then_inc(fills(key), 1)
                if n >= 4 and (n - 4) % 4 == 3:
                    G = (n - 4) // 4
                    key = ("latent", G)
                    open_bank(pe, key)
                    taken(pe, ("ptp", 4 * G + 3))
                    for c in range(NC):
                        mm = pe.matmul(bank(key)[:, :], kvt[:, c, :], ptt[:, G % 2, c, :], start=(c == 0),
                                       stop=(c == NC - 1))
                    mm.then_inc(fills(key), 1)

        def dve_latent(v):
            v.wait_ge(S("land_latent"), 16 * 3)
            for part in range(3):
                v.tensor_copy(tbl3[:, part, :], tbl[:, :]).then_inc(S("tbl_split"), 1)
                if part < 2:
                    v.wait_ge(S("tbl_split"), 2 * part + 1)
                    v.tensor_tensor(tbl[:, :], tbl[:, :], tbl3[:, part, :], ALU.subtract)\
                        .then_inc(S("tbl_split"), 1)
                    v.wait_ge(S("tbl_split"), 2 * part + 2)
            for n in range(NG + 2):
                if n < NG:
                    for e in range(2):
                        key = ("ohb", n, e)
                        full(v, key)
                        if n >= 2:
                            full(v, ("logit", n - 2))
                        v.tensor_scalar(oh[:, n % 2, e, :], bank(key)[:, :], bcol[:, 0:1], None, ALU.is_equal)\
                            .then_inc(reads(key), 1)
                if 1 <= n <= NG:
                    m = n - 1
                    key = ("logit", m)
                    full(v, key)
                    v.tensor_reduce(st2[:, 0, m % 3:m % 3 + 1], bank(key)[:, :], AX, ALU.max)\
                        .then_inc(S("logit_max"), 1)
                    v.wait_ge(S("logit_max"), m + 1)
                    v.tensor_scalar(st2[:, 0, m % 3:m % 3 + 1], st2[:, 0, m % 3:m % 3 + 1], -1.0, None, ALU.mult)\
                        .then_inc(S("neg_logit_max"), 1)
                if n >= 2:
                    m = n - 2
                    taken(v, ("logit", m))
                    v.reciprocal(st2[:, 2, m % 3:m % 3 + 1], st2[:, 1, m % 3:m % 3 + 1]).then_inc(S("p_inverse"), 1)
                    v.wait_ge(S("p_inverse"), m + 1)
                    v.tensor_scalar(pr2[:, m % 3, :], pr2[:, m % 3, :], st2[:, 2, m % 3:m % 3 + 1], None,
                                    ALU.mult).then_inc(S("p_scaled"), 1)

        def act_latent(a):
            a.wait_ge(S("land_latent"), 16 * 3)
            for n in range(1, NG + 6):
                if n <= NG:
                    m = n - 1
                    key = ("logit", m)
                    a.wait_ge(S("neg_logit_max"), m + 1)
                    if m >= 3:
                        full(a, ("ptp", m - 3))
                    a.activation(pr2[:, m % 3, :], bank(key)[:, :], ACT.Exp, bias=st2[:, 0, m % 3:m % 3 + 1],
                                 accum_out=st2[:, 1, m % 3:m % 3 + 1]).then_inc(reads(key), 1)
                if 3 <= n < NG + 3:
                    m = n - 3
                    key = ("ptp", m)
                    full(a, key)
                    g = m % 4
                    a.activation(ptt[:, m // 4 % 2, :, g * P:(g + 1) * P], chunked(bank(key)[:, :]), ACT.Copy)\
                        .then_inc(reads(key), 1)
                if n >= 5 and (n - 5) % 4 == 3:
                    G = (n - 5) // 4
                    key = ("latent", G)
                    full(a, key)
                    a.activation(qh[:, G * T:(G + 1) * T], bank(key)[:, :], ACT.Copy).then_inc(reads(key), 1)

        def pe_values(pe):
            by_head = qh[:, :].rearrange("p (q h) -> p q h", h=16)
            for t in range(8):
                key = ("uv", t)
                open_bank(pe, key)
                taken(pe, ("latent", NG // 4 - 1))
                for s_ in range(2):
                    h = 2 * t + s_
                    mm = pe.matmul(bank(key)[64 * s_:64 * s_ + 64, :], wuv[:, h * 64:(h + 1) * 64], by_head[:, :, h],
                                   start=True, stop=True)
                mm.then_inc(fills(key), 1)

        def act_values(a):
            for t in range(8):
                full(a, ("uv", t))
                a.activation(hn_hi[:, t, :], bank(("uv", t))[:, :], ACT.Copy).then_inc(S("attn_hi"), 1)

        def dve_values(v):
            for t in range(8):
                v.wait_ge(S("attn_hi"), t + 1)
                v.tensor_tensor(hn_lo[:, t, :], bank(("uv", t))[:, :], hn_hi[:, t, :].bitcast(F32), ALU.subtract)\
                    .then_inc(reads(("uv", t)), 1)

        def pe_ssd_turned(pe, g):
            gr = grp[:, g % 2]
            pe.wait_ge(S(f"land_group{g % 2}"), 48 * (g // 2 + 1))
            for key, src in ((("xt", g, 0), 0), (("xt", g, 1), 1), (("bt", g), 2)):
                open_bank(pe, key)
                for c in range(NC - 1 if src == 2 else NC):
                    cc = slice(c * P, (c + 1) * P)
                    mm = pe.transpose(bank(key)[:, cc], gr[:, src, cc], ident[:, :])
                mm.then_inc(fills(key), 1)
            key = ("cb", g)
            open_bank(pe, key)
            for c in range(NC):
                cc = slice(c * P, (c + 1) * P)
                mm = pe.matmul(bank(key)[:, cc], gr[:, 2, cc], gr[:, 3, cc], start=True, stop=True)
            mm.then_inc(fills(key), 1)

        def pe_ssd(pe, g):
            gr = grp[:, g % 2]
            if g % 4 == 0:
                pe_ssd_turned(pe, g)
            for t in range(2):
                for s_ in range(2):
                    h = 4 * g + 2 * t + s_
                    key = ("lm", g, t, s_)
                    open_bank(pe, key)
                    head = pick[HB, h:h + 1].broadcast_to([32, P])
                    pe.matmul(bank(key)[:, :], head, r2_hi[HB, :], start=True, stop=False)
                    pe.matmul(bank(key)[:, :], head, r2_lo[HB, :], start=False, stop=True).then_inc(fills(key), 1)
            taken(pe, ("bt", g))
            pe.wait_ge(S("xdk"), 2 * g + 2)
            for chunks in (0, 1), (2,):
                key = ("st", g, chunks[-1] // 2)
                open_bank(pe, key)
                for c in chunks:
                    mm = pe.matmul(bank(key)[:, c % 2 * 256:c % 2 * 256 + 256], btok[:, c, :], xdk[:, c, :, :],
                                   start=True, stop=True)
                mm.then_inc(fills(key), 1)
            for t in range(2):
                key = ("yd", g, t)
                open_bank(pe, key)
                pe.wait_ge(S("m_made"), 4 * g + 2 * t + 2)
                taken(pe, ("xt", g, t))
                for c in range(NC):
                    for s_ in range(2):
                        mm = pe.matmul(bank(key)[64 * s_:64 * s_ + 64, c * P:(c + 1) * P],
                                       xd[:, c, t, 64 * s_:64 * s_ + 64], lb[:, t, s_, c * P:(c + 1) * P],
                                       start=True, stop=True, skip_group_check=True)
                mm.then_inc(fills(key), 1)
                key = ("yo", g, t)
                open_bank(pe, key)
                taken(pe, ("st", g, 1))
                for c in range(1, NC):
                    cc = slice(c * P, (c + 1) * P)
                    mm = pe.matmul(bank(key)[:, cc], sst[:, c - 1, t, :], gr[:, 3, cc], start=True, stop=True)
                mm.then_inc(fills(key), 1)
            if g % 4 < 3:
                pe_ssd_turned(pe, g + 1)

        def pe_ssd_sum(pe):
            key = ("ssn",)
            open_bank(pe, key)
            pe.wait_ge(S("y_summed"), 15)
            pe.matmul(bank(key)[:, :], ones[:, :], ysq[:, 0, :], start=True, stop=True).then_inc(fills(key), 1)

        def act_ssd(a, g):
            key = ("bt", g)
            full(a, key)
            if g:
                full(a, ("st", g - 1, 1))
            a.activation(btok[:, :, :], chunked(bank(key)[:, :])[:, 0:NC - 1, :], ACT.Copy).then_inc(reads(key), 1)
            for t in range(2):
                for s_ in range(2):
                    a.wait_ge(S("acum_diff"), 4 * g + 2 * t + s_ + 1)
                    a.activation(lb[:, t, s_, :], lb[:, t, s_, :], ACT.Exp).then_inc(S("l_exp"), 1)
            for t in range(2):
                if 2 * g + t:
                    a.wait_ge(S("y_off"), 2 * g + t)
                for s_ in range(2):
                    key, hs = ("lm", g, t, s_), slice(64 * s_, 64 * s_ + 64)
                    a.activation(ea[hs, :], bank(key)[hs, :], ACT.Exp).then_inc(reads(key), 1)
            for t in range(2):
                i = 2 * g + t
                a.wait_ge(S("y_gated"), i + 1)
                if i > 1:
                    a.wait_ge(S("y_summed"), i - 1)
                a.activation(ysq[:, min(i, 1), :], ysd[:, t, :], ACT.Square).then_inc(S("y_squared"), 1)
                full(a, ("unit", U["ossd0" if i >= 8 else "oattn", 3], 1))
                a.activation(hn_hi[:, i % 8, :], ysd[:, t, :], ACT.Copy, scale=ssdg[:, i:i + 1])\
                    .then_inc(S("y_hi"), 1)

        def pool_ssd(pool, g):
            for t in range(2):
                taken(pool, ("xt", g, t))
                if g:
                    full(pool, ("st", g - 1, 1))
                else:
                    pool.wait_ge(S("chunk_decays"), 1)
                h, last = 4 * g + 2 * t, slice(0, NC - 1)
                pool.tensor_tensor(xdk[:, :, t, :].rearrange("p c (s d) -> p c s d", s=2),
                                   xd[:, last, t, :].rearrange("p c (s d) -> p c s d", s=2),
                                   tolast[:, last, h:h + 2, None].broadcast_to([P, NC - 1, 2, 64]), ALU.mult)\
                    .then_inc(S("xdk"), 1)
            pool.wait_ge(S("land_zt"), 16 * (g + 1))
            for t in range(2):
                i = 2 * g + t
                pool.wait_ge(S("y_off"), i + 1)
                pool.tensor_tensor(ysd[:, t, :], ysd[:, t, :], zt[:, t, :], ALU.mult)\
                    .then_inc(S("y_gated"), 1)
                if i:
                    pool.wait_ge(S("y_squared"), i + 1)
                    if i > 1:
                        pool.wait_ge(S("y_summed"), i - 1)
                    pool.tensor_tensor(ysq[:, 0, :], ysq[:, 0, :], ysq[:, 1, :], ALU.add)\
                        .then_inc(S("y_summed"), 1)

        def dve_ssd(v, g):
            gr = grp[:, g % 2]
            v.wait_ge(S("chunk_decays"), 1)
            taken(v, ("cl",))
            v.wait_ge(S(f"land_group{g % 2}"), 48 * (g // 2 + 1))
            for t in range(2):
                key = ("xt", g, t)
                full(v, key)
                if g:
                    full(v, ("yd", g - 1, t))
                    v.wait_ge(S("xdk"), 2 * g)
                h = 96 + 4 * g + 2 * t
                dtc = c1[:, :, h:h + 2, None].broadcast_to([P, NC, 2, 64])
                v.tensor_tensor(xd[:, :, t, :].rearrange("p c (s d) -> p c s d", s=2),
                                chunked(bank(key)[:, :]).rearrange("p c (s d) -> p c s d", s=2), dtc, ALU.mult)\
                    .then_inc(reads(key), 1)
            key = ("cb", g)
            full(v, key)
            v.tensor_tensor(chunked(cbm[:, :]), chunked(bank(key)[:, :]),
                            causal[:, None, :].broadcast_to([P, NC, P]), ALU.mult).then_inc(reads(key), 1)

            def differences(t):
                for s_ in range(2):
                    h = 4 * g + 2 * t + s_
                    key = ("lm", g, t, s_)
                    full(v, key)
                    if g:
                        full(v, ("yd", g - 1, t))
                    for c in range(NC):
                        cc = slice(c * P, (c + 1) * P)
                        ins = v.tensor_scalar(lb[:, t, s_, cc], bank(key)[:, cc], c2[:, c, h:h + 1], 0.0,
                                              ALU.subtract, ALU.min)
                    ins.then_inc(S("acum_diff"), 1)

            def decayed(t):
                taken(v, ("cb", g))
                for s_ in range(2):
                    v.wait_ge(S("l_exp"), 4 * g + 2 * t + s_ + 1)
                    v.tensor_tensor(lb[:, t, s_, :], lb[:, t, s_, :], cbm[:, :], ALU.mult).then_inc(S("m_made"), 1)

            def states():
                key = ("st", g, 0)
                full(v, key)
                if g:
                    full(v, ("yo", g - 1, 1))
                v.tensor_copy(sst[:, 0, :, :], bank(key)[:, 0:256].rearrange("p (t d) -> p t d", t=2))\
                    .then_inc(S("state_decayed"), 1)
                for c in (1, 2):
                    key = ("st", g, c // 2)
                    if c == 1:
                        v.wait_ge(S("state_decayed"), 3 * g + 1)
                    else:
                        taken(v, ("st", g, 0))
                    v.tensor_tensor(
                        sst[:, c, :, :].rearrange("p t (s d) -> p (t s) d", s=2),
                        sst[:, c - 1, :, :].rearrange("p t (s d) -> p (t s) d", s=2),
                        cdall[:, 4 * g:4 * g + 4, c:c + 1].broadcast_to([P, 4, 64]), ALU.mult)\
                        .then_inc(S("state_decayed"), 1)
                    full(v, key)
                    v.wait_ge(S("state_decayed"), 3 * g + c + 1)
                    added = bank(key)[:, c % 2 * 256:c % 2 * 256 + 256]
                    v.tensor_tensor(sst[:, c, :, :], sst[:, c, :, :], added.rearrange("p (t d) -> p t d", t=2),
                                    ALU.add).then_inc(reads(key), 1)

            def output(t):
                i = 2 * g + t
                full(v, ("yd", g, t))
                if i >= 2:
                    v.wait_ge(S("y_lo"), i - 1)
                v.scalar_tensor_tensor(out=ysd[:, t, :], in0=gr[:, t, :], scalar=dskip[:, i:i + 1],
                                       in1=bank(("yd", g, t))[:, :], op0=ALU.mult, op1=ALU.add)\
                    .then_inc(reads(("yd", g, t)), 1)
                taken(v, ("lm", g, t, 1))
                full(v, ("yo", g, t))
                v.tensor_tensor(ea[:, P:T], ea[:, P:T], bank(("yo", g, t))[:, P:T], ALU.mult)\
                    .then_inc(reads(("yo", g, t)), 1)
                taken(v, ("yo", g, t))
                taken(v, ("yd", g, t))
                v.tensor_tensor(ysd[:, t, P:T], ysd[:, t, P:T], ea[:, P:T], ALU.add).then_inc(S("y_off"), 1)

            def low(i):
                v.wait_ge(S("y_hi"), i + 1)
                v.scalar_tensor_tensor(out=hn_lo[:, i % 8, :], in0=ysd[:, i % 2, :], scalar=ssdg[:, i:i + 1],
                                       in1=hn_hi[:, i % 8, :].bitcast(F32), op0=ALU.mult, op1=ALU.subtract)\
                    .then_inc(S("y_lo"), 1)

            differences(0)
            differences(1)
            if g % 4:
                low(2 * g - 1)
            states()
            decayed(0)
            decayed(1)
            output(0)
            output(1)
            low(2 * g)
            if g % 4 == 3:
                low(2 * g + 1)

        def dve_attn_gate(v):
            v.wait_ge(S("land_gate"), 16)
            for i in range(4):
                for t in range(2):
                    key, j = ("unit", U["oattn", i], t), 2 * i + t
                    full(v, key)
                    v.tensor_tensor(ma[:, j, :], ma[:, j, :], bank(key)[:, :], ALU.mult).then_inc(reads(key), 1)

        def dve_mix(v):
            taken(v, ("ssn",))
            v.reciprocal(rs[:, :], rs[:, :]).then_inc(S("ssd_rstd"), 1)
            v.wait_ge(S("ssd_rstd"), 1)
            v.wait_ge(S("land_gate"), 32)
            gate = grp[:, :, :, :].rearrange("p a b t -> p (a b) t")

            def step(ins):
                ins.then_inc(S("mixed"), 1)
                count[0] += 1
                v.wait_ge(S("mixed"), count[0])
            count = [0]
            for i in range(4):
                for t in range(2):
                    key, j = ("unit", U["ossd1", i], t), 2 * i + t
                    step(v.tensor_tensor(gate[:, j, :], gate[:, j, :], rs[:, :], ALU.mult))
                    full(v, key)
                    v.tensor_tensor(tmp[:, j, :], tmp[:, j, :], bank(key)[:, :], ALU.add).then_inc(reads(key), 1)
                    taken(v, key)
                    step(v.tensor_tensor(tmp[:, j, :], tmp[:, j, :], gate[:, j, :], ALU.mult))
                    step(v.tensor_tensor(tmp[:, j, :], tmp[:, j, :], ma[:, j, :], ALU.add))
            for k in range(KT):
                v.wait_ge(S("blend_hi"), k + 1)
                v.tensor_tensor(hn_lo[:, k, :], tmp[:, k, :], hn_hi[:, k, :].bitcast(F32), ALU.subtract)\
                    .then_inc(S("blend_lo"), 1)

        def act_mix(a):
            full(a, ("ssn",))
            a.activation(rs[:, :], bank(("ssn",))[:, :], ACT.Sqrt, bias=eps[:, 0:1], scale=1.0 / 2048)\
                .then_inc(reads(("ssn",)), 1)
            over_units(a, "ossd1", lambda u, i: prep_hi(a, u, i))
            full(a, ("unit", U["ossd1", 3], 1))
            for k in range(KT):
                a.wait_ge(S("mixed"), 3 * k + 3)
                a.activation(hn_hi[:, k, :], tmp[:, k, :], ACT.Copy).then_inc(S("blend_hi"), 1)

        def sp_group(sp, g):
            land = S(f"land_group{g % 2}")
            if g >= 2:
                full(sp, ("yo", g - 2, 1))
                sp.wait_ge(S("y_gated"), 2 * g - 2)
            sp.dma_start(grp[:, g % 2, 0:2, :], spill[16 + 2 * g:18 + 2 * g].rearrange("n p t -> p n t"))\
                .then_inc(land, 16)
            sp.dma_start(grp[:, g % 2, 2, :], spill[32 + g]).then_inc(land, 16)
            sp.dma_start(grp[:, g % 2, 3, :], spill[40 + g]).then_inc(land, 16)

        def sp_gate(sp, g):
            if g:
                sp.wait_ge(S("y_gated"), 2 * g)
            sp.dma_start(zt[:, :, :], spill[2 * g:2 * g + 2].rearrange("n p t -> p n t"))\
                .then_inc(S("land_zt"), 16)

        FIRST = [(ones, "ones"), (gains, "gains"), (c_col, "c_col"), (sinks, "sinks")]
        LOADS = [(ident, "ident"), (identb, "identb"),
                 (cw, "cw"), (gng, "gng"), (col1, "col1"), (sel, "sel"), (mask4, "mask4"), (strict, "strict"),
                 (levels, "levels"), (mod, "mod"), (gain2, "gain2")]
        SECOND = [(small2, "small2"), (cw2, "cw2"), (dskip, "dskip"), (ssdg, "ssdg"), (causal, "causal"),
                  (wuv, "wuv"), (bcol, "bcol"), (reset2, "reset2"), (qpi, "qpi")]
        block = ctx.enter_context(nc.Block())

        @block.sync
        def _(sp):
            sp.dma_start(memx, I["memT"]).then_inc(S("land_mem"), 16)
            for q in range(2):
                sp.dma_start(raw[:, q, :], I["W"][q]).then_inc(w_land[q], 16)
            sp.dma_start(x[:, :, :], I["xT"]).then_inc(S("land_x"), 16)
            for ap, name in LOADS:
                sp.dma_start(ap[tuple(slice(None) for _ in ap.shape)], I[name]).then_inc(S("land_const"), 16)
            sp.dma_start(gcst[32:32 + HG, :], I["gcst"]).then_inc(S("land_const"), 16)
            sp.dma_start(reset[32:32 + HG, :], I["reset"]).then_inc(S("land_const"), 16)

            def load_units(first, last):
                pairs = (last - first) // 2
                with sp.Fori(0, pairs) as i:
                    for q in range(2):
                        u = first + q
                        sp.wait_ge(S("w_lo"), i * 2 + (u - 1))
                        sp.dma_start(raw[:, u % 2, :], I["W"][i * 2 + u]).then_inc(w_land[u % 2], 16)
                for u in range(first + 2 * pairs, last):
                    sp.wait_ge(S("w_lo"), u - 1)
                    sp.dma_start(raw[:, u % 2, :], I["W"][u]).then_inc(w_land[u % 2], 16)

            u = U["oattn", 0]
            load_units(2, u + 2)
            full(sp, ("uv", 7))
            for q in range(2):
                sp.wait_ge(S(f"spilled{q}"), 16 * 32)
            sp.dma_start(ma[:, :, :], spill[48:56].rearrange("n p t -> p n t")).then_inc(S("land_gate"), 16)
            sp_group(sp, 0)
            sp_gate(sp, 0)
            sp_group(sp, 1)
            load_units(u + 2, u + 6)
            for g in range(1, 4):
                sp_gate(sp, g)
                sp_group(sp, g + 1)
            load_units(u + 6, u + 8)
            sp_gate(sp, 4)
            sp_group(sp, 5)
            load_units(u + 8, u + 10)
            for g in range(5, 8):
                sp_gate(sp, g)
                if g < 7:
                    sp_group(sp, g + 1)
            full(sp, ("yo", 7, 1))
            sp.wait_ge(S("y_gated"), 16)
            sp.dma_start(grp[:, :, :, :], spill[56:64].rearrange("(a b) p t -> p a b t", a=2))\
                .then_inc(S("land_gate"), 16)
            load_units(u + 10, NU)
            sp.wait_ge(S("post_added"), 2 * KT)
            sp.dma_start(O["out"], x[:, :, :]).then_inc(S("stored"), 16)
            sp.wait_ge(S("stored"), 16)

        @block.gpsimd
        def _(pool):
            pool.memset(eps[:, :], EPS).then_inc(S("eps_set"), 1)
            pool.memset(bg[:, :], 0.0).then_inc(S("bg_zero"), 1)

            def low_units(first, last):
                pairs = (last - first) // 2
                with pool.Fori(0, pairs) as i:
                    for q in range(2):
                        u = first + q
                        pool.wait_ge(S("w_hi"), i * 2 + (u + 1))
                        pool.tensor_tensor(w_lo[:, u % 2, :], raw[:, u % 2, :], w_hi[:, u % 2, :].bitcast(F32),
                                           ALU.subtract).then_inc(S("w_lo"), 1)
                for u in range(first + 2 * pairs, last):
                    pool.wait_ge(S("w_hi"), u + 1)
                    pool.tensor_tensor(w_lo[:, u % 2, :], raw[:, u % 2, :], w_hi[:, u % 2, :].bitcast(F32),
                                       ALU.subtract).then_inc(S("w_lo"), 1)

            u = U["ossd0", 0]
            low_units(0, u + 2)
            for g in range(4):
                pool_ssd(pool, g)
            low_units(u + 2, u + 6)
            for g in range(4, 8):
                pool_ssd(pool, g)
            low_units(u + 6, NU)

        @block.scalar
        def _(a):
            for ap, name in FIRST:
                a.dma_start(ap[tuple(slice(None) for _ in ap.shape)], I[name]).then_inc(S("land_first"), 16)
            def first_hi(q):
                a.wait_ge(w_land[q], 16)
                a.activation(w_hi[:, q, :], raw[:, q, :], ACT.Copy).then_inc(S("w_hi"), 1)

            a.wait_ge(S("land_first"), 16 * len(FIRST))
            a.wait_ge(S("eps_set"), 1)
            a.activation(c_col[:, :], c_col[:, :], ACT.Silu).then_inc(S("c_silu"), 1)
            a.wait_ge(S("c_silu"), 1)
            a.activation(c_pair[:, :, 0], c_col[:, :], ACT.Copy).then_inc(S("c_split"), 1)
            act_norm(a, 0, lambda k: mem_of(k), MEM, lambda e, k: e.wait_ge(S("land_mem"), 16),
                     between=lambda: first_hi(0))
            first_hi(1)
            act_norm_round(a, 0, MEM)
            for i in range(4):
                prep_hi(a, U["mem", i])
            act_norm(a, 1, x_of, T, lambda e, k: e.wait_ge(S("land_x"), 16))
            act_norm_round(a, 1)
            a.wait_ge(S("land_const"), 16 * (len(LOADS) + 2))
            act_gates(a)
            act_qkv(a)
            act_z(a)
            act_heads(a)
            act_recurrence(a)
            act_attention(a, 0)
            act_squares(a, "wout0", ("norm", 2), x_of, sq_tmp)
            act_norm_round(a, 2)
            act_ffn(a, 0)
            taken(a, ("unit", U["dn02", 3], 1))
            for ap, name in ((rcol, "rcol"), (perm, "perm"), (band, "band"), (posi, "posi")):
                a.dma_start(ap[:, :], I[name]).then_inc(S("land_rope"), 16)
            act_norm_round(a, 3)
            rope_tables_act(a)
            prep_hi(a, U["kv", 0])
            act_norm_round(a, 4)
            over_units(a, "swaq", lambda u, i: prep_hi(a, u, i))
            act_attention(a, 1)
            act_squares(a, "wout1", ("norm", 5), x_of, sq_tmp)
            act_norm_round(a, 5)
            act_ffn(a, 1)
            full(a, ("unit", U["dn12", 3], 1))
            for ap, name in SECOND:
                a.dma_start(ap[tuple(slice(None) for _ in ap.shape)], I[name]).then_inc(S("land_second"), 16)
            act_norm(a, 7, x_of, T, lambda e, k: e.wait_ge(S("final"), k + 1))
            act_round2(a, 0)
            act_small(a)
            a.wait_ge(S("land_second"), 16 * len(SECOND))
            act_zed(a, 0, 1)
            act_small_late(a)
            act_zed(a, 1, 8)
            act_decays(a)
            full(a, ("unit", U["qidx", 0], 7))
            prep_hi(a, U["qidx", 0])
            act_steps(a)
            full(a, ("unit", U["gab", 7], 1))
            a.wait_ge(S("bucket"), 4 * (5 + len(BUCKET_STEPS)))
            for ap, name in ((qsel4, "qsel4"), (qsel8, "qsel8"), (tbl, "tbl")):
                a.dma_start(ap[:, :], I[name]).then_inc(S("land_latent"), 16)
            queries(a, 0)
            act_latent(a)
            act_values(a)
            over_units(a, "oattn", lambda u, i: prep_hi(a, u, i))
            for g in range(4):
                act_ssd(a, g)
            over_units(a, "ossd0", lambda u, i: prep_hi(a, u, i))
            for g in range(4, 8):
                act_ssd(a, g)
            act_mix(a)
            act_squares(a, "wout2", ("post", 0), sq_tmp, lambda k: ysq[:, min(k, 1), :])
            act_norm(a, 8, x_of, T, lambda e, k: e.wait_ge(S("post_added"), k + 1))
            act_round2(a, 1)
            act_ffn(a, 2)

        @block.vector
        def _(v):
            v.wait_ge(S("land_first"), 16 * len(FIRST))
            v.tensor_scalar(nsinks[:, :, :], sinks[:, :, :], -1.0, None, ALU.mult).then_inc(S("nsinks"), 1)
            v.wait_ge(S("nsinks"), 1)
            v.wait_ge(S("c_split"), 1)
            v.tensor_tensor(c_pair[:, :, 1], c_col[:, :], c_pair[:, :, 0].bitcast(F32), ALU.subtract)\
                .then_inc(S("c_split"), 1)
            dve_rstd(v, 0, MEM, 0)
            dve_norm(v, 0, 0, mem_of, MEM)
            dve_mem(v)
            dve_rstd(v, 1, T, 1)
            dve_norm(v, 1, 1, x_of)
            v.wait_ge(S("land_const"), 16 * (len(LOADS) + 2))
            dve_gates(v)
            dve_qkv(v)
            dve_memq(v, U["memq", 0])
            dve_heads(v)
            dve_inverse(v)
            dve_turned(v)
            dve_recurrence(v)
            dve_onorm(v)
            dve_attention(v, 0)
            dve_squares(v, "wout0", to_x(v), sq_tmp)
            dve_rstd(v, 2, T, 2)
            dve_norm(v, 2, 2, x_of)
            dve_ffn(v, 0)
            dve_rstd(v, 3, T, 3)
            dve_norm(v, 3, 3, x_of)
            rope_tables_dve(v)
            dve_kv(v)
            dve_norm(v, 4, 4, x_of)
            for i in range(4):
                for j in (2 * i, 2 * i + 1):
                    key = ("unit", U["swaq", i], j % 2)
                    full(v, key)
                    dst = qraw[:, j, :] if j < 6 else mem_q[:, j - 6, :]
                    v.tensor_copy(dst, bank(key)[:, :]).then_inc(reads(key), 1)
                for j in ROPE_AFTER[i]:
                    taken(v, ("unit", U["swaq", j // 2], j % 2) if j < 6 else ("unit", U["kv", 0], 0))
                    dve_rope(v, j)
            dve_attention(v, 1)
            dve_squares(v, "wout1", to_x(v), sq_tmp)
            dve_rstd(v, 5, T, 4)
            dve_norm(v, 5, 5, x_of)
            dve_ffn(v, 1)
            dve_rstd(v, 6, T, 5)
            for k in range(KT):
                v.scalar_tensor_tensor(out=x[:, k, :], in0=x[:, k, :], scalar=gains[:, 6, k:k + 1],
                                       in1=rs[:, :], op0=ALU.mult, op1=ALU.mult).then_inc(S("final"), 1)
            dve_modulation(v)
            dve_rstd(v, 7, T, 6)
            dve_ada_norm(v, 7, 0)
            dve_small(v)
            for t in range(8):
                key = ("unit", U["qidx", 0], t)
                full(v, key)
                v.tensor_copy(qi[:, t, :], bank(key)[:, :]).then_inc(reads(key), 1)
            v.wait_ge(S("wcol"), 1)
            dve_steps(v)
            queries(v, 1)
            dve_latent(v)
            dve_values(v)
            dve_attn_gate(v)
            for g in range(4):
                dve_ssd(v, g)
            dve_gather(v, "ossd0", False)
            for g in range(4, 8):
                dve_ssd(v, g)
            dve_mix(v)
            dve_squares(v, "wout2", to_tmp(v, False), lambda k: ysq[:, min(k, 1), :])
            dve_post(v, 0)
            dve_rstd(v, 8, T, 7)
            dve_ada_norm(v, 8, 1)
            dve_ffn(v, 2)
            dve_post(v, 1)

        @block.tensor
        def _(pe):
            pe.wait_ge(S("land_first"), 16 * len(FIRST))
            pe_norm(pe, 0, MEM, 0)
            pe_mem(pe)
            pe_norm(pe, 1, T, 1)
            pe.wait_ge(S("land_const"), 16 * (len(LOADS) + 2))
            pe_gdn_in(pe)
            pe_heads(pe)
            pe_inverse(pe)
            pe_turned(pe)
            pe_recurrence(pe)
            pe_onorm(pe)
            pe_attention(pe, 0, lambda e, kind, t: taken(e, ("unit", U["memq", 0], t)))
            pe.wait_ge(S("mix_lo"), HG)
            for j in range(2):
                taken(pe, ("value", 0, j))
            pe_linear(pe, "wout0")
            pe_squares(pe, "wout0", ("norm", 2), sq_tmp)
            pe_ffn(pe, 0, hn_ready(pe, 2))
            pe_squares(pe, "dn02", ("norm", 3), sq_tmp)
            pe_kv(pe)
            for i in range(4):
                unit_jobs(pe, U["swaq", i], 0, *hn_of, KT, ready=None if i else hn_ready(pe, 4))
                for j in ROPE_AFTER[i]:
                    pe_rope(pe, j)
            pe.wait_ge(S("roped"), 7)
            pe_attention(pe, 1, lambda e, kind, t: kind == "mem" and taken(e, ("unit", U["swaq", 3], t)))
            for j in range(8):
                taken(pe, ("value", 1, j))
            pe_linear(pe, "wout1")
            pe_squares(pe, "wout1", ("norm", 5), sq_tmp)
            pe_ffn(pe, 1, hn_ready(pe, 5))
            pe_squares(pe, "dn12", ("norm", 6), sq_tmp)
            pe_norm(pe, 7, T, 2)
            pe_linear(pe, "qlat", ready=ada_ready(pe, 0))
            pe_linear(pe, "misc")
            pe_small(pe)
            for i in range(8):
                unit_jobs(pe, U["zed", i], 0, *hn_of, KT)
                if i == 3:
                    pe_small_late(pe)
            pe.wait_ge(S("qn_lo"), 2)
            multi_unit(pe, U["qidx", 0], range(8))
            taken(pe, ("kid",))
            taken(pe, ("unit", U["qidx", 0], 7))
            pe_steps(pe)
            for i in range(2):
                multi_unit(pe, U["uq", i], range(8))
            for t in range(4, 8):
                taken(pe, ("unit", U["uq", 1], t))
            pe_latent(pe)
            pe_values(pe)
            pe_linear(pe, "oattn", ready=lambda k: taken(pe, ("uv", k)))
            for g in range(4):
                pe_ssd(pe, g)
            pe_linear(pe, "ossd0", ready=lambda k: pe.wait_ge(S("y_lo"), k + 1))
            for g in range(4, 8):
                pe_ssd(pe, g)
            pe_ssd_sum(pe)
            pe_linear(pe, "ossd1", ready=lambda k: pe.wait_ge(S("y_lo"), k + 9))
            pe_linear(pe, "wout2", ready=lambda k: pe.wait_ge(S("blend_lo"), k + 1))
            pe_squares(pe, "wout2", ("post", 0), lambda k: ysq[:, min(k, 1), :])
            pe_norm(pe, 8, T, 3)
            pe_ffn(pe, 2, ada_ready(pe, 1))
            pe_squares(pe, "dn22", ("post", 1), lambda k: sg[:, min(k, 1), :])


def units_of(w):
    out = []
    for k0 in range(0, w.shape[0], D):
        part = w[k0:k0 + D]
        rows = np.zeros((D, w.shape[1]), np.float32)
        rows[:part.shape[0]] = part
        for c0 in range(0, w.shape[1], 2 * P):
            block = np.zeros((D, 2 * P), np.float32)
            block[:, :min(2 * P, w.shape[1] - c0)] = rows[:, c0:c0 + 2 * P]
            out.append(block.reshape(KT, P, 2 * P).transpose(1, 0, 2).reshape(P, UW))
    return out


def ffn_units(gate_up, down):
    pairs = np.stack([gate_up[:, :FF].reshape(D, FT, P), gate_up[:, FF:].reshape(D, FT, P)], 2)
    gu = units_of(pairs.reshape(D, 2 * FF))
    dn = units_of(down)
    return gu[0:16] + dn[0:4] + gu[16:22] + dn[4:12]


def short_units(w):
    return [w[:, c:c + D].reshape(2, P, D).transpose(1, 0, 2).reshape(P, UW) for c in range(0, w.shape[1], D)]


def tiles(a):
    return np.ascontiguousarray(a.reshape(-1, P, *a.shape[1:]).swapaxes(0, 1))


def layout(i):
    BF = mybir.dt.np(BF16)
    a = {}
    eye = np.eye(P, dtype=np.float32)
    w = []
    for layer in range(2):
        w += units_of(i["w_mem_kv"][layer])
    win = i["gdn_w_in"][0]
    ba = np.zeros((D, P), np.float32)
    ba[:, 0:HG] = win[:, 3072:3072 + HG]
    ba[:, 32:32 + HG] = win[:, 3072 + HG:3072 + 2 * HG]
    w += units_of(ba) + units_of(win[:, 0:3072]) + units_of(win[:, 3072 + 2 * HG:])
    w += units_of(i["w_out"][0]) + ffn_units(i["w_gate_up"][0], i["w_down"][0]) + units_of(i["w_kv"])
    order = np.arange(12 * 64).reshape(2, 6, 64).transpose(1, 0, 2).reshape(-1)
    order = np.concatenate([order, np.arange(12 * 64, D)])
    w += units_of(i["swa_w_q"][0][:, order]) + units_of(i["ada_w_2"]) + units_of(i["w_out"][1][order])
    w += ffn_units(i["w_gate_up"][1], i["w_down"][1])
    cuts = np.cumsum([0, 256, 128, 64, 16, 2048, 4096, 32, D, D])
    qlat, kvl, kid, wid, zed, xbc, dt, ga, gb = (i["w_in_2"][:, lo:hi] for lo, hi in zip(cuts[:-1], cuts[1:]))
    misc = np.concatenate([kvl, kid, wid, np.zeros((D, 16), np.float32), dt], 1)
    w += units_of(qlat) + units_of(misc) + units_of(zed) + short_units(i["w_qidx_2"])
    w += units_of(xbc) + units_of(ga) + units_of(gb) + short_units(i["w_uq_2"])
    w += units_of(i["w_o_attn_2"]) + units_of(i["w_o_ssd_2"]) + units_of(i["w_out_2"])
    w += ffn_units(i["w_ffn_in_2"], i["w_ffn_out_2"])
    a["W"] = np.stack(w)
    a["xT"] = tiles(i["x"][0].T)
    a["memT"] = tiles(i["mem"][0].T)
    a["ident"] = eye
    a["identb"] = eye.astype(BF)
    a["ones"] = np.ones((P, P), np.float32)
    a["gains"] = np.ascontiguousarray(np.stack([g.reshape(KT, P) for g in (
        i["ln_mem"], i["ln_mix"][0], i["ln_ffn"][0], i["ln_kv"], i["ln_mix"][1], i["ln_ffn"][1],
        i["ln_final"])]).transpose(2, 0, 1))
    sinks = np.full((8, 2), NEG, np.float32)
    sinks[0:6] = i["swa_sinks"][0].reshape(2, 6).T
    a["sinks"] = np.tile(sinks, (P, 1, 1))
    a["cw"] = tiles(i["gdn_conv"][0].T)
    a["gng"] = i["gdn_norm"][0].reshape(P, 1)
    a["gcst"] = np.ascontiguousarray(np.stack([i["gdn_dt_bias"][0], i["gdn_A_log"][0]], 1))
    a["col1"] = np.zeros((P, 127), np.float32)
    a["col1"][:, 63] = 1
    a["sel"] = np.zeros((64, 2 * HG, P), np.float32)
    for h in range(HG):
        a["sel"][h, h] = 1
        a["sel"][32 + h, HG + h] = 1
    s, c = np.arange(P)[:, None], np.arange(P)[None, :]
    a["mask4"] = np.tile(np.where(s > c, NEG, 0.0), (1, 4)).astype(BF)
    a["strict"] = (s < c).astype(np.float32)
    a["levels"] = np.stack([((s >> lv) % 2 == 1) & ((s >> lv) - 1 == (c >> lv)) for lv in range(7)], 1)\
        .astype(np.float32)
    reset = np.ones((HG, T), np.float32)
    reset[:, ::P] = 0
    a["reset"] = reset
    f = np.arange(P) % 64
    inv = (np.float32(500000.0) ** (-np.arange(0, 16, 2, dtype=np.float32) / np.float32(16))).astype(np.float32)
    a["rcol"] = np.zeros((P, 2), np.float32)
    a["rcol"][:, 0] = np.where(f < 16, inv[f % 8], 0)
    a["rcol"][:, 1] = np.where(f < 8, -1, np.where(f < 16, 1, 0))
    a["perm"] = np.zeros((P, P), np.float32)
    for r in np.flatnonzero(f < 16):
        a["perm"][r + 8 if f[r] < 8 else r - 8, r] = 1
    k = np.arange(256)[None, :]
    a["band"] = np.where((k > s) & (k <= s + P), 0.0, NEG).astype(BF)
    a["posi"] = np.tile(i["positions"].astype(np.int32), (P, 1))
    a["mod"] = tiles(i["ada_b_2"])
    a["c_col"] = tiles(i["c_2"][0])
    a["gain2"] = np.ascontiguousarray(np.stack([i[g + "_2"].reshape(KT, P) for g in (
        "pre_norm_mix", "post_norm_mix", "pre_norm_ffn", "post_norm_ffn")]).transpose(2, 0, 1))
    small = np.zeros((P, 6), np.float32)
    small[:, 0:2] = tiles(i["q_norm_2"])
    small[:, 2] = i["kv_norm_2"]
    small[0:64, 3] = i["kidx_norm_2"]
    small[96:128, 4] = i["dt_bias_2"]
    small[96:128, 5] = i["a_log_2"]
    a["small2"] = small
    a["cw2"] = np.concatenate([tiles(i["conv_w_2"].T), tiles(i["conv_b_2"])[:, :, None]], 2)
    a["dskip"] = tiles(np.repeat(i["d_skip_2"], 64))
    a["ssdg"] = tiles(i["ssd_norm_2"])
    a["causal"] = (s <= c).astype(np.float32)
    a["reset2"] = np.tile(reset[0], (P, 1))
    a["wuv"] = np.ascontiguousarray(i["w_uv_2"].transpose(1, 0, 2).reshape(P, 16 * 64))
    a["bcol"] = (np.arange(P) % 32).astype(np.float32)[:, None]
    a["qpi"] = tiles(i["positions_2"][0].astype(np.int32))
    a["posi2"] = np.tile(i["positions_2"].astype(np.int32), (P, 1))
    a["qsel4"] = (s == np.arange(32 * P)[None, :] // 32).astype(BF)
    a["qsel8"] = (s == np.arange(16 * P)[None, :] // 16).astype(BF)
    tbl = np.zeros((4, 32, 2, 8, 16), np.float32)
    for q in range(8):
        tbl[q % 4, :, q // 4, q, :] = i["rel_bias_2"]
    a["tbl"] = tbl.reshape(P, 2 * P)
    return a


def kernel(**inputs):
    import concourse.bacc as bacc
    from concourse.bass_utils import run_bass_kernel_spmd

    arrays = layout({name: np.asarray(value) for name, value in inputs.items()})
    nc = bacc.Bacc("TRN2", target_bir_lowering=False, num_devices=1)
    I = {k: nc.dram_tensor("in_" + k, v.shape, mybir.dt.from_np(v.dtype), kind="ExternalInput").ap()
         for k, v in arrays.items()}
    O = {"out": nc.dram_tensor("out_x", (P, KT, T), F32, kind="ExternalOutput").ap()}
    build(nc, I, O)
    result = run_bass_kernel_spmd(nc, [{"in_" + k: v for k, v in arrays.items()}], core_ids=[0])
    out = result.results[0]["out_x"]
    return np.ascontiguousarray(out.transpose(1, 0, 2).reshape(1, D, T).transpose(0, 2, 1))
```
